# Optimizing a Trainium2 kernel written in Bass

```python
import math
import jax, jax.numpy as jnp
from jax import lax
import numpy as np

D_MODEL = 1024
BATCH = 1
SEQ = 256
DEPTH = 2

N_EVEN = (DEPTH + 1) // 2
N_ODD = DEPTH // 2
N_SUB = 3
RMS_EPS = 1e-6
FFN_RES = 0.5
D_FF = ((8 * D_MODEL // 3 + 127) // 128) * 128
POOL_WINDOWS = (2, 4, 8, 16)
POOL_GROUPS = len(POOL_WINDOWS)
POOL_DIM = D_MODEL // 2
POOL_GROUP_DIM = POOL_DIM // POOL_GROUPS
D_SSM = D_MODEL
SSD_HEADDIM = 64
SSD_HEADS = D_SSM // SSD_HEADDIM
SSD_GROUPS = 2
D_STATE = 128
CONV_K = 4
CONV_DIM = D_SSM + 2 * SSD_GROUPS * D_STATE
SSD_CHUNK = 128
IN_AB = POOL_DIM + D_SSM + CONV_DIM + SSD_HEADS
OUT_AB = POOL_DIM + D_SSM
MLA_HEADS = 16
QK_NOPE = 64
QK_ROPE = 32
V_DIM = 64
Q_LORA = 768
KV_LORA = 256
IN_MLA = Q_LORA + KV_LORA + QK_ROPE
ROPE_THETA = 10000.0
Q_BLOCK = 128


def rmsnorm(x, g):
    xf = x.astype(jnp.float32)
    y = xf * lax.rsqrt(jnp.mean(xf * xf, axis=-1, keepdims=True) + RMS_EPS)
    return (y * g.astype(jnp.float32)).astype(x.dtype)

def modulate(h, shift, scale):
    return h * (1 + scale[:, None, :]) + shift[:, None, :]

def swiglu(h, w13, w2):
    a, b = jnp.split(h @ w13, 2, axis=-1)
    return (jax.nn.silu(a) * b) @ w2

def multiscale_pool(u, w, scale):
    bsz, L, _ = u.shape
    uf = u.astype(jnp.float32)
    cs_pad = jnp.pad(jnp.cumsum(uf, axis=1), ((0, 0), (1, 0), (0, 0)))
    t = jnp.arange(L, dtype=jnp.float32)
    outs = []
    for gi, win in enumerate(POOL_WINDOWS):
        sl = slice(gi * POOL_GROUP_DIM, (gi + 1) * POOL_GROUP_DIM)
        c_g = cs_pad[:, :, sl]
        lag = jnp.pad(c_g[:, :L + 1 - win], ((0, 0), (win - 1, 0), (0, 0)))
        count = jnp.minimum(t + 1.0, float(win))[None, :, None]
        outs.append((c_g[:, 1:] - lag) / count - uf[:, :, sl])
    d = jnp.stack(outs, axis=2)
    y = jnp.einsum("blgc,gcd->blgd", d, w.astype(jnp.float32)).reshape(bsz, L, POOL_DIM)
    return (y * scale.astype(jnp.float32)).astype(u.dtype)

def causal_depthwise_conv(u, w, b):
    y = lax.conv_general_dilated(u, w[:, None, :], window_strides=(1,),
                                 padding=[(CONV_K - 1, 0)],
                                 dimension_numbers=("NWC", "WIO", "NWC"),
                                 feature_group_count=u.shape[-1])
    return y + b

def ssd_chunked(xh, dt, a, bm, cm):
    bsz, L, H, P = xh.shape
    nc = L // SSD_CHUNK
    r = H // SSD_GROUPS
    x = (xh * dt[..., None]).reshape(bsz, nc, SSD_CHUNK, SSD_GROUPS, r, P)
    adt = (dt * a).reshape(bsz, nc, SSD_CHUNK, SSD_GROUPS, r).transpose(0, 3, 4, 1, 2)
    bc = bm.reshape(bsz, nc, SSD_CHUNK, SSD_GROUPS, D_STATE)
    cc = cm.reshape(bsz, nc, SSD_CHUNK, SSD_GROUPS, D_STATE)
    a_cs = jnp.cumsum(adt, axis=-1)
    causal = jnp.tril(jnp.ones((SSD_CHUNK, SSD_CHUNK), dtype=bool))
    decay = jnp.exp(jnp.where(causal, a_cs[..., :, None] - a_cs[..., None, :], -jnp.inf))
    cb = jnp.einsum("bclgn,bcsgn->bgcls", cc, bc)
    y_diag = jnp.einsum("bgcls,bgrcls,bcsgrp->bclgrp", cb, decay, x)
    decay_to_end = jnp.exp(a_cs[..., -1:] - a_cs)
    states = jnp.einsum("bcsgn,bgrcs,bcsgrp->cbgrpn", bc, decay_to_end, x)
    chunk_decay = jnp.exp(a_cs[..., -1]).transpose(3, 0, 1, 2)

    def step(h, inp):
        s_c, d_c = inp
        return d_c[..., None, None] * h + s_c, h

    h0 = jnp.zeros(states.shape[1:], states.dtype)
    _, prev = lax.scan(step, h0, (states, chunk_decay))
    y_off = jnp.einsum("bclgn,cbgrpn,bgrcl->bclgrp", cc, prev, jnp.exp(a_cs))
    return (y_diag + y_off).reshape(bsz, L, H, P)

def pool_ssd_mixer(h, w_in, pool_w, pool_scale, conv_w, conv_b, dt_bias, a_log, d_skip, norm_g, w_out):
    bsz, L, _ = h.shape
    proj = h @ w_in
    u_pool, z, xbc, dt_raw = jnp.split(
        proj, [POOL_DIM, POOL_DIM + D_SSM, POOL_DIM + D_SSM + CONV_DIM], axis=-1)
    y_pool = multiscale_pool(u_pool, pool_w, pool_scale)
    xbc = jax.nn.silu(causal_depthwise_conv(xbc, conv_w, conv_b))
    xs, bm, cm = jnp.split(xbc, [D_SSM, D_SSM + SSD_GROUPS * D_STATE], axis=-1)
    f32 = jnp.float32
    xh = xs.astype(f32).reshape(bsz, L, SSD_HEADS, SSD_HEADDIM)
    dt = jax.nn.softplus(dt_raw.astype(f32) + dt_bias.astype(f32))
    a = -jnp.exp(a_log.astype(f32))
    y = ssd_chunked(xh, dt, a,
                    bm.astype(f32).reshape(bsz, L, SSD_GROUPS, D_STATE),
                    cm.astype(f32).reshape(bsz, L, SSD_GROUPS, D_STATE))
    y = y + d_skip.astype(f32)[:, None] * xh
    y = y.reshape(bsz, L, D_SSM) * jax.nn.silu(z.astype(f32))
    yg = y.reshape(bsz, L, SSD_GROUPS, D_SSM // SSD_GROUPS)
    yg = yg * lax.rsqrt(jnp.mean(yg * yg, axis=-1, keepdims=True) + RMS_EPS)
    y = (yg.reshape(bsz, L, D_SSM) * norm_g.astype(f32)).astype(h.dtype)
    return jnp.concatenate([y_pool, y], axis=-1) @ w_out

def rope_tables(positions):
    inv_freq = ROPE_THETA ** (-jnp.arange(0, QK_ROPE, 2, dtype=jnp.float32) / QK_ROPE)
    ang = positions.astype(jnp.float32)[..., None] * inv_freq
    return jnp.cos(ang), jnp.sin(ang)

def apply_rope(x, cos, sin):
    xf = x.astype(jnp.float32)
    x1, x2 = jnp.split(xf, 2, axis=-1)
    return jnp.concatenate([x1 * cos - x2 * sin, x2 * cos + x1 * sin], axis=-1).astype(x.dtype)

def mla_mixer(h, positions, w_in, q_norm_g, w_uq, kv_norm_g, w_ukv, w_o):
    bsz, L, _ = h.shape
    q_a, kv_a, k_rope = jnp.split(h @ w_in, [Q_LORA, Q_LORA + KV_LORA], axis=-1)
    q = (rmsnorm(q_a, q_norm_g) @ w_uq).reshape(bsz, L, MLA_HEADS, QK_NOPE + QK_ROPE)
    q_nope, q_rope = q[..., :QK_NOPE], q[..., QK_NOPE:]
    kv = (rmsnorm(kv_a, kv_norm_g) @ w_ukv).reshape(bsz, L, MLA_HEADS, QK_NOPE + V_DIM)
    k_nope, v = kv[..., :QK_NOPE], kv[..., QK_NOPE:]
    cos, sin = rope_tables(positions)
    q_rope = apply_rope(q_rope, cos[:, :, None], sin[:, :, None])
    k_rope = apply_rope(k_rope, cos, sin)
    scale = 1.0 / math.sqrt(QK_NOPE + QK_ROPE)
    nb = L // Q_BLOCK
    k_idx = jnp.arange(L)

    def blocks(t):
        return jnp.moveaxis(t.reshape(bsz, nb, Q_BLOCK, *t.shape[2:]), 1, 0)

    def attend(args):
        qn, qr, start = args
        s = (jnp.einsum("bqhd,bkhd->bhqk", qn, k_nope, preferred_element_type=jnp.float32)
             + jnp.einsum("bqhd,bkd->bhqk", qr, k_rope, preferred_element_type=jnp.float32)) * scale
        q_idx = start + jnp.arange(Q_BLOCK)
        s = jnp.where(k_idx[None, :] <= q_idx[:, None], s, -jnp.inf)
        p = jax.nn.softmax(s, axis=-1).astype(v.dtype)
        return jnp.einsum("bhqk,bkhd->bqhd", p, v)

    starts = jnp.arange(nb, dtype=jnp.int32) * Q_BLOCK
    o = lax.map(attend, (blocks(q_nope), blocks(q_rope), starts))
    o = jnp.moveaxis(o, 0, 1).reshape(bsz, L, MLA_HEADS * V_DIM)
    return o @ w_o

def first_inputs(seed: int = 0) -> dict:
    key = jax.random.key(seed)
    ks = jax.random.split(key, 32)
    f32 = jnp.float32

    def nrm(k, shape, std):
        return jax.random.normal(k, shape, f32) * std

    def gain(k, shape):
        return 1.0 + 0.05 * jax.random.normal(k, shape, f32)

    x = jax.random.normal(ks[0], (BATCH, SEQ, D_MODEL), f32)
    c = jax.random.normal(ks[1], (BATCH, D_MODEL), f32)
    positions = (jnp.arange(SEQ, dtype=jnp.int32)[None, :]
                 + jax.random.randint(ks[2], (BATCH, 1), 0, 1024, dtype=jnp.int32))
    mod_w = nrm(ks[3], (DEPTH, D_MODEL, 3 * N_SUB * D_MODEL), 0.5 * D_MODEL ** -0.5)
    mod_b = nrm(ks[4], (DEPTH, 3 * N_SUB * D_MODEL), 0.02)
    norm_g = gain(ks[5], (DEPTH, N_SUB, D_MODEL))
    ffn_w13 = nrm(ks[6], (DEPTH, 2, D_MODEL, 2 * D_FF), D_MODEL ** -0.5)
    ffn_w2 = nrm(ks[7], (DEPTH, 2, D_FF, D_MODEL), D_FF ** -0.5)
    ab_w_in = nrm(ks[8], (N_EVEN, D_MODEL, IN_AB), D_MODEL ** -0.5)
    pool_w = nrm(ks[9], (N_EVEN, POOL_GROUPS, POOL_GROUP_DIM, POOL_GROUP_DIM), POOL_GROUP_DIM ** -0.5)
    pool_scale = gain(ks[10], (N_EVEN, POOL_DIM))
    ssd_conv_w = nrm(ks[11], (N_EVEN, CONV_K, CONV_DIM), CONV_K ** -0.5)
    ssd_conv_b = nrm(ks[12], (N_EVEN, CONV_DIM), 0.02)
    dt0 = jnp.exp(jax.random.uniform(ks[13], (N_EVEN, SSD_HEADS), f32,
                                     minval=math.log(1e-3), maxval=math.log(1e-1)))
    ssd_dt_bias = dt0 + jnp.log(-jnp.expm1(-dt0))
    ssd_a_log = jnp.log(jax.random.uniform(ks[14], (N_EVEN, SSD_HEADS), f32, minval=1.0, maxval=16.0))
    ssd_d = gain(ks[15], (N_EVEN, SSD_HEADS))
    ssd_norm_g = gain(ks[16], (N_EVEN, D_SSM))
    ab_w_out = nrm(ks[17], (N_EVEN, OUT_AB, D_MODEL), OUT_AB ** -0.5)
    mla_w_in = nrm(ks[18], (N_ODD, D_MODEL, IN_MLA), D_MODEL ** -0.5)
    mla_q_norm_g = gain(ks[19], (N_ODD, Q_LORA))
    mla_w_uq = nrm(ks[20], (N_ODD, Q_LORA, MLA_HEADS * (QK_NOPE + QK_ROPE)), Q_LORA ** -0.5)
    mla_kv_norm_g = gain(ks[21], (N_ODD, KV_LORA))
    mla_w_ukv = nrm(ks[22], (N_ODD, KV_LORA, MLA_HEADS * (QK_NOPE + V_DIM)), KV_LORA ** -0.5)
    mla_w_o = nrm(ks[23], (N_ODD, MLA_HEADS * V_DIM, D_MODEL), (MLA_HEADS * V_DIM) ** -0.5)
    final_norm_g = gain(ks[24], (D_MODEL,))
    return {"x": x, "c": c, "positions": positions, "mod_w": mod_w, "mod_b": mod_b,
            "norm_g": norm_g, "ffn_w13": ffn_w13, "ffn_w2": ffn_w2, "ab_w_in": ab_w_in,
            "pool_w": pool_w, "pool_scale": pool_scale, "ssd_conv_w": ssd_conv_w,
            "ssd_conv_b": ssd_conv_b, "ssd_dt_bias": ssd_dt_bias, "ssd_a_log": ssd_a_log,
            "ssd_d": ssd_d, "ssd_norm_g": ssd_norm_g, "ab_w_out": ab_w_out,
            "mla_w_in": mla_w_in, "mla_q_norm_g": mla_q_norm_g, "mla_w_uq": mla_w_uq,
            "mla_kv_norm_g": mla_kv_norm_g, "mla_w_ukv": mla_w_ukv, "mla_w_o": mla_w_o,
            "final_norm_g": final_norm_g}

def first_block(x, c, positions, mod_w, mod_b, norm_g, ffn_w13, ffn_w2, ab_w_in, pool_w,
              pool_scale, ssd_conv_w, ssd_conv_b, ssd_dt_bias, ssd_a_log, ssd_d, ssd_norm_g,
              ab_w_out, mla_w_in, mla_q_norm_g, mla_w_uq, mla_kv_norm_g, mla_w_ukv, mla_w_o,
              final_norm_g):
    c_act = jax.nn.silu(c)
    for i in range(DEPTH):
        mod = c_act @ mod_w[i] + mod_b[i]
        sh1, sc1, g1, sh2, sc2, g2, sh3, sc3, g3 = jnp.split(mod, 3 * N_SUB, axis=-1)
        h = modulate(rmsnorm(x, norm_g[i, 0]), sh1, sc1)
        x = x + FFN_RES * g1[:, None, :] * swiglu(h, ffn_w13[i, 0], ffn_w2[i, 0])
        h = modulate(rmsnorm(x, norm_g[i, 1]), sh2, sc2)
        j = i // 2
        if i % 2 == 0:
            m = pool_ssd_mixer(h, ab_w_in[j], pool_w[j], pool_scale[j], ssd_conv_w[j],
                               ssd_conv_b[j], ssd_dt_bias[j], ssd_a_log[j], ssd_d[j],
                               ssd_norm_g[j], ab_w_out[j])
        else:
            m = mla_mixer(h, positions, mla_w_in[j], mla_q_norm_g[j], mla_w_uq[j],
                          mla_kv_norm_g[j], mla_w_ukv[j], mla_w_o[j])
        x = x + g2[:, None, :] * m
        h = modulate(rmsnorm(x, norm_g[i, 2]), sh3, sc3)
        x = x + FFN_RES * g3[:, None, :] * swiglu(h, ffn_w13[i, 1], ffn_w2[i, 1])
    return rmsnorm(x, final_norm_g)


DEPTH_2 = 1

MEM_LEN = 256
HEAD_DIM = 64
N_HEADS = D_MODEL // HEAD_DIM
N_KV_GROUPS = 4
HEADS_PER_GROUP = N_HEADS // N_KV_GROUPS
CMP_BLOCK = 32
CMP_STRIDE = 16
SEL_BLOCK = 64
SEL_TOP_N = 16
WINDOW = 512
SEL_Q_CHUNK = 16
CONV_CH = D_MODEL
CONV_WIDTH = 31
X_HEADS = 4
X_HEAD_DIM = D_MODEL // X_HEADS
D_FF_2 = int(math.ceil(8 * D_MODEL / 3 / 256)) * 256
REL_BUCKETS = 32
REL_MAX_DIST = 128
EPS = 1e-6

SPLIT_SIZES = (
    2 * CONV_CH,
    N_HEADS * HEAD_DIM,
    N_KV_GROUPS * HEAD_DIM,
    N_KV_GROUPS * HEAD_DIM,
    N_KV_GROUPS * HEAD_DIM,
    N_KV_GROUPS * HEAD_DIM,
    N_KV_GROUPS * HEAD_DIM,
    N_KV_GROUPS * HEAD_DIM,
    3 * N_HEADS,
    D_MODEL,
    D_MODEL,
)
N_IN = sum(SPLIT_SIZES)
SPLIT_POINTS = tuple(int(v) for v in np.cumsum(SPLIT_SIZES)[:-1])


def rms_norm(x, g):
    xf = x.astype(jnp.float32)
    y = xf * lax.rsqrt(jnp.mean(xf * xf, axis=-1, keepdims=True) + EPS)
    return (y * g.astype(jnp.float32)).astype(x.dtype)

def layer_norm(x, g, b):
    xf = x.astype(jnp.float32)
    mu = jnp.mean(xf, axis=-1, keepdims=True)
    xc = xf - mu
    y = xc * lax.rsqrt(jnp.mean(xc * xc, axis=-1, keepdims=True) + EPS)
    return (y * g.astype(jnp.float32) + b.astype(jnp.float32)).astype(x.dtype)

def t5_bucket(dist):
    n = jnp.maximum(dist, 0)
    max_exact = REL_BUCKETS // 2
    nf = jnp.maximum(n, 1).astype(jnp.float32)
    large = max_exact + (jnp.log(nf / max_exact) / math.log(REL_MAX_DIST / max_exact)
                         * (REL_BUCKETS - max_exact)).astype(jnp.int32)
    large = jnp.minimum(large, REL_BUCKETS - 1)
    return jnp.where(n < max_exact, n, large)

def masked_softmax(s, mask):
    s = jnp.where(mask, s, -1e30)
    m = jnp.max(s, axis=-1, keepdims=True)
    p = jnp.where(mask, jnp.exp(s - m), 0.0)
    return p / jnp.maximum(jnp.sum(p, axis=-1, keepdims=True), 1e-30)

def conv_module(u, dw_w, dw_b, ln_g, ln_b, pw_w):
    a, gt = jnp.split(u, 2, axis=-1)
    v = a * jax.nn.sigmoid(gt)
    v = lax.conv_general_dilated(
        v, dw_w[:, None, :], window_strides=(1,),
        padding=((CONV_WIDTH - 1, 0),),
        dimension_numbers=("NWC", "WIO", "NWC"),
        feature_group_count=CONV_CH) + dw_b
    v = jax.nn.silu(layer_norm(v, ln_g, ln_b))
    return v @ pw_w

def compress_blocks(blocks, pos, w1, w2):
    z = blocks + pos[None, None, :, None, :]
    z = jnp.einsum("bnlgd,lde->bnge", z, w1)
    return jax.nn.silu(z) @ w2

def nsa_attention(q, kc, vc, ks, vs, kw, vw, gate_logits, cmp_pos, cmp_w1, cmp_w2, rel_bias):
    B, S = q.shape[0], q.shape[1]
    G, R, Dh = N_KV_GROUPS, HEADS_PER_GROUP, HEAD_DIM
    scale = 1.0 / math.sqrt(Dh)
    qg = q.reshape(B, S, G, R, Dh)
    t = jnp.arange(S)

    n_cmp = (S - CMP_BLOCK) // CMP_STRIDE + 1
    cidx = np.arange(n_cmp)[:, None] * CMP_STRIDE + np.arange(CMP_BLOCK)[None, :]
    k_cmp = compress_blocks(kc[:, cidx], cmp_pos[0], cmp_w1[0], cmp_w2[0])
    v_cmp = compress_blocks(vc[:, cidx], cmp_pos[1], cmp_w1[1], cmp_w2[1])
    c_end = jnp.arange(n_cmp) * CMP_STRIDE + CMP_BLOCK - 1
    dist_c = t[:, None] - c_end[None, :]
    bias_c = rel_bias[t5_bucket(dist_c)].reshape(S, n_cmp, G, R).transpose(2, 3, 0, 1)
    s_c = jnp.einsum("bsgrd,bngd->bgrsn", qg, k_cmp).astype(jnp.float32) * scale + bias_c
    p_cmp = masked_softmax(s_c, dist_c >= 0)
    o_cmp = jnp.einsum("bgrsn,bngd->bsgrd", p_cmp.astype(v_cmp.dtype), v_cmp)

    n_sel = S // SEL_BLOCK
    top_n = min(SEL_TOP_N, n_sel)
    jj = np.arange(n_cmp)[:, None] * CMP_STRIDE
    mm0 = np.arange(n_sel)[None, :] * SEL_BLOCK
    overlap = ((jj < mm0 + SEL_BLOCK) & (jj + CMP_BLOCK > mm0)).astype(np.float32)
    imp = jnp.einsum("bgrsn,nm->bsgm", p_cmp, jnp.asarray(overlap))
    blk_t = (t // SEL_BLOCK)[:, None]
    mm = jnp.arange(n_sel)[None, :]
    forced = (mm == 0) | (mm == blk_t) | (mm == blk_t - 1)
    valid = mm <= blk_t
    score = jnp.where(forced[None, :, None, :], jnp.inf,
                      jnp.where(valid[None, :, None, :], imp, -jnp.inf))
    _, sel_idx = lax.top_k(score, top_n)

    ksg = ks.reshape(B, n_sel, SEL_BLOCK, G, Dh).transpose(0, 3, 1, 2, 4)
    vsg = vs.reshape(B, n_sel, SEL_BLOCK, G, Dh).transpose(0, 3, 1, 2, 4)
    bias_g = rel_bias.reshape(REL_BUCKETS, G, R)
    nc = S // SEL_Q_CHUNK
    q_ch = qg.reshape(B, nc, SEL_Q_CHUNK, G, R, Dh).swapaxes(0, 1)
    i_ch = sel_idx.reshape(B, nc, SEL_Q_CHUNK, G, top_n).swapaxes(0, 1)
    starts = jnp.arange(nc) * SEL_Q_CHUNK
    b_ix = jnp.arange(B)[:, None, None, None]
    g_ix = jnp.arange(G)[None, None, :, None]
    n_keys = top_n * SEL_BLOCK

    def sel_chunk(args):
        qc, ic, st = args
        kg = ksg[b_ix, g_ix, ic].reshape(B, SEL_Q_CHUNK, G, n_keys, Dh)
        vg = vsg[b_ix, g_ix, ic].reshape(B, SEL_Q_CHUNK, G, n_keys, Dh)
        kpos = (ic[..., None] * SEL_BLOCK + jnp.arange(SEL_BLOCK)).reshape(B, SEL_Q_CHUNK, G, n_keys)
        tq = st + jnp.arange(SEL_Q_CHUNK)
        dist = tq[None, :, None, None] - kpos
        bias = bias_g[t5_bucket(dist), g_ix]
        s = jnp.einsum("bqgrd,bqgkd->bqgrk", qc, kg).astype(jnp.float32) * scale \
            + bias.swapaxes(-1, -2)
        p = masked_softmax(s, (dist >= 0)[:, :, :, None, :])
        return jnp.einsum("bqgrk,bqgkd->bqgrd", p.astype(vg.dtype), vg)

    o_slc = lax.map(sel_chunk, (q_ch, i_ch, starts)).swapaxes(0, 1).reshape(B, S, G, R, Dh)

    nq = S // Q_BLOCK
    kwp = jnp.pad(kw, ((0, 0), (WINDOW, 0), (0, 0), (0, 0)))
    vwp = jnp.pad(vw, ((0, 0), (WINDOW, 0), (0, 0), (0, 0)))
    q_bl = qg.reshape(B, nq, Q_BLOCK, G, R, Dh).swapaxes(0, 1)

    def win_block(args):
        qb, i = args
        start = i * Q_BLOCK
        kb = lax.dynamic_slice_in_dim(kwp, start, Q_BLOCK + WINDOW, axis=1)
        vb = lax.dynamic_slice_in_dim(vwp, start, Q_BLOCK + WINDOW, axis=1)
        tq = start + jnp.arange(Q_BLOCK)
        kpos = start - WINDOW + jnp.arange(Q_BLOCK + WINDOW)
        dist = tq[:, None] - kpos[None, :]
        mask = (dist >= 0) & (dist < WINDOW) & (kpos[None, :] >= 0)
        bias = rel_bias[t5_bucket(dist)].reshape(Q_BLOCK, Q_BLOCK + WINDOW, G, R).transpose(2, 3, 0, 1)
        s = jnp.einsum("bqgrd,bkgd->bgrqk", qb, kb).astype(jnp.float32) * scale + bias
        p = masked_softmax(s, mask)
        return jnp.einsum("bgrqk,bkgd->bqgrd", p.astype(vb.dtype), vb)

    o_win = lax.map(win_block, (q_bl, jnp.arange(nq))).swapaxes(0, 1).reshape(B, S, G, R, Dh)

    g = jax.nn.sigmoid(gate_logits).reshape(B, S, 3, G, R, 1)
    o = g[:, :, 0] * o_cmp + g[:, :, 1] * o_slc + g[:, :, 2] * o_win
    return o.reshape(B, S, N_HEADS * HEAD_DIM)

def hybrid_mixer(h, w_in, conv_dw_w, conv_dw_b, conv_ln_g, conv_ln_b, conv_pw_w,
                 cmp_pos, cmp_w1, cmp_w2, w_out, rel_bias):
    B, S = h.shape[0], h.shape[1]
    (u_conv, q, kc, vc, ks, vs, kw, vw, g_nsa_heads, g_conv, g_attn) = jnp.split(
        h @ w_in, SPLIT_POINTS, axis=-1)
    kv_shape = (B, S, N_KV_GROUPS, HEAD_DIM)
    conv_out = conv_module(u_conv, conv_dw_w, conv_dw_b, conv_ln_g, conv_ln_b, conv_pw_w)
    nsa_out = nsa_attention(
        q.reshape(B, S, N_HEADS, HEAD_DIM),
        kc.reshape(kv_shape), vc.reshape(kv_shape), ks.reshape(kv_shape),
        vs.reshape(kv_shape), kw.reshape(kv_shape), vw.reshape(kv_shape),
        g_nsa_heads.reshape(B, S, 3, N_HEADS), cmp_pos, cmp_w1, cmp_w2, rel_bias)
    y = jax.nn.sigmoid(g_conv) * conv_out + jax.nn.sigmoid(g_attn) * nsa_out
    return y @ w_out

def cross_attention(h, mem, wq, wkv, wo):
    B, S = h.shape[0], h.shape[1]
    M = mem.shape[1]
    q = (h @ wq).reshape(B, S, X_HEADS, X_HEAD_DIM)
    k, v = jnp.split(mem @ wkv, 2, axis=-1)
    k = k.reshape(B, M, X_HEADS, X_HEAD_DIM)
    v = v.reshape(B, M, X_HEADS, X_HEAD_DIM)
    s = jnp.einsum("bshd,bmhd->bhsm", q, k).astype(jnp.float32) / math.sqrt(X_HEAD_DIM)
    p = jax.nn.softmax(s, axis=-1).astype(v.dtype)
    o = jnp.einsum("bhsm,bmhd->bshd", p, v).reshape(B, S, X_HEADS * X_HEAD_DIM)
    return o @ wo

def swiglu_2(h, w_in, w_out):
    a, b = jnp.split(h @ w_in, 2, axis=-1)
    return (jax.nn.silu(a) * b) @ w_out

def second_inputs(seed: int = 0) -> dict:
    key = jax.random.key(seed)
    ks = jax.random.split(key, 24)
    f32 = jnp.float32

    def nrm(k, shape, scale):
        return jax.random.normal(k, shape, f32) * scale

    def gain(k, shape):
        return 1.0 + 0.02 * jax.random.normal(k, shape, f32)

    return {
        "x": jax.random.normal(ks[0], (BATCH, SEQ, D_MODEL), f32),
        "mem": jax.random.normal(ks[1], (BATCH, MEM_LEN, D_MODEL), f32),
        "norm_mix_g": gain(ks[2], (DEPTH_2, D_MODEL)),
        "w_in": nrm(ks[3], (DEPTH_2, D_MODEL, N_IN), D_MODEL ** -0.5),
        "conv_dw_w": nrm(ks[4], (DEPTH_2, CONV_WIDTH, CONV_CH), CONV_WIDTH ** -0.5),
        "conv_dw_b": nrm(ks[5], (DEPTH_2, CONV_CH), 0.02),
        "conv_ln_g": gain(ks[6], (DEPTH_2, CONV_CH)),
        "conv_ln_b": nrm(ks[7], (DEPTH_2, CONV_CH), 0.02),
        "conv_pw_w": nrm(ks[8], (DEPTH_2, CONV_CH, D_MODEL), CONV_CH ** -0.5),
        "cmp_pos": nrm(ks[9], (DEPTH_2, 2, CMP_BLOCK, HEAD_DIM), 0.1),
        "cmp_w1": nrm(ks[10], (DEPTH_2, 2, CMP_BLOCK, HEAD_DIM, HEAD_DIM), (CMP_BLOCK * HEAD_DIM) ** -0.5),
        "cmp_w2": nrm(ks[11], (DEPTH_2, 2, HEAD_DIM, HEAD_DIM), HEAD_DIM ** -0.5),
        "w_out": nrm(ks[12], (DEPTH_2, D_MODEL, D_MODEL), D_MODEL ** -0.5),
        "norm_x_g": gain(ks[13], (DEPTH_2, D_MODEL)),
        "xq_w": nrm(ks[14], (DEPTH_2, D_MODEL, X_HEADS * X_HEAD_DIM), D_MODEL ** -0.5),
        "xkv_w": nrm(ks[15], (DEPTH_2, D_MODEL, 2 * X_HEADS * X_HEAD_DIM), D_MODEL ** -0.5),
        "xo_w": nrm(ks[16], (DEPTH_2, X_HEADS * X_HEAD_DIM, D_MODEL), (X_HEADS * X_HEAD_DIM) ** -0.5),
        "norm_ffn_g": gain(ks[17], (DEPTH_2, D_MODEL)),
        "ffn_in_w": nrm(ks[18], (DEPTH_2, D_MODEL, 2 * D_FF_2), D_MODEL ** -0.5),
        "ffn_out_w": nrm(ks[19], (DEPTH_2, D_FF_2, D_MODEL), D_FF_2 ** -0.5),
        "rel_bias": nrm(ks[20], (REL_BUCKETS, N_HEADS), 0.5),
        "final_norm_g": gain(ks[21], (D_MODEL,)),
    }

def second_block(x, mem, norm_mix_g, w_in, conv_dw_w, conv_dw_b, conv_ln_g, conv_ln_b,
              conv_pw_w, cmp_pos, cmp_w1, cmp_w2, w_out, norm_x_g, xq_w, xkv_w, xo_w,
              norm_ffn_g, ffn_in_w, ffn_out_w, rel_bias, final_norm_g):
    for l in range(DEPTH_2):
        h = rms_norm(x, norm_mix_g[l])
        x = x + hybrid_mixer(h, w_in[l], conv_dw_w[l], conv_dw_b[l], conv_ln_g[l], conv_ln_b[l],
                             conv_pw_w[l], cmp_pos[l], cmp_w1[l], cmp_w2[l], w_out[l], rel_bias)
        h = rms_norm(x, norm_x_g[l])
        x = x + cross_attention(h, mem, xq_w[l], xkv_w[l], xo_w[l])
        h = rms_norm(x, norm_ffn_g[l])
        x = x + swiglu_2(h, ffn_in_w[l], ffn_out_w[l])
    return rms_norm(x, final_norm_g)


def setup_inputs(seed=0):
    out = dict(first_inputs(seed))
    for name, value in second_inputs(seed + 1).items():
        if name != "x":
            out[name + "_2"] = value
    return out


def reference(
    x, c, positions, mod_w, mod_b, norm_g, ffn_w13, ffn_w2, ab_w_in, pool_w, pool_scale,
    ssd_conv_w, ssd_conv_b, ssd_dt_bias, ssd_a_log, ssd_d, ssd_norm_g, ab_w_out, mla_w_in,
    mla_q_norm_g, mla_w_uq, mla_kv_norm_g, mla_w_ukv, mla_w_o, final_norm_g, mem_2,
    norm_mix_g_2, w_in_2, conv_dw_w_2, conv_dw_b_2, conv_ln_g_2, conv_ln_b_2, conv_pw_w_2,
    cmp_pos_2, cmp_w1_2, cmp_w2_2, w_out_2, norm_x_g_2, xq_w_2, xkv_w_2, xo_w_2, norm_ffn_g_2,
    ffn_in_w_2, ffn_out_w_2, rel_bias_2, final_norm_g_2,
):
    x = first_block(
        x, c, positions, mod_w, mod_b, norm_g, ffn_w13, ffn_w2, ab_w_in, pool_w, pool_scale,
        ssd_conv_w, ssd_conv_b, ssd_dt_bias, ssd_a_log, ssd_d, ssd_norm_g, ab_w_out, mla_w_in,
        mla_q_norm_g, mla_w_uq, mla_kv_norm_g, mla_w_ukv, mla_w_o, final_norm_g,
    )
    return second_block(
        x, mem_2, norm_mix_g_2, w_in_2, conv_dw_w_2, conv_dw_b_2, conv_ln_g_2, conv_ln_b_2,
        conv_pw_w_2, cmp_pos_2, cmp_w1_2, cmp_w2_2, w_out_2, norm_x_g_2, xq_w_2, xkv_w_2,
        xo_w_2, norm_ffn_g_2, ffn_in_w_2, ffn_out_w_2, rel_bias_2, final_norm_g_2,
    )


_drawn_inputs = setup_inputs


def setup_inputs(seed=0):
    import zlib

    import numpy as np

    out = dict(_drawn_inputs(seed))
    spreads = {}
    factors = {'pool_scale': 6.117,
     'ssd_conv_b': 7.591,
     'ssd_d': 8.0,
     'ssd_norm_g': 4.305,
     'mla_q_norm_g': 8.0,
     'mla_kv_norm_g': 8.0,
     'norm_mix_g_2': 6.385,
     'conv_dw_b_2': 11.392,
     'conv_ln_g_2': 23.351,
     'conv_ln_b_2': 21.917,
     'cmp_pos_2': 3.568,
     'norm_x_g_2': 168.146,
     'norm_ffn_g_2': 11.502,
     'final_norm_g_2': 22.836}
    for name, (base, spread) in spreads.items():
        noise = np.random.default_rng([zlib.crc32(name.encode()), seed]).standard_normal(out[name].shape)
        drawn = base * np.exp(spread * noise) if base else spread * noise
        out[name] = __import__('jax').numpy.asarray(drawn.astype(out[name].dtype))
    for name, factor in factors.items():
        out[name] = (out[name] * factor).astype(out[name].dtype)
    return out
```

```python
from contextlib import ExitStack
import math

import numpy as np

import concourse.bass as bass
from concourse import mybir

F32 = mybir.dt.float32
F32R = mybir.dt.float32r
I32 = mybir.dt.int32
ALU = mybir.AluOpType
ACT = mybir.ActivationFunctionType
AX = mybir.AxisListType.X

P = 128
D = 1024
L = 256
QT = L // P
KT = D // P
FF = 2816
FT = FF // P
FG = FT // 2
EPS = 1e-6
NEG = -1e30
BLK = 1024
RING = 6
MODC = 512
N_MOD = 2 * 9 * D // MODC
HEADS = 16
N_CMP = (L - 32) // 16 + 1


COLS = [("c", 8), ("mod_b", 144), ("norm_g", 48), ("pool_scale", 4), ("conv_w", 48), ("conv_b", 12),
        ("q_norm", 6), ("kv_norm", 2), ("ssd_norm", 8), ("mix", 8), ("dw_w", 248), ("dw_b", 8),
        ("ln_g", 8), ("ln_b", 8), ("nx", 8), ("nffn", 8)]
SMALL = [("dt_w", 128), ("rope_w", 256), ("gh_w", 384), ("pool_w", 512), ("w1", 2048), ("w2", 128),
         ("pos", 32), ("relb", 16)]
CONST = [("ident", 128), ("upper", 128), ("ssd_mask", 128), ("causal", 256), ("ones", 128), ("sel", 1),
         ("invf", 16), ("recip", 64), ("cmp01", 32), ("cmpneg", 32)]


def offsets(table):
    at, out = 0, {}
    for name, width in table:
        out[name] = (at, at + width)
        at += width
    return out, at


COL, NCOL = offsets(COLS)
SML, NSML = offsets(SMALL)
CST, NCST = offsets(CONST)


N_BLOCKS = 5 * FG * 6 + (16 + 8) + 12 + (8 + 6 + 3 + 4 + 8) + (16 + 8 + 2 + 2 + 2 + 2 + 2 + 2 + 8 + 8 + 8 + 8) \
    + (8 + 8 + 8 + 8)


def build(nc, a):
    n_stream = N_BLOCKS
    ctx = ExitStack()
    with ctx:
        def sb(name, shape, dt=F32):
            return ctx.enter_context(nc.sbuf_tensor(name, shape, dt))

        def sem(name):
            return ctx.enter_context(nc.semaphore(name))

        class Count:

            def __init__(self, name):
                self.sem, self.n = sem(name), 0

            def up(self, by=1):
                self.n += by
                return by

        raw = sb("raw", [P, RING, BLK])
        w_hi = sb("w_hi", [P, RING, BLK], F32R)
        w_lo = sb("w_lo", [P, RING, BLK], F32R)
        x = sb("resid", [P, QT, D])
        t_hi = sb("t_hi", [P, 12, L], F32R)
        t_lo = sb("t_lo", [P, 12, L], F32R)
        tmp = sb("tmp", [P, 2, 512])
        act_s = sb("act_s", [P, 2, 512])
        g_hi = sb("g_hi", [P, 2, L], F32R)
        g_lo = sb("g_lo", [P, 2, L], F32R)
        cols = sb("cols", [P, NCOL])
        small = sb("small", [P, NSML])
        cst = sb("cst", [P, NCST])
        modc = sb("modc", [P, 144])
        sg = sb("sg", [P, 8])
        grow = sb("grow", [P, D])
        cb = sb("cb", [P, KT, 32])
        biasc = sb("biasc", [P, QT, 16, HEADS])
        st = sb("st", [P, 64])
        rowv = sb("rowv", [P, 48])
        posi = sb("posi", [P, QT], I32)
        AW = 16448
        arena = sb("arena", [P, AW])
        ps = [ctx.enter_context(nc.psum_tensor(f"ps{i}", [P, 512], F32)) for i in range(8)]
        u_dram = nc.dram_tensor("u_scratch", [HEADS, P, 384], F32, kind="Internal").ap()

        def col(name, i=0, n=1):
            return cols[:, COL[name][0] + i:COL[name][0] + i + n]

        def cs(name, lo=0, hi=None, rows=P):
            s, e = CST[name]
            return cst[0:rows, s + lo:(e if hi is None else s + hi)]

        def sm(name, lo=0, hi=None, rows=slice(0, P)):
            s, e = SML[name]
            return small[rows, s + lo:(e if hi is None else s + hi)]

        def ar(at, *shape, parts=slice(0, P)):
            n = int(np.prod(shape))
            assert at + n <= AW, (at, shape)
            v = arena[parts, at:at + n]
            if len(shape) == 2:
                return v.rearrange("p (a b) -> p a b", b=shape[1])
            if len(shape) == 3:
                return v.rearrange("p (a b c) -> p a b c", b=shape[1], c=shape[2])
            return v

        ident = cs("ident")

        V, A, T, G = Count("vector_steps"), Count("scalar_steps"), Count("tensor_steps"), Count("pool_steps")
        landed = [sem(f"block_landed{i}") for i in range(RING)]
        hi_done, lo_done, used = sem("block_hi_done"), sem("block_lo_done"), sem("block_used")
        mod_landed = [sem("mod_landed0"), sem("mod_landed1")]
        mod_used = sem("mod_half_used")
        gated, gate_hi, gate_lo = sem("hidden_gated"), sem("hidden_hi_done"), sem("hidden_lo_done")
        silu_done = sem("silu_done")
        mod_sum, mod_kept, mod_cols, mod_added = sem("mod_summed"), sem("mod_kept"), sem("mod_columns"), sem("mod_added")
        inputs, later, scratch, stored = Count("inputs_landed"), Count("rows_landed"), Count("scratch_stored"), Count("output_stored")
        biasld = Count("bias_landed")

        block = ctx.enter_context(nc.Block())
        E, VE, TE, GE = nc.scalar, nc.vector, nc.tensor, nc.gpsimd

        blocks = {"pe": 0, "hi": 0, "lo": 0}

        def split_hi(act, h):
            s = h % RING
            act.wait_ge(landed[s], 16 * (h // RING + 1))
            if h >= RING:
                act.wait_ge(used, h - (RING - 1))
            E.activation(w_hi[:, s, :], raw[:, s, :], ACT.Copy).then_inc(hi_done, 1)

        def split_lo(dve, h):
            s = h % RING
            dve.wait_ge(hi_done, h + 1)
            VE.tensor_tensor(w_lo[:, s, :], raw[:, s, :], w_hi[:, s, :].bitcast(F32),
                             ALU.subtract).then_inc(lo_done, 1)

        def next_split():
            h = blocks["hi"]
            if h >= n_stream:
                return
            blocks["hi"] += 1

            @block.scalar
            def _(act):
                split_hi(act, h)

            @block.vector
            def _(dve):
                split_lo(dve, h)

        @block.sync
        def _(sp):
            for s in range(RING):
                sp.dma_start(raw[:, s, :], a["stream"][s, :, :]).then_inc(landed[s], 16)
            with sp.Fori(1, n_stream // RING) as i:
                for s in range(RING):
                    sp.wait_ge(lo_done, i * RING + (s - RING + 1))
                    sp.dma_start(raw[:, s, :], a["stream"][bass.ds(i * RING + s, 1), :, :]
                                 .rearrange("a p n -> p (a n)")).then_inc(landed[s], 16)
            for h in range(n_stream // RING * RING, n_stream):
                sp.wait_ge(lo_done, h - RING + 1)
                sp.dma_start(raw[:, h % RING, :], a["stream"][h, :, :]).then_inc(landed[h % RING], 16)

        oh = ar(0, 512, parts=slice(0, 33))
        ohd = ar(512, 512, parts=slice(0, 32))
        relx = ar(1024, 16, parts=slice(0, 33))

        @block.gpsimd
        def _(pool):
            for dst, src in ((cols[:, :], a["cols"]), (cst[:, :], a["const"]),
                             (x[:, :, :], a["x"].rearrange("(q p) d -> p q d", p=P)),
                             (small[:, :], a["small"]), (rowv[:, :], a["rows"][0:1, :].to_broadcast([P, 48])),
                             (posi[:, :], a["positions"]), (oh, a["onehot"][:, 0:512]), (ohd, a["onehot"][0:32, 512:1024]),
                             (relx[0:32, :], a["small"][0:32, SML["relb"][0]:SML["relb"][1]])):
                pool.dma_start(dst, src).then_inc(inputs.sem, inputs.up(16))
            GE.memset(relx[32:33, :], NEG).then_inc(G.sem, G.up())
            pool.wait_ge(G.sem, G.n)
            GE.memset(st[:, 60:62], -0.5).then_inc(G.sem, G.up())

        mraw = ar(2048, 2, 4, MODC)
        modp = ar(6144, MODC)

        def mod_load(act, half, c, first=False):
            if not first:
                act.wait_ge(mod_used, c * 2 + (half - 1))
            act.dma_start(mraw[:, half, :, :], (a["mod_w"][c, half, :, :] if isinstance(c, int) else
                          a["mod_w"][bass.ds(c, 1), half, :, :].rearrange("a p n -> p (a n)"))
                          .rearrange("p (t n) -> p t n", t=4)).then_inc(mod_landed[half], 16)

        def mod_products(pe, c, first=False):
            for half in range(2):
                pe.wait_ge(mod_landed[half], c * 16 + 16)
                if half == 0 and not first:
                    pe.wait_ge(mod_kept, c)
                for t in range(4):
                    last = TE.matmul(ps[6][32 * t:32 * t + 32, :], cb[:, half * 4 + t, :], mraw[:, half, t, :],
                                     start=(half == 0), stop=(half == 1), tile_position=(0, 32 * t))
                last.then_inc(mod_used, 1)

        def mod_keep(dve, c, first=False):
            dve.wait_ge(mod_used, c * 2 + 2)
            if not first:
                dve.wait_ge(mod_cols, c)
            VE.tensor_copy(modp, ps[6][:, :]).then_inc(mod_kept, 1)

        def mod_turn(pe, c, first=False):
            pe.wait_ge(mod_kept, c + 1)
            if not first:
                pe.wait_ge(mod_added, c)
            for j in range(4):
                last = TE.matmul(ps[7][:, j:j + 1], modp[:, j * P:(j + 1) * P], cs("sel"), start=True, stop=True)
            last.then_inc(mod_cols, 1)

        def mod_add(dve, c):
            dve.wait_ge(mod_cols, c + 1)
            sl = slice(c * 4, c * 4 + 4) if isinstance(c, int) else bass.ds(c * 4, 4)
            bl = slice(COL["mod_b"][0] + c * 4, COL["mod_b"][0] + c * 4 + 4) if isinstance(c, int) \
                else bass.ds(c * 4 + COL["mod_b"][0], 4)
            VE.tensor_tensor(modc[:, sl], ps[7][:, 0:4], cols[:, bl], ALU.add).then_inc(mod_added, 1)

        @block.scalar
        def _(act):
            for half in range(2):
                mod_load(act, half, 0, first=True)
            act.wait_ge(inputs.sem, inputs.n)
            E.activation(st[:, 0:8], col("c", 0, 8), ACT.Silu).then_inc(A.sem, A.up())

        @block.vector
        def _(dve):
            dve.wait_ge(A.sem, A.n)
            VE.tensor_copy(cb[:, :, :], st[:, 0:8].unsqueeze(2).to_broadcast([P, KT, 32])).then_inc(V.sem, V.up())

        @block.tensor
        def _(pe):
            pe.wait_ge(V.sem, V.n)
            pe.wait_ge(G.sem, G.n)
            pe.wait_ge(inputs.sem, inputs.n)
            TE.matmul(ps[0][0:16, :], relx, oh, start=True, stop=True).then_inc(T.sem, T.up())
            for q in range(QT):
                for n in range(N_CMP):
                    d0 = 256 + q * P - (16 * n + 31)
                    last = TE.matmul(ps[1][:, (q * 16 + n) * 16:(q * 16 + n + 1) * 16], ohd[:, d0:d0 + P],
                                     sm("relb", rows=slice(0, 32)), start=True, stop=True)
            last.then_inc(T.sem, T.up())

        @block.vector
        def _(dve):
            dve.wait_ge(T.sem, T.n)
            dve.wait_ge(used, blocks["pe"])
            VE.tensor_copy(ar(1100, 512, parts=slice(0, 16)), ps[0][0:16, :]).then_inc(V.sem, V.up())
            for q in range(QT):
                VE.tensor_copy(biasc[:, q, 0:N_CMP, :],
                                 ps[1][:, q * 256:q * 256 + N_CMP * 16].rearrange("p (n h) -> p n h", h=16)).then_inc(V.sem, V.up())

        @block.scalar
        def _(act):
            act.wait_ge(V.sem, V.n)
            act.dma_start(u_dram, ar(1100, 384, parts=slice(0, 16)).unsqueeze(1)
                                  .to_broadcast([HEADS, P, 384])).then_inc(scratch.sem, scratch.up(16))
        for _i in range(RING):
            next_split()
        PRE = 5
        for c in range(PRE):
            @block.tensor
            def _(pe):
                mod_products(pe, c, first=c == 0)

            @block.scalar
            def _(act):
                for half in range(2):
                    mod_load(act, half, c + 1)

            @block.vector
            def _(dve):
                mod_keep(dve, c, first=c == 0)

            @block.tensor
            def _(pe):
                mod_turn(pe, c, first=c == 0)

            @block.vector
            def _(dve):
                mod_add(dve, c)

        def turn(src, n_kt, segs=None, scale=None, shift=None, kt0=0, dst=None):
            if segs:
                n = len(segs)

                @block.scalar
                def _(act):
                    act.wait_ge(V.sem, V.n)
                    act.wait_ge(A.sem, A.n)
                    for q in range(QT):
                        for s, (b, e) in enumerate(segs):
                            E.activation(dst(q)[:, b:e], src(q)[:, b:e], ACT.Square,
                                           accum_out=st[:, q * n + s:q * n + s + 1]).then_inc(A.sem, A.up())

                @block.vector
                def _(dve):
                    dve.wait_ge(A.sem, A.n)
                    b, e = segs[0]
                    if len({y - z for z, y in segs}) == 1:
                        VE.tensor_scalar(st[:, 8:8 + 2 * n], st[:, 0:2 * n], 1.0 / (e - b), EPS, ALU.mult, ALU.add).then_inc(V.sem, V.up())
                    else:
                        for q in range(QT):
                            for s, (b, e) in enumerate(segs):
                                i = q * n + s
                                VE.tensor_scalar(st[:, 8 + i:9 + i], st[:, i:i + 1], 1.0 / (e - b), EPS,
                                                   ALU.mult, ALU.add).then_inc(V.sem, V.up())

                @block.gpsimd
                def _(pool):
                    pool.wait_ge(V.sem, V.n)
                    GE.tensor_tensor(st[:, 16:16 + 2 * n], st[:, 8:8 + 2 * n],
                                       st[:, 60:61].to_broadcast([P, 2 * n]), ALU.pow).then_inc(G.sem, G.up())
                done = {}

                @block.vector
                def _(dve):
                    dve.wait_ge(G.sem, G.n)
                    for q in range(QT):
                        for s, (b, e) in enumerate(segs):
                            i = q * n + s
                            VE.tensor_scalar(dst(q)[:, b:e], src(q)[:, b:e], st[:, 16 + i:17 + i], None,
                                                         ALU.mult).then_inc(V.sem, V.up())
                            done[q] = V.n
                src = dst
            evac = {}
            for p in range(n_kt // 2):
                bank = ps[6 + p % 2]

                @block.tensor
                def _(pe):
                    if p < 2:
                        pe.wait_ge(V.sem, V.n)
                        pe.wait_ge(A.sem, A.n)
                    else:
                        pe.wait_ge(V.sem, evac[p - 2])
                    for k in range(2):
                        for q in range(QT):
                            kt = 2 * p + k
                            last = TE.transpose(bank[:, k * L + q * P:k * L + (q + 1) * P],
                                                src(q)[:, kt * P:(kt + 1) * P], ident)
                    last.then_inc(T.sem, T.up())

                @block.vector
                def _(dve):
                    dve.wait_ge(T.sem, T.n)
                    dve.wait_ge(used, blocks["pe"])
                    if p == 0:
                        dve.wait_ge(A.sem, A.n)
                    for k in range(2):
                        kt = 2 * p + k
                        sl = slice(k * L, (k + 1) * L)
                        if scale is None:
                            VE.tensor_copy(tmp[:, p % 2, sl], bank[:, sl]).then_inc(V.sem, V.up())
                        elif shift is None:
                            VE.tensor_scalar(tmp[:, p % 2, sl], bank[:, sl], scale(kt), None, ALU.mult).then_inc(V.sem, V.up())
                        else:
                            VE.tensor_scalar(tmp[:, p % 2, sl], bank[:, sl], scale(kt), shift(kt),
                                               ALU.mult, ALU.add).then_inc(V.sem, V.up())
                    evac[p] = V.n

                split_T(tmp[:, p % 2, :], kt0 + 2 * p, 2)

        def split_T(src, kt, n):
            @block.scalar
            def _(act):
                act.wait_ge(V.sem, V.n)
                act.wait_ge(T.sem, T.n)
                act.wait_ge(used, blocks["pe"])
                E.activation(t_hi[:, kt:kt + n, :].rearrange("p a b -> p (a b)"), src, ACT.Copy).then_inc(A.sem, A.up())

            @block.vector
            def _(dve):
                dve.wait_ge(A.sem, A.n)
                VE.tensor_tensor(t_lo[:, kt:kt + n, :].rearrange("p a b -> p (a b)"), src,
                                   t_hi[:, kt:kt + n, :].rearrange("p a b -> p (a b)").bitcast(F32), ALU.subtract).then_inc(V.sem, V.up())

        def triple(out, xh, xl, wh, wl, w_first, start, stop):
            for i, (xx, ww) in enumerate(((xh, wh), (xl, wh), (xh, wl))):
                lhs, rhs = (ww, xx) if w_first else (xx, ww)
                last = TE.matmul(out, lhs, rhs, start=start and i == 0, stop=stop and i == 2)
            return last

        def rows_product(n_kt, width, kt0=0, xh=None, xl=None):
            per = BLK // width
            hv = (width + 511) // 512
            wd = min(width, 512)
            kt = 0
            while kt < n_kt:
                h = blocks["pe"]
                blocks["pe"] += 1
                s = h % RING
                take = min(per, n_kt - kt)

                @block.tensor
                def _(pe):
                    if kt == 0:
                        pe.wait_ge(V.sem, V.n)
                        pe.wait_ge(A.sem, A.n)
                    pe.wait_ge(lo_done, h + 1)
                    for j in range(take):
                        k = kt0 + kt + j
                        for q in range(QT):
                            qs = slice(q * P, (q + 1) * P)
                            for f in range(hv):
                                ws = slice(j * width + f * 512, j * width + f * 512 + wd)
                                last = triple(ps[q * 2 + f][:, 0:wd], t_hi[:, k, qs], t_lo[:, k, qs],
                                              w_hi[:, s, ws], w_lo[:, s, ws], False,
                                              kt + j == 0, kt + j == n_kt - 1)
                    last.then_inc(used, 1)
                kt += take
                next_split()

        def columns_product(n_tiles, evac):
            free = {}
            for pair in range(n_tiles // 2):
                bank = ps[4 + pair % 2]
                for half in range(2):
                    h = blocks["pe"]
                    blocks["pe"] += 1
                    s = h % RING

                    @block.tensor
                    def _(pe):
                        if half == 0:
                            if pair < 2:
                                pe.wait_ge(V.sem, V.n)
                                pe.wait_ge(A.sem, A.n)
                            else:
                                pe.wait_ge(V.sem, free[pair - 2][0])
                                pe.wait_ge(A.sem, free[pair - 2][1])
                        pe.wait_ge(lo_done, h + 1)
                        wv_hi = w_hi[:, s, :].rearrange("p (k c) -> p k c", c=P)
                        wv_lo = w_lo[:, s, :].rearrange("p (k c) -> p k c", c=P)
                        for k in range(KT):
                            last = triple(bank[:, half * L:(half + 1) * L], t_hi[:, k, :], t_lo[:, k, :],
                                          wv_hi[:, k, :], wv_lo[:, k, :], True, k == 0, k == KT - 1)
                        last.then_inc(used, 1)
                    if half == 0:
                        next_split()
                evac(pair, bank)
                next_split()
                free[pair] = (V.n, A.n)

        def mod_first(c):
            @block.scalar
            def _(act):
                act.wait_ge(V.sem, V.n)
                act.wait_ge(T.sem, T.n)
                act.wait_ge(used, blocks["pe"])
                for half in range(2):
                    mod_load(act, half, c)

        def ffn(call, n_mod, mod0, residual):
            h0 = blocks["pe"]
            assert blocks["hi"] == h0 + RING

            hb = 2 * FG * call
            A0, V0 = A.n, V.n

            def slot(j):
                return (h0 + j) % RING

            def pe_body(pe, i, first, last_body, mod):
                for t in range(2):
                    for which in range(2):
                        j = 2 * t + which
                        pe.wait_ge(lo_done, h0 + j + 1 + RING * i)
                        if which == 0 and not (first and call == 0):
                            pe.wait_ge(gated, hb + 2 * i + (t - 1))
                        wh = w_hi[:, slot(j), :].rearrange("p (k c) -> p k c", c=P)
                        wl = w_lo[:, slot(j), :].rearrange("p (k c) -> p k c", c=P)
                        for k in range(KT):
                            last = triple(ps[4 + t][:, which * L:(which + 1) * L], t_hi[:, k, :], t_lo[:, k, :],
                                          wh[:, k, :], wl[:, k, :], True, k == 0, k == KT - 1)
                        last.then_inc(used, 1)
                    if t == 0 and mod is not None:
                        mod_products(pe, mod)
                for t in range(2):
                    j = 4 + t
                    pe.wait_ge(lo_done, h0 + j + 1 + RING * i)
                    pe.wait_ge(gate_lo, hb + t + 1 + 2 * i)
                    for q in range(QT):
                        qs = slice(q * P, (q + 1) * P)
                        for f in range(2):
                            fs = slice(f * 512, (f + 1) * 512)
                            last = triple(ps[2 * q + f][:, :], g_hi[:, t, qs], g_lo[:, t, qs],
                                          w_hi[:, slot(j), fs], w_lo[:, slot(j), fs], False,
                                          first and t == 0, last_body and t == 1)
                    last.then_inc(used, 1)
                    if t == 0 and mod is not None:
                        mod_turn(pe, mod)

            def hi_next(act, i, j, static):
                h = h0 + j + RING
                if static:
                    if h + RING * i >= n_stream:
                        return
                    split_hi(act, h + RING * i)
                    return
                s = slot(j)
                act.wait_ge(landed[s], 16 * (h // RING + 1) + 16 * i)
                act.wait_ge(used, h - (RING - 1) + RING * i)
                E.activation(w_hi[:, s, :], raw[:, s, :], ACT.Copy).then_inc(hi_done, 1)

            def lo_next(dve, i, j, static):
                h = h0 + j + RING
                if static:
                    if h + RING * i >= n_stream:
                        return
                    split_lo(dve, h + RING * i)
                    return
                s = slot(j)
                dve.wait_ge(hi_done, h + 1 + RING * i)
                VE.tensor_tensor(w_lo[:, s, :], raw[:, s, :], w_hi[:, s, :].bitcast(F32),
                                 ALU.subtract).then_inc(lo_done, 1)

            def act_body(act, i, static, mod, more):
                for t in range(2):
                    hi_next(act, i, 2 * t, static)
                    act.wait_ge(used, h0 + 2 * t + 2 + RING * i)
                    E.activation(act_s[:, t, 0:L], ps[4 + t][:, 0:L], ACT.Silu).then_inc(silu_done, 1)
                    act.wait_ge(gated, hb + t + 1 + 2 * i)
                    E.activation(g_hi[:, t, :], act_s[:, t, L:2 * L], ACT.Copy).then_inc(gate_hi, 1)
                    hi_next(act, i, 2 * t + 1, static)
                    if t == 0 and mod is not None and more:
                        for half in range(2):
                            mod_load(act, half, mod + 1)
                hi_next(act, i, 4, static)
                hi_next(act, i, 5, static)

            def dve_body(dve, i, static, mod):
                for t in range(2):
                    lo_next(dve, i, 2 * t, static)
                    dve.wait_ge(silu_done, hb + t + 1 + 2 * i)
                    VE.tensor_tensor(act_s[:, t, L:2 * L], ps[4 + t][:, L:2 * L], act_s[:, t, 0:L],
                                     ALU.mult).then_inc(gated, 1)
                    dve.wait_ge(gate_hi, hb + t + 1 + 2 * i)
                    VE.tensor_tensor(g_lo[:, t, :], act_s[:, t, L:2 * L], g_hi[:, t, :].bitcast(F32),
                                     ALU.subtract).then_inc(gate_lo, 1)
                    lo_next(dve, i, 2 * t + 1, static)
                    if t == 0 and mod is not None:
                        mod_keep(dve, mod)
                lo_next(dve, i, 4, static)
                if mod is not None:
                    mod_add(dve, mod)
                lo_next(dve, i, 5, static)

            def emit(lo, hi, mod_of):
                loop = hi - lo > 1

                @block.tensor
                def _(pe):
                    if lo == 0:
                        pe.wait_ge(V.sem, V0)
                        pe.wait_ge(A.sem, A0)
                    if loop:
                        with pe.Fori(lo, hi) as i:
                            pe_body(pe, i, False, False, mod_of(i))
                    else:
                        pe_body(pe, lo, lo == 0, lo == FG - 1, mod_of(lo))

                @block.scalar
                def _(act):
                    if loop:
                        with act.Fori(lo, hi) as i:
                            act_body(act, i, False, mod_of(i), True)
                    else:
                        m = mod_of(lo)
                        act_body(act, lo, True, m, m is not None and lo + 1 < n_mod)

                @block.vector
                def _(dve):
                    if loop:
                        with dve.Fori(lo, hi) as i:
                            dve_body(dve, i, False, mod_of(i))
                    else:
                        dve_body(dve, lo, True, mod_of(lo))

            def with_mod(i):
                return i + mod0

            def no_mod(i):
                return None
            if n_mod:
                blocks["hi"] = h0 + RING
                emit(0, 1, with_mod)
                if n_mod == FG:
                    emit(1, FG - 1, with_mod)
                    emit(FG - 1, FG, with_mod)
                else:
                    emit(1, n_mod - 1, with_mod)
                    emit(n_mod - 1, n_mod, with_mod)
                    for i in range(n_mod, FG):
                        emit(i, i + 1, no_mod)
            else:
                emit(0, 1, no_mod)
                emit(1, FG - 1, no_mod)
                emit(FG - 1, FG, no_mod)
            blocks["pe"] = h0 + FG * RING
            blocks["hi"] = min(n_stream, h0 + FG * RING + RING)

            add_residual(residual)

        def make_row(colsrc):
            @block.vector
            def _(dve):
                dve.wait_ge(A.sem, A.n)
                dve.wait_ge(T.sem, T.n)
                dve.wait_ge(used, blocks["pe"])
                dve.wait_ge(mod_added, 1)
                for k in range(KT):
                    VE.tensor_scalar(ar(AW - 1024, KT, P)[:, k, :], ident, colsrc(k), None, ALU.mult).then_inc(V.sem, V.up())

            @block.tensor
            def _(pe):
                pe.wait_ge(V.sem, V.n)
                for k in range(KT):
                    last = TE.matmul(ps[6 + k // 4][:, (k % 4) * P:(k % 4 + 1) * P], cs("ones"),
                                     ar(AW - 1024, KT, P)[:, k, :], start=True, stop=True)
                last.then_inc(T.sem, T.up())

        def add_residual(kind):
            if kind is not None:
                m0, factor = kind
                make_row(lambda k: modc[:, m0 + k:m0 + k + 1])

                @block.vector
                def _(dve):
                    dve.wait_ge(T.sem, T.n)
                    dve.wait_ge(used, blocks["pe"])
                    for k in range(2):
                        VE.tensor_scalar(grow[:, k * 512:(k + 1) * 512], ps[6 + k][:, :], float(factor), None,
                                           ALU.mult).then_inc(V.sem, V.up())

            @block.vector
            def _(dve):
                dve.wait_ge(T.sem, T.n)
                dve.wait_ge(used, blocks["pe"])
                dve.wait_ge(A.sem, A.n)
                for q in range(QT):
                    for f in range(2):
                        fs = slice(f * 512, (f + 1) * 512)
                        if kind is not None:
                            dve.wait_ge(V.sem, V.n)
                            VE.tensor_tensor(tmp[:, f, :], ps[2 * q + f][:, :], grow[:, fs], ALU.mult).then_inc(V.sem, V.up())
                            r = V.n
                            dve.wait_ge(V.sem, r)
                            VE.tensor_tensor(x[:, q, fs], x[:, q, fs], tmp[:, f, :], ALU.add).then_inc(V.sem, V.up())
                        else:
                            VE.tensor_tensor(x[:, q, fs], x[:, q, fs], ps[2 * q + f][:, :], ALU.add).then_inc(V.sem, V.up())

        XN = AW - 2048

        def norm_x(gain, mods=None):
            if mods is not None:
                sh, sc = mods

                @block.vector
                def _(dve):
                    dve.wait_ge(T.sem, T.n)
                    dve.wait_ge(used, blocks["pe"])
                    dve.wait_ge(mod_added, (max(sh, sc) + 8) // 4)
                    VE.scalar_tensor_tensor(out=sg[:, :], in0=modc[:, sc:sc + 8], scalar=1.0, in1=gain(0, 8),
                                              op0=ALU.add, op1=ALU.mult).then_inc(V.sem, V.up())
                    dve.wait_ge(V.sem, V.n)
                turn(lambda q: x[:, q, :], KT, [(0, D)], lambda k: sg[:, k:k + 1], lambda k: modc[:, sh + k:sh + k + 1],
                     dst=lambda q: ar(XN, QT, D)[:, q, :])
            else:
                turn(lambda q: x[:, q, :], KT, [(0, D)], lambda k: gain(k, 1), None,
                     dst=lambda q: ar(XN, QT, D)[:, q, :])

        def mod_at(layer, which):
            return layer * 72 + which * 8

        def small_product(bank, width, name):
            @block.tensor
            def _(pe):
                pe.wait_ge(V.sem, V.n)
                pe.wait_ge(A.sem, A.n)
                for q in range(QT):
                    for k in range(KT):
                        for i, part in enumerate((t_hi, t_lo)):
                            last = TE.matmul(bank[:, q * width:(q + 1) * width],
                                             part[:, k, q * P:(q + 1) * P].bitcast(F32),
                                             sm(name, k * width, (k + 1) * width),
                                             start=(k == 0 and i == 0), stop=(k == KT - 1 and i == 1))
                last.then_inc(T.sem, T.up())

        norm_x(lambda k, n: col("norm_g", k, n), (mod_at(0, 0), mod_at(0, 1)))
        ffn(0, FG, PRE, (mod_at(0, 2), 0.5))

        norm_x(lambda k, n: col("norm_g", 8 + k, n), (mod_at(0, 3), mod_at(0, 4)))
        xb = ar(0, 12, 259)
        xc = ar(3108, 12, L)
        up = ar(6180, 4, 272)
        zt = ar(7268, QT, D)
        xdt, xde = ar(0, QT, D), ar(2048, D)
        xs = ar(9316, QT, D)
        ys = ar(11364, QT, D)
        btok = ar(13412, 2, P)
        s0 = 13668
        dtr, dtm, dte, dtu, dtv, adt, acs, eacs = (ar(s0 + 32 * k, QT, 16) for k in range(8))
        flat = {id(v): ar(s0 + 32 * k, 32) for k, v in enumerate((dtr, dtm, dte, dtu, dtv, adt, acs, eacs))}
        alog, dend = ar(s0 + 256, 16), ar(s0 + 272, 16)
        decay = ar(13960, 2, 512)
        state = ar(14984, D)

        @block.vector
        def _(dve):
            dve.wait_ge(T.sem, T.n)
            dve.wait_ge(used, blocks["pe"])
            dve.wait_ge(A.sem, A.n)
            VE.memset(xb[:, :, 0:3], 0.0).then_inc(V.sem, V.up())
            VE.memset(up[:, :, 0:16], 0.0).then_inc(V.sem, V.up())

        small_product(ps[0], 16, "dt_w")

        @block.vector
        def _(dve):
            dve.wait_ge(T.sem, T.n)
            dve.wait_ge(used, blocks["pe"])
            VE.tensor_tensor(dtr, ps[0][:, 0:32].rearrange("p (q h) -> p q h", h=16),
                               rowv[:, 0:16].unsqueeze(1).to_broadcast([P, QT, 16]), ALU.add).then_inc(V.sem, V.up())
            dve.wait_ge(V.sem, V.n)
            VE.tensor_scalar(dtu, dtr, -1.0, None, ALU.mult).then_inc(V.sem, V.up())
            VE.tensor_scalar(dtm, dtr, 0.0, None, ALU.max).then_inc(V.sem, V.up())
            dve.wait_ge(V.sem, V.n)
            VE.tensor_tensor(dtu, dtu, dtr, ALU.min).then_inc(V.sem, V.up())

        @block.scalar
        def _(act):
            act.wait_ge(V.sem, V.n)
            E.activation(dte, dtu, ACT.Exp).then_inc(A.sem, A.up())
            E.activation(alog, rowv[:, 16:32], ACT.Exp).then_inc(A.sem, A.up())

        @block.vector
        def _(dve):
            dve.wait_ge(A.sem, A.n)
            VE.tensor_scalar(dtu, dte, 1.0, None, ALU.add).then_inc(V.sem, V.up())

        @block.scalar
        def _(act):
            act.wait_ge(V.sem, V.n)
            E.activation(dtv, dtu, ACT.Ln).then_inc(A.sem, A.up())

        @block.vector
        def _(dve):
            dve.wait_ge(A.sem, A.n)
            VE.tensor_tensor(dtm, dtm, dtv, ALU.add).then_inc(V.sem, V.up())
            VE.tensor_scalar(adt, dtu, -1.0, None, ALU.add).then_inc(V.sem, V.up())
            dve.wait_ge(V.sem, V.n)
            VE.tensor_tensor(dte, dte, adt, ALU.subtract).then_inc(V.sem, V.up())
            VE.reciprocal(dtu, dtu).then_inc(V.sem, V.up())
            dve.wait_ge(V.sem, V.n)
            VE.tensor_tensor(dte, dte, dtu, ALU.mult).then_inc(V.sem, V.up())
            dve.wait_ge(V.sem, V.n)
            VE.tensor_tensor(dtr, dtm, dte, ALU.add).then_inc(V.sem, V.up())
            VE.tensor_scalar(alog, alog, -1.0, None, ALU.mult).then_inc(V.sem, V.up())
            dve.wait_ge(V.sem, V.n)
            VE.tensor_tensor(adt, dtr, alog.unsqueeze(1).to_broadcast([P, QT, 16]), ALU.mult).then_inc(V.sem, V.up())

        def evac_xbc(pair, bank):
            dst = xb[:, 2 * pair:2 * pair + 2, 3:259] if pair < 6 else up[:, 2 * pair - 12:2 * pair - 10, 16:272]

            @block.scalar
            def _(act):
                act.wait_ge(T.sem, T.n)
                act.wait_ge(used, blocks["pe"])
                act.wait_ge(V.sem, V.n)
                E.activation(dst, bank[:, :].rearrange("p (a b) -> p a b", b=L), ACT.Copy).then_inc(A.sem, A.up())
            if pair >= 6:
                return

            @block.vector
            def _(dve):
                dve.wait_ge(A.sem, A.n)
                for k in range(4):
                    for tl in (2 * pair, 2 * pair + 1):
                        if k == 0:
                            VE.tensor_scalar(xc[:, tl, :], xb[:, tl, 0:L], col("conv_w", tl), col("conv_b", tl),
                                               ALU.mult, ALU.add).then_inc(V.sem, V.up())
                        else:
                            VE.scalar_tensor_tensor(out=xc[:, tl, :], in0=xb[:, tl, k:k + L],
                                                      scalar=col("conv_w", 12 * k + tl), in1=xc[:, tl, :],
                                                      op0=ALU.mult, op1=ALU.add).then_inc(V.sem, V.up())
                    if k < 3:
                        dve.wait_ge(V.sem, V.n)

            @block.scalar
            def _(act):
                act.wait_ge(V.sem, V.n)
                E.activation(xc[:, 2 * pair:2 * pair + 2, :], xc[:, 2 * pair:2 * pair + 2, :], ACT.Silu).then_inc(A.sem, A.up())

        columns_product(16, evac_xbc)
        rows_product(KT, D)

        for g, win in enumerate((2, 4, 8, 16)):
            u = up[:, g, :]
            bufs = [act_s[:, 0, 0:272], act_s[:, 1, 0:272]]

            @block.vector
            def _(dve):
                dve.wait_ge(A.sem, A.n)
                dve.wait_ge(T.sem, T.n)
                dve.wait_ge(used, blocks["pe"])
                cur, k, w_ = u, 0, 1
                while w_ < win:
                    dve.wait_ge(V.sem, V.n)
                    VE.tensor_tensor(bufs[k][:, 2 * w_:272], cur[:, 2 * w_:272], cur[:, w_:272 - w_], ALU.add).then_inc(V.sem, V.up())
                    cur, k, w_ = bufs[k], 1 - k, 2 * w_
                dve.wait_ge(V.sem, V.n)
                o = bufs[k]
                VE.tensor_scalar(o[:, 16:272], cur[:, 16:272], 1.0 / win, None, ALU.mult).then_inc(V.sem, V.up())
                dve.wait_ge(V.sem, V.n)
                VE.tensor_tensor(o[:, 16:32], cur[:, 16:32], cs("recip", 16 * g, 16 * g + 16), ALU.mult).then_inc(V.sem, V.up())
                dve.wait_ge(V.sem, V.n)
                VE.tensor_tensor(o[:, 16:272], o[:, 16:272], u[:, 16:272], ALU.subtract).then_inc(V.sem, V.up())
            k = {2: 1, 4: 0, 8: 1, 16: 0}[win]

            @block.tensor
            def _(pe):
                pe.wait_ge(V.sem, V.n)
                pe.wait_ge(A.sem, A.n)
                TE.matmul(ps[6][:, 0:L], sm("pool_w", g * P, (g + 1) * P), bufs[k][:, 16:272], start=True, stop=True).then_inc(T.sem, T.up())

            @block.vector
            def _(dve):
                dve.wait_ge(T.sem, T.n)
                dve.wait_ge(used, blocks["pe"])
                dve.wait_ge(A.sem, A.n)
                VE.tensor_scalar(tmp[:, g // 2, (g % 2) * L:(g % 2 + 1) * L], ps[6][:, 0:L], col("pool_scale", g),
                                   None, ALU.mult).then_inc(V.sem, V.up())
            if g % 2:
                split_T(tmp[:, g // 2, :], 8 + g - 1, 2)

        @block.scalar
        def _(act):
            act.wait_ge(T.sem, T.n)
            act.wait_ge(used, blocks["pe"])
            for q in range(QT):
                for f in range(2):
                    E.activation(zt[:, q, f * 512:(f + 1) * 512], ps[2 * q + f][:, :], ACT.Silu).then_inc(A.sem, A.up())


        @block.tensor
        def _(pe):
            pe.wait_ge(V.sem, V.n)
            pe.wait_ge(A.sem, A.n)
            for c in range(QT):
                TE.matmul(ps[7][:, c * 16:(c + 1) * 16], cs("upper"), adt[:, c, :], start=True, stop=True)
            TE.matmul(ps[7][:, 32:48], cs("ones"), adt[:, 0, :], start=True, stop=True).then_inc(T.sem, T.up())

        @block.vector
        def _(dve):
            dve.wait_ge(T.sem, T.n)
            dve.wait_ge(used, blocks["pe"])
            VE.tensor_copy(acs, ps[7][:, 0:32].rearrange("p (q h) -> p q h", h=16)).then_inc(V.sem, V.up())
            dve.wait_ge(V.sem, V.n)
            VE.tensor_tensor(dend, ps[7][:, 32:48], acs[:, 0, :], ALU.subtract).then_inc(V.sem, V.up())

        @block.scalar
        def _(act):
            act.wait_ge(V.sem, V.n)
            E.activation(dend, dend, ACT.Exp).then_inc(A.sem, A.up())
            E.activation(eacs, acs, ACT.Exp).then_inc(A.sem, A.up())

        for n in range(5):
            bank = ps[4 + n % 2]
            q, t0 = (n // 2, 4 * (n % 2)) if n < 4 else (0, 8)
            tiles = 4 if n < 4 else 2

            @block.tensor
            def _(pe):
                pe.wait_ge(A.sem, A.n)
                pe.wait_ge(V.sem, V.n)
                for k in range(tiles):
                    last = TE.transpose(bank[:, k * P:(k + 1) * P], xc[:, t0 + k, q * P:(q + 1) * P], ident)
                last.then_inc(T.sem, T.up())

            @block.scalar
            def _(act):
                act.wait_ge(T.sem, T.n)
                act.wait_ge(used, blocks["pe"])
                if n < 4:
                    E.activation(xs[:, q, t0 * P:(t0 + 4) * P], bank[:, :], ACT.Copy).then_inc(A.sem, A.up())
                else:
                    E.activation(btok[:, :, :].rearrange("p a b -> p (a b)"), bank[:, 0:2 * P], ACT.Copy).then_inc(A.sem, A.up())

        @block.vector
        def _(dve):
            dve.wait_ge(A.sem, A.n)
            for q in range(QT):
                VE.tensor_tensor(xdt[:, q, :].rearrange("p (h d) -> p h d", d=64),
                                   xs[:, q, :].rearrange("p (h d) -> p h d", d=64),
                                   dtr[:, q, :].unsqueeze(2).to_broadcast([P, 16, 64]), ALU.mult).then_inc(V.sem, V.up())
            dve.wait_ge(V.sem, V.n)
            VE.tensor_tensor(xde.rearrange("p (h d) -> p h d", d=64), xdt[:, 0, :].rearrange("p (h d) -> p h d", d=64),
                               dend.unsqueeze(2).to_broadcast([P, 16, 64]), ALU.mult).then_inc(V.sem, V.up())

        @block.tensor
        def _(pe):
            pe.wait_ge(V.sem, V.n)
            pe.wait_ge(A.sem, A.n)
            for c in range(QT):
                for g in range(2):
                    last = TE.matmul(ps[6][:, (2 * c + g) * P:(2 * c + g + 1) * P], xc[:, 8 + g, c * P:(c + 1) * P],
                                     xc[:, 10 + g, c * P:(c + 1) * P], start=True, stop=True)
            for g in range(2):
                last = TE.matmul(ps[4 + g][:, :], btok[:, g, :], xde[:, g * 512:(g + 1) * 512], start=True, stop=True)
            last.then_inc(T.sem, T.up())
        cbt = tmp[:, 0, :]

        @block.vector
        def _(dve):
            dve.wait_ge(T.sem, T.n)
            dve.wait_ge(used, blocks["pe"])
            dve.wait_ge(A.sem, A.n)
            VE.tensor_copy(cbt, ps[6][:, :]).then_inc(V.sem, V.up())
            for g in range(2):
                VE.tensor_copy(state[:, g * 512:(g + 1) * 512], ps[4 + g][:, :]).then_inc(V.sem, V.up())
        for c in range(QT):
            for quad in range(4):
                n = 4 * c + quad
                g = quad // 2
                bank, out = ps[6 + n % 2], ps[2 * c + g]

                @block.tensor
                def _(pe):
                    pe.wait_ge(V.sem, V.n)
                    for h in range(4):
                        last = TE.matmul(bank[:, h * P:(h + 1) * P],
                                         adt[:, c, 4 * quad + h:4 * quad + h + 1].to_broadcast([P, P]), cs("upper"),
                                         start=True, stop=True)
                    last.then_inc(T.sem, T.up())

                @block.vector
                def _(dve):
                    dve.wait_ge(T.sem, T.n)
                    dve.wait_ge(used, blocks["pe"])
                    for h in range(4):
                        VE.scalar_tensor_tensor(out=decay[:, n % 2, h * P:(h + 1) * P],
                                                  in0=bank[:, h * P:(h + 1) * P],
                                                  scalar=acs[:, c, 4 * quad + h:4 * quad + h + 1], in1=cs("ssd_mask"),
                                                  op0=ALU.subtract, op1=ALU.add).then_inc(V.sem, V.up())

                @block.scalar
                def _(act):
                    act.wait_ge(V.sem, V.n)
                    E.activation(decay[:, n % 2, :], decay[:, n % 2, :], ACT.Exp).then_inc(A.sem, A.up())

                @block.vector
                def _(dve):
                    dve.wait_ge(A.sem, A.n)
                    VE.tensor_tensor(decay[:, n % 2, :].rearrange("p (h s) -> p h s", s=P),
                                       decay[:, n % 2, :].rearrange("p (h s) -> p h s", s=P),
                                       cbt[:, (2 * c + g) * P:(2 * c + g + 1) * P].unsqueeze(1).to_broadcast([P, 4, P]),
                                       ALU.mult).then_inc(V.sem, V.up())

                @block.tensor
                def _(pe):
                    pe.wait_ge(V.sem, V.n)
                    for h in range(4):
                        hh = 4 * quad + h
                        last = TE.matmul(out[:, (hh % 8) * 64:(hh % 8 + 1) * 64], decay[:, n % 2, h * P:(h + 1) * P],
                                         xdt[:, c, hh * 64:(hh + 1) * 64], start=True, stop=True)
                    last.then_inc(T.sem, T.up())

        @block.tensor
        def _(pe):
            for g in range(2):
                last = TE.matmul(ps[4 + g][:, :], xc[:, 10 + g, P:2 * P], state[:, g * 512:(g + 1) * 512],
                                 start=True, stop=True)
            last.then_inc(T.sem, T.up())

        @block.vector
        def _(dve):
            dve.wait_ge(T.sem, T.n)
            dve.wait_ge(used, blocks["pe"])
            for q in range(QT):
                for g in range(2):
                    gs = slice(g * 512, (g + 1) * 512)
                    y3 = ys[:, q, gs].rearrange("p (h d) -> p h d", d=64)
                    VE.tensor_tensor(y3, xs[:, q, gs].rearrange("p (h d) -> p h d", d=64),
                                       rowv[:, 32 + 8 * g:40 + 8 * g].unsqueeze(2).to_broadcast([P, 8, 64]), ALU.mult).then_inc(V.sem, V.up())
                    dve.wait_ge(V.sem, V.n)
                    VE.tensor_tensor(ys[:, q, gs], ys[:, q, gs], ps[2 * q + g][:, :], ALU.add).then_inc(V.sem, V.up())
                    if q == 1:
                        VE.tensor_tensor(tmp[:, 1, :].rearrange("p (h d) -> p h d", d=64),
                                               ps[4 + g][:, :].rearrange("p (h d) -> p h d", d=64),
                                               eacs[:, 1, 8 * g:8 * g + 8].unsqueeze(2).to_broadcast([P, 8, 64]),
                                               ALU.mult).then_inc(V.sem, V.up())
                        r = V.n
                        dve.wait_ge(V.sem, r)
                        VE.tensor_tensor(ys[:, q, gs], ys[:, q, gs], tmp[:, 1, :], ALU.add).then_inc(V.sem, V.up())
                    dve.wait_ge(V.sem, V.n)
                    VE.tensor_tensor(ys[:, q, gs], ys[:, q, gs], zt[:, q, gs], ALU.mult).then_inc(V.sem, V.up())
        turn(lambda q: ys[:, q, :], KT, [(0, 512), (512, 1024)], lambda k: col("ssd_norm", k), None,
             dst=lambda q: xs[:, q, :])
        rows_product(12, D)
        add_residual((mod_at(0, 5), 1.0))

        mod_first(PRE + FG)
        norm_x(lambda k, n: col("norm_g", 16 + k, n), (mod_at(0, 6), mod_at(0, 7)))
        ffn(1, FG, PRE + FG, (mod_at(0, 8), 0.5))
        mod_first(PRE + 2 * FG)
        norm_x(lambda k, n: col("norm_g", 24 + k, n), (mod_at(1, 0), mod_at(1, 1)))
        ffn(2, N_MOD - PRE - 2 * FG, PRE + 2 * FG, (mod_at(1, 2), 0.5))
        def attention(n, spans, dk, scores, values, dv, out, scale, bias, prepare=None, v0=0):
            at = [0]
            for kts in spans:
                at.append(at[-1] + P * len(kts))
            width = at[-1]
            prep_done, prep_free, exp_done, sc_free, pt_done, pt_evac, out_done = {}, {}, {}, {}, {}, {}, {}
            s_used, pv_done = {}, {}
            start = (V.n, A.n)
            for step in range(n + 3):
                h = step
                if prepare is not None and h < n:
                    prepare(h, prep_done, prep_free, start)
                h = step - 1
                if 0 <= h < n:
                    bank = ps[2 + h % 2]
                    sl = act_s[:, h % 2, 0:width]
                    nm, sums = st[:, 20 + 4 * (h % 2):22 + 4 * (h % 2)], st[:, 32 + 2 * (h % 4):34 + 2 * (h % 4)]

                    @block.tensor
                    def _(pe):
                        pe.wait_ge(V.sem, sc_free.get(h - 2, start[0]))
                        pe.wait_ge(A.sem, prep_done.get(h, start[1]))
                        for q, kts in enumerate(spans):
                            steps = scores(h, q, kts)
                            for i, (lhs, rhs) in enumerate(steps):
                                last = TE.matmul(bank[:, at[q]:at[q + 1]], lhs, rhs, start=i == 0,
                                                 stop=i == len(steps) - 1)
                        last.then_inc(T.sem, T.up())
                        prep_free[h] = T.n

                    @block.vector
                    def _(dve):
                        dve.wait_ge(T.sem, prep_free[h])
                        if bias is None:
                            VE.tensor_scalar(sl, bank[:, 0:width], scale, None, ALU.mult).then_inc(V.sem, V.up())
                            sc_free[h] = V.n
                        else:
                            for lo, hi, b in bias(h):
                                VE.scalar_tensor_tensor(out=sl[:, lo:hi], in0=bank[:, lo:hi],
                                                                       scalar=scale, in1=b, op0=ALU.mult,
                                                                       op1=ALU.add).then_inc(V.sem, V.up())
                                sc_free[h] = V.n
                        dve.wait_ge(V.sem, V.n)
                        for q in range(QT):
                            VE.tensor_reduce(nm[:, q:q + 1], sl[:, at[q]:at[q + 1]], AX, ALU.max, negate=True).then_inc(V.sem, V.up())

                    @block.scalar
                    def _(act):
                        act.wait_ge(V.sem, V.n)
                        for q in range(QT):
                            E.activation(sl[:, at[q]:at[q + 1]], sl[:, at[q]:at[q + 1]], ACT.Exp,
                                                         bias=nm[:, q:q + 1], accum_out=sums[:, q:q + 1]).then_inc(A.sem, A.up())
                            exp_done[h] = A.n
                h = step - 2
                if 0 <= h < n:
                    sl = act_s[:, h % 2, 0:width]
                    pbank = ps[4 + h % 2]

                    @block.tensor
                    def _(pe):
                        pe.wait_ge(A.sem, exp_done[h])
                        pe.wait_ge(A.sem, pt_evac.get(h - 2, 0))
                        for k in range(width // P):
                            last = TE.transpose(pbank[:, k * P:(k + 1) * P], sl[:, k * P:(k + 1) * P], ident)
                        last.then_inc(T.sem, T.up())
                        s_used[h] = T.n

                    @block.scalar
                    def _(act):
                        act.wait_ge(T.sem, s_used[h])
                        E.activation(tmp[:, h % 2, 0:width], pbank[:, 0:width], ACT.Copy).then_inc(A.sem, A.up())
                        pt_evac[h] = A.n
                h = step - 3
                if 0 <= h < n:
                    obank = ps[6 + h % 2]
                    sums, rinv = st[:, 32 + 2 * (h % 4):34 + 2 * (h % 4)], st[:, 40 + 2 * (h % 4):42 + 2 * (h % 4)]

                    @block.tensor
                    def _(pe):
                        pe.wait_ge(A.sem, pt_evac[h])
                        pe.wait_ge(V.sem, out_done.get(h - 2, start[0]))
                        for q, kts in enumerate(spans):
                            for i, kt in enumerate(kts):
                                c = at[q] + i * P
                                last = TE.matmul(obank[:, q * dv:(q + 1) * dv], tmp[:, h % 2, c:c + P], values(h, kt),
                                                 start=i == 0, stop=i == len(kts) - 1)
                        last.then_inc(T.sem, T.up())
                        pv_done[h] = T.n

                    @block.vector
                    def _(dve):
                        dve.wait_ge(T.sem, pv_done[h])
                        dve.wait_ge(A.sem, exp_done[h])
                        out(dve, h, obank, sums, rinv)
                        out_done[h] = V.n

        norm_x(lambda k, n: col("norm_g", 32 + k, n), (mod_at(1, 3), mod_at(1, 4)))
        qa = ar(0, QT, D)
        qm = ar(2048, QT, 1536)
        kf = ar(5120, QT, 1536)
        vm = ar(8192, QT, D)
        om = ar(10240, QT, D)
        qk = ar(12288, 2, 512)
        kr = ar(13312, QT, 32)
        cosr, sinr = ar(13376, QT, 16), ar(13408, QT, 16)
        ang, rnd = ar(13440, QT, 16), ar(13472, QT, 16)
        posf = ar(13504, QT)
        rt = [ar(13520 + 256 * k, 256) for k in range(4)]

        @block.vector
        def _(dve):
            dve.wait_ge(T.sem, T.n)
            dve.wait_ge(used, blocks["pe"])
            dve.wait_ge(A.sem, A.n)
            TWO_PI = 2 * math.pi
            parts, rest = [], TWO_PI
            for bits in (6, 9, 22):
                c = float(np.float32(math.floor(rest * 2 ** bits) / 2 ** bits)) if bits < 22 else float(np.float32(rest))
                parts.append(c)
                rest -= c
            big = 1.5 * 2.0 ** 23
            edge = 3.1415925
            VE.tensor_copy(posf, posi[:, :]).then_inc(V.sem, V.up())
            dve.wait_ge(V.sem, V.n)
            for q in range(QT):
                VE.tensor_scalar(ang[:, q, :], cs("invf"), posf[:, q:q + 1], None, ALU.mult).then_inc(V.sem, V.up())
            dve.wait_ge(V.sem, V.n)
            VE.tensor_scalar(rnd, ang, 1.0 / TWO_PI, big, ALU.mult, ALU.add).then_inc(V.sem, V.up())
            dve.wait_ge(V.sem, V.n)
            VE.tensor_scalar(rnd, rnd, -big, None, ALU.add).then_inc(V.sem, V.up())
            for c in parts:
                dve.wait_ge(V.sem, V.n)
                VE.scalar_tensor_tensor(out=ang, in0=rnd, scalar=-c, in1=ang, op0=ALU.mult, op1=ALU.add).then_inc(V.sem, V.up())
            dve.wait_ge(V.sem, V.n)
            VE.tensor_scalar(rnd, ang, math.pi / 2, -TWO_PI, ALU.is_gt, ALU.mult).then_inc(V.sem, V.up())
            dve.wait_ge(V.sem, V.n)
            VE.scalar_tensor_tensor(out=rnd, in0=ang, scalar=math.pi / 2, in1=rnd, op0=ALU.add, op1=ALU.add).then_inc(V.sem, V.up())
            dve.wait_ge(V.sem, V.n)
            for v in (ang, rnd):
                VE.tensor_scalar(v, v, edge, -edge, ALU.min, ALU.max).then_inc(V.sem, V.up())

        @block.scalar
        def _(act):
            act.wait_ge(V.sem, V.n)
            E.activation(sinr, ang, ACT.Sin).then_inc(A.sem, A.up())
            E.activation(cosr, rnd, ACT.Sin).then_inc(A.sem, A.up())

        def rope(dve, dst, src, q, heads, out1, out2):
            def wide(v):
                return v[:, q, :].unsqueeze(1).to_broadcast([P, heads, 16])
            t = [r[:, 0:heads * 16].rearrange("p (h d) -> p h d", d=16) for r in rt]
            x1, x2 = src[:, :, 0:16], src[:, :, 16:32]
            VE.tensor_tensor(t[0], x1, wide(cosr), ALU.mult).then_inc(V.sem, V.up())
            VE.tensor_tensor(t[1], x2, wide(sinr), ALU.mult).then_inc(V.sem, V.up())
            VE.tensor_tensor(t[2], x2, wide(cosr), ALU.mult).then_inc(V.sem, V.up())
            VE.tensor_tensor(t[3], x1, wide(sinr), ALU.mult).then_inc(V.sem, V.up())
            dve.wait_ge(V.sem, V.n)
            VE.tensor_tensor(out1, t[0], t[1], ALU.subtract).then_inc(V.sem, V.up())
            VE.tensor_tensor(out2, t[2], t[3], ALU.add).then_inc(V.sem, V.up())
            dve.wait_ge(V.sem, V.n)

        small_product(ps[4], 32, "rope_w")

        @block.vector
        def _(dve):
            dve.wait_ge(T.sem, T.n)
            dve.wait_ge(used, blocks["pe"])
            dve.wait_ge(A.sem, A.n)
            VE.tensor_copy(kr, ps[4][:, 0:64].rearrange("p (q n) -> p q n", n=32)).then_inc(V.sem, V.up())
            dve.wait_ge(V.sem, V.n)
            for q in range(QT):
                k3 = kf[:, q, :].rearrange("p (h d) -> p h d", d=96)
                s3 = kr[:, q, :].rearrange("p (h d) -> p h d", d=32)
                rope(dve, None, s3, q, 1, kr[:, q, 0:16].unsqueeze(1), kr[:, q, 16:32].unsqueeze(1))
                VE.tensor_copy(k3[:, :, 64:96], kr[:, q, :].unsqueeze(1).to_broadcast([P, HEADS, 32])).then_inc(V.sem, V.up())

        rows_product(KT, D)

        @block.scalar
        def _(act):
            act.wait_ge(T.sem, T.n)
            act.wait_ge(used, blocks["pe"])
            for q in range(QT):
                for f in range(2):
                    E.activation(qa[:, q, f * 512:(f + 1) * 512], ps[2 * q + f][:, :], ACT.Copy).then_inc(A.sem, A.up())

        turn(lambda q: qa[:, q, :], KT, [(0, 768), (768, 1024)],
             lambda k: col("q_norm", k) if k < 6 else col("kv_norm", k - 6), None, dst=lambda q: ar(XN - 512, QT, D)[:, q, :])
        rows_product(6, D)

        @block.scalar
        def _(act):
            act.wait_ge(T.sem, T.n)
            act.wait_ge(used, blocks["pe"])
            for q in range(QT):
                for f in range(2):
                    E.activation(qm[:, q, f * 512:(f + 1) * 512], ps[2 * q + f][:, :], ACT.Copy).then_inc(A.sem, A.up())
        rows_product(6, 512)

        @block.scalar
        def _(act):
            act.wait_ge(T.sem, T.n)
            act.wait_ge(used, blocks["pe"])
            for q in range(QT):
                E.activation(qm[:, q, 1024:1536], ps[2 * q][:, :], ACT.Copy).then_inc(A.sem, A.up())

        @block.vector
        def _(dve):
            dve.wait_ge(A.sem, A.n)
            for q in range(QT):
                q3 = qm[:, q, :].rearrange("p (h d) -> p h d", d=96)
                rope(dve, None, q3[:, :, 64:96], q, HEADS, q3[:, :, 64:80], q3[:, :, 80:96])
        for part in range(2):
            rows_product(2, D, kt0=6)

            @block.scalar
            def _(act):
                act.wait_ge(T.sem, T.n)
                act.wait_ge(used, blocks["pe"])
                act.wait_ge(V.sem, V.n)
                for q in range(QT):
                    for f in range(2):
                        src = ps[2 * q + f][:, :].rearrange("p (h d) -> p h d", d=P)
                        h0 = 8 * part + 4 * f
                        k3 = kf[:, q, :].rearrange("p (h d) -> p h d", d=96)
                        v3 = vm[:, q, :].rearrange("p (h d) -> p h d", d=64)
                        E.activation(k3[:, h0:h0 + 4, 0:64], src[:, :, 0:64], ACT.Copy).then_inc(A.sem, A.up())
                        E.activation(v3[:, h0:h0 + 4, :], src[:, :, 64:128], ACT.Copy).then_inc(A.sem, A.up())

        def mla_prepare(h, done, free, start):
            bank = ps[h % 2]

            @block.tensor
            def _(pe):
                pe.wait_ge(V.sem, start[0])
                pe.wait_ge(A.sem, done.get(h - 2, start[1]))
                for i, src in enumerate((qm, kf)):
                    for q in range(QT):
                        last = TE.transpose(bank[0:96, (2 * i + q) * P:(2 * i + q + 1) * P],
                                            src[:, q, h * 96:(h + 1) * 96], ident)
                last.then_inc(T.sem, T.up())

            @block.scalar
            def _(act):
                act.wait_ge(T.sem, T.n)
                act.wait_ge(used, blocks["pe"])
                act.wait_ge(T.sem, free.get(h - 2, 0))
                E.activation(qk[0:96, h % 2, :], bank[0:96, :], ACT.Copy).then_inc(A.sem, A.up())
                done[h] = A.n

        def mla_out(dve, h, acc, sums, rinv):
            VE.reciprocal(rinv, sums).then_inc(V.sem, V.up())
            dve.wait_ge(V.sem, V.n)
            for q in range(QT):
                VE.tensor_scalar(om[:, q, h * 64:(h + 1) * 64], acc[:, q * 64:(q + 1) * 64], rinv[:, q:q + 1], None,
                                   ALU.mult).then_inc(V.sem, V.up())
        causal = cs("causal")
        attention(HEADS, [[0], [0, 1]], 96,
                  lambda h, q, kts: [(qk[0:96, h % 2, q * P:(q + 1) * P], qk[0:96, h % 2, 2 * P:2 * P + P * len(kts)])],
                  lambda h, kt: vm[:, kt, h * 64:(h + 1) * 64], 64, mla_out, 1.0 / math.sqrt(96.0),
                  lambda h: [(0, P, causal[:, P:2 * P]), (P, 3 * P, causal)], mla_prepare)
        turn(lambda q: om[:, q, :], KT)
        rows_product(KT, D)
        add_residual((mod_at(1, 5), 1.0))
        norm_x(lambda k, n: col("norm_g", 40 + k, n), (mod_at(1, 6), mod_at(1, 7)))
        ffn(3, 0, 0, (mod_at(1, 8), 0.5))
        def norm_rows(gain):
            @block.gpsimd
            def _(pool):
                pool.wait_ge(V.sem, V.n)
                pool.dma_start(grow[:, :], a[gain][0:1, :].to_broadcast([P, D])).then_inc(later.sem, later.up(16))

            @block.scalar
            def _(act):
                act.wait_ge(V.sem, V.n)
                for q in range(QT):
                    E.activation(ar(XN, QT, D)[:, q, :], x[:, q, :], ACT.Square, accum_out=st[:, q:q + 1]).then_inc(A.sem, A.up())

            @block.vector
            def _(dve):
                dve.wait_ge(A.sem, A.n)
                VE.tensor_scalar(st[:, 8:10], st[:, 0:2], 1.0 / D, EPS, ALU.mult, ALU.add).then_inc(V.sem, V.up())

            @block.gpsimd
            def _(pool):
                pool.wait_ge(V.sem, V.n)
                GE.tensor_tensor(st[:, 16:18], st[:, 8:10], st[:, 60:62], ALU.pow).then_inc(G.sem, G.up())

            @block.vector
            def _(dve):
                dve.wait_ge(G.sem, G.n)
                dve.wait_ge(later.sem, later.n)
                for q in range(QT):
                    VE.scalar_tensor_tensor(out=x[:, q, :], in0=x[:, q, :], scalar=st[:, 16 + q:17 + q],
                                              in1=grow[:, :], op0=ALU.mult, op1=ALU.mult).then_inc(V.sem, V.up())
        norm_rows("g_first")
        norm_x(lambda k, n: col("mix", k, n))
        qT = ar(0, KT, L)
        kd = [ar(2048, 4, L), ar(3072, 4, L)]
        vd = [ar(4096, QT, L), ar(4608, QT, L)]
        gattn = ar(5120, QT, D)
        cin = ar(7168, KT, 286)
        cv = ar(9456, KT, L)
        gconv = ar(11504, QT, D)
        cmp_in = [ar(13552, 4, L), ar(14576, 4, L)]
        gates = ar(15600, QT, 48)
        kcmp = ar(15700, 64)
        zc = ar(15764, 64)
        coef = ar(15828, QT, 16)
        cm = ar(15860, 16)
        csum = ar(15876, 16)
        ymix, om2 = ar(7168, QT, D), ar(9216, QT, D)
        bias_t = ar(11504, HEADS, L)
        vcmp = grow[:, :].rearrange("p (g n) -> p g n", g=4)

        @block.vector
        def _(dve):
            dve.wait_ge(T.sem, T.n)
            dve.wait_ge(used, blocks["pe"])
            dve.wait_ge(A.sem, A.n)
            dve.wait_ge(V.sem, V.n)
            VE.memset(cin[:, :, 0:30], 0.0).then_inc(V.sem, V.up())
            VE.memset(grow[:, :], 0.0).then_inc(V.sem, V.up())

        small_product(ps[6], 48, "gh_w")

        @block.scalar
        def _(act):
            act.wait_ge(T.sem, T.n)
            act.wait_ge(used, blocks["pe"])
            E.activation(gates[:, :, :].rearrange("p a b -> p (a b)"), ps[6][:, 0:96], ACT.Sigmoid).then_inc(A.sem, A.up())

        def evac_conv(pair, bank):
            s = act_s[:, pair % 2, 0:L]

            @block.scalar
            def _(act):
                act.wait_ge(T.sem, T.n)
                act.wait_ge(used, blocks["pe"])
                act.wait_ge(V.sem, V.n)
                E.activation(s, bank[:, L:2 * L], ACT.Sigmoid).then_inc(A.sem, A.up())

            @block.vector
            def _(dve):
                dve.wait_ge(A.sem, A.n)
                VE.tensor_tensor(cin[:, pair, 30:286], bank[:, 0:L], s, ALU.mult).then_inc(V.sem, V.up())

        def taps(tile, lo, hi):
            @block.vector
            def _(dve):
                for k in range(lo, hi):
                    dve.wait_ge(V.sem, V.n)
                    if k == 0:
                        VE.tensor_scalar(cv[:, tile, :], cin[:, tile, 0:L], col("dw_w", tile), col("dw_b", tile),
                                           ALU.mult, ALU.add).then_inc(V.sem, V.up())
                    else:
                        VE.scalar_tensor_tensor(out=cv[:, tile, :], in0=cin[:, tile, k:k + L],
                                                  scalar=col("dw_w", 8 * k + tile), in1=cv[:, tile, :],
                                                  op0=ALU.mult, op1=ALU.add).then_inc(V.sem, V.up())

        columns_product(16, evac_conv)
        pending = [(tile, lo, min(31, lo + 8)) for tile in range(KT) for lo in range(0, 31, 8)]

        def some_taps(n):
            for _ in range(n):
                if pending:
                    taps(*pending.pop(0))

        def evac_cmp_in(pair, bank):
            b3 = bank[:, :].rearrange("p (a b) -> p a b", b=L)
            dst = cmp_in[pair]

            @block.scalar
            def _(act):
                act.wait_ge(T.sem, T.n)
                act.wait_ge(used, blocks["pe"])
                for half in range(2):
                    src = b3[64 * half:64 * half + 64]
                    E.activation(dst[0:64, half:4:2, :], src, ACT.Copy).then_inc(A.sem, A.up())
                    E.activation(dst[64:128, half:4:2, 0:L - 1], src[:, :, 1:L], ACT.Copy).then_inc(A.sem, A.up())
            some_taps(2)

        def evac_keys(which):
            def evac(pair, bank):
                b3 = bank[:, :].rearrange("p (a b) -> p a b", b=L)

                @block.scalar
                def _(act):
                    act.wait_ge(T.sem, T.n)
                    act.wait_ge(used, blocks["pe"])
                    for half in range(2):
                        for to in range(2):
                            E.activation(kd[which][64 * to:64 * to + 64, half:4:2, :],
                                           b3[64 * half:64 * half + 64], ACT.Copy).then_inc(A.sem, A.up())
                some_taps(2)
            return evac

        def evac_q(dst):
            def evac(pair, bank):
                @block.scalar
                def _(act):
                    act.wait_ge(T.sem, T.n)
                    act.wait_ge(used, blocks["pe"])
                    E.activation(dst[:, 2 * pair:2 * pair + 2, :].rearrange("p a b -> p (a b)"), bank[:, :],
                                   ACT.Copy).then_inc(A.sem, A.up())
                some_taps(3)
            return evac
        columns_product(4, evac_cmp_in)
        columns_product(2, evac_keys(0))
        columns_product(2, evac_keys(1))
        columns_product(8, evac_q(qT))
        for which in range(2):
            rows_product(KT, L)

            @block.scalar
            def _(act):
                act.wait_ge(T.sem, T.n)
                act.wait_ge(used, blocks["pe"])
                for q in range(QT):
                    E.activation(vd[which][:, q, :], ps[2 * q][:, 0:L], ACT.Copy).then_inc(A.sem, A.up())
            some_taps(2)

        def evac_rows(dst, func):
            @block.scalar
            def _(act):
                act.wait_ge(T.sem, T.n)
                act.wait_ge(used, blocks["pe"])
                for q in range(QT):
                    for f in range(2):
                        E.activation(dst[:, q, f * 512:(f + 1) * 512], ps[2 * q + f][:, :], func).then_inc(A.sem, A.up())
        rows_product(KT, D)
        evac_rows(gconv, ACT.Sigmoid)
        some_taps(4)

        for kind in range(2):
            src = cmp_in[kind]

            @block.tensor
            def _(pe):
                pe.wait_ge(A.sem, A.n)
                pe.wait_ge(V.sem, V.n)
                for lp in range(16):
                    w = sm("w1", (kind * 16 + lp) * 64, (kind * 16 + lp + 1) * 64)
                    TE.matmul(ps[6][0:64, 0:60], w, src[:, :, 2 * lp:2 * lp + 16 * (N_CMP - 1) + 1:16],
                              start=lp == 0, stop=lp == 15)
                for lp in range(16):
                    w = sm("w1", (kind * 16 + lp) * 64, (kind * 16 + lp + 1) * 64)
                    last = TE.matmul(ps[7][0:64, 0:1], w, sm("pos", kind * 16 + lp, kind * 16 + lp + 1),
                                     start=lp == 0, stop=lp == 15)
                last.then_inc(T.sem, T.up())

            @block.vector
            def _(dve):
                dve.wait_ge(T.sem, T.n)
                dve.wait_ge(used, blocks["pe"])
                dve.wait_ge(A.sem, A.n)
                VE.tensor_copy(zc[0:64, 60:61], ps[7][0:64, 0:1]).then_inc(V.sem, V.up())

            @block.scalar
            def _(act):
                act.wait_ge(V.sem, V.n)
                E.activation(zc[0:64, 0:60], ps[6][0:64, 0:60], ACT.Silu, bias=zc[0:64, 60:61]).then_inc(A.sem, A.up())

            @block.tensor
            def _(pe):
                pe.wait_ge(A.sem, A.n)
                w = sm("w2", kind * 64, kind * 64 + 64, rows=slice(0, 64))
                if kind == 0:
                    TE.matmul(ps[7][0:64, 0:60], w, zc[0:64, 0:60], start=True, stop=True).then_inc(T.sem, T.up())
                else:
                    for g in range(4):
                        last = TE.matmul(ps[7][0:N_CMP, g * 64:(g + 1) * 64], zc[0:64, g * N_CMP:(g + 1) * N_CMP], w,
                                         start=True, stop=True)
                    last.then_inc(T.sem, T.up())

            @block.vector
            def _(dve):
                dve.wait_ge(T.sem, T.n)
                dve.wait_ge(used, blocks["pe"])
                if kind == 0:
                    for to in range(2):
                        VE.tensor_copy(kcmp[64 * to:64 * to + 64, 0:60], ps[7][0:64, 0:60]).then_inc(V.sem, V.up())
                else:
                    for r in range(4):
                        VE.tensor_copy(vcmp[32 * r:32 * r + N_CMP, :, r * 64:(r + 1) * 64],
                                         ps[7][0:N_CMP, 0:256].rearrange("p (g d) -> p g d", d=64)).then_inc(V.sem, V.up())
        rows_product(KT, D)
        evac_rows(gattn, ACT.Sigmoid)
        some_taps(len(pending))

        def channel_sums(src):
            @block.tensor
            def _(pe):
                pe.wait_ge(V.sem, V.n)
                pe.wait_ge(A.sem, A.n)
                for k in range(KT):
                    last = TE.matmul(ps[6][:, 0:L], cs("ones"), src[:, k, :], start=k == 0, stop=k == KT - 1)
                last.then_inc(T.sem, T.up())
        square = cin[:, :, 0:L]
        mean, rstd = act_s[:, 0, 0:L], act_s[:, 1, 0:L]
        channel_sums(cv)

        @block.vector
        def _(dve):
            dve.wait_ge(T.sem, T.n)
            dve.wait_ge(used, blocks["pe"])
            dve.wait_ge(A.sem, A.n)
            VE.tensor_scalar(mean, ps[6][:, 0:L], 1.0 / D, None, ALU.mult).then_inc(V.sem, V.up())
            dve.wait_ge(V.sem, V.n)
            VE.tensor_tensor(cv, cv, mean.unsqueeze(1).to_broadcast([P, KT, L]), ALU.subtract).then_inc(V.sem, V.up())

        @block.scalar
        def _(act):
            act.wait_ge(V.sem, V.n)
            E.activation(square, cv, ACT.Square).then_inc(A.sem, A.up())
        channel_sums(square)

        @block.vector
        def _(dve):
            dve.wait_ge(T.sem, T.n)
            dve.wait_ge(used, blocks["pe"])
            VE.tensor_scalar(rstd, ps[6][:, 0:L], 1.0 / D, EPS, ALU.mult, ALU.add).then_inc(V.sem, V.up())

        @block.gpsimd
        def _(pool):
            pool.wait_ge(V.sem, V.n)
            GE.tensor_tensor(rstd, rstd, st[:, 60:61].to_broadcast([P, L]), ALU.pow).then_inc(G.sem, G.up())

        @block.vector
        def _(dve):
            dve.wait_ge(G.sem, G.n)
            VE.tensor_tensor(cv, cv, rstd.unsqueeze(1).to_broadcast([P, KT, L]), ALU.mult).then_inc(V.sem, V.up())

        @block.scalar
        def _(act):
            act.wait_ge(V.sem, V.n)
            for k in range(KT):
                E.activation(cv[:, k, :], cv[:, k, :], ACT.Silu, scale=col("ln_g", k), bias=col("ln_b", k)).then_inc(A.sem, A.up())
            act.wait_ge(A.sem, A.n)
        for k in range(0, KT, 2):
            split_T(cv[:, k:k + 2, :].rearrange("p a b -> p (a b)"), k, 2)
        rows_product(KT, D)

        @block.vector
        def _(dve):
            dve.wait_ge(T.sem, T.n)
            dve.wait_ge(used, blocks["pe"])
            dve.wait_ge(A.sem, A.n)
            for q in range(QT):
                for f in range(2):
                    fs = slice(f * 512, (f + 1) * 512)
                    VE.tensor_tensor(ymix[:, q, fs], ps[2 * q + f][:, :], gconv[:, q, fs], ALU.mult).then_inc(V.sem, V.up())

        @block.gpsimd
        def _(pool):
            pool.wait_ge(V.sem, V.n)
            pool.wait_ge(T.sem, T.n)
            pool.wait_ge(used, blocks["pe"])
            pool.wait_ge(scratch.sem, scratch.n)
            skew = bass.AP(tensor=u_dram.tensor, offset=P - 1, ap=[[383, P], [P * 384, HEADS], [1, L]])
            pool.dma_start(bias_t, skew).then_inc(biasld.sem, biasld.up(16))

        scale64 = 1.0 / math.sqrt(64.0)
        for q in range(QT):
            pt = act_s[:, q, :].rearrange("p (h n) -> p h n", n=32)
            pn = pt[:, :, 0:N_CMP]

            @block.tensor
            def _(pe):
                pe.wait_ge(V.sem, V.n)
                pe.wait_ge(A.sem, A.n)
                for h in range(HEADS):
                    b = 64 * (h % 2)
                    c = (h // 2) * 32
                    last = TE.matmul(ps[4 + h % 2][:, c:c + N_CMP], qT[b:b + 64, h // 2, q * P:(q + 1) * P],
                                     kcmp[b:b + 64, (h // 4) * N_CMP:(h // 4 + 1) * N_CMP], start=True, stop=True)
                last.then_inc(T.sem, T.up())

            def over_heads(v):
                return v.unsqueeze(1).to_broadcast([P, HEADS, N_CMP])

            def over_keys(v):
                return v.unsqueeze(2).to_broadcast([P, HEADS, N_CMP])

            @block.vector
            def _(dve):
                VE.memset(act_s[:, q, :], 0.0).then_inc(V.sem, V.up())
                dve.wait_ge(T.sem, T.n)
                dve.wait_ge(used, blocks["pe"])
                dve.wait_ge(V.sem, V.n)
                for odd in range(2):
                    VE.scalar_tensor_tensor(
                        out=pn[:, odd:HEADS:2, :],
                        in0=ps[4 + odd][:, 0:256].rearrange("p (h n) -> p h n", n=32)[:, :, 0:N_CMP], scalar=scale64,
                        in1=biasc[:, q, 0:N_CMP, odd:HEADS:2].rearrange("p n h -> p h n"), op0=ALU.mult, op1=ALU.add).then_inc(V.sem, V.up())
                dve.wait_ge(V.sem, V.n)
                VE.tensor_tensor(pn, pn, over_heads(cs("cmpneg", q * 16, q * 16 + N_CMP)), ALU.add).then_inc(V.sem, V.up())
                dve.wait_ge(V.sem, V.n)
                VE.tensor_reduce(cm, pn, AX, ALU.max).then_inc(V.sem, V.up())
                dve.wait_ge(V.sem, V.n)
                VE.tensor_tensor(pn, pn, over_keys(cm), ALU.subtract).then_inc(V.sem, V.up())

            @block.scalar
            def _(act):
                act.wait_ge(V.sem, V.n)
                E.activation(pn, pn, ACT.Exp).then_inc(A.sem, A.up())

            @block.vector
            def _(dve):
                dve.wait_ge(A.sem, A.n)
                VE.tensor_tensor(pn, pn, over_heads(cs("cmp01", q * 16, q * 16 + N_CMP)), ALU.mult).then_inc(V.sem, V.up())
                dve.wait_ge(V.sem, V.n)
                VE.tensor_reduce(csum, pn, AX, ALU.add).then_inc(V.sem, V.up())
                dve.wait_ge(V.sem, V.n)
                VE.tensor_scalar(csum, csum, 1e-30, None, ALU.max).then_inc(V.sem, V.up())
                dve.wait_ge(V.sem, V.n)
                VE.reciprocal(csum, csum).then_inc(V.sem, V.up())
                dve.wait_ge(V.sem, V.n)
                VE.tensor_tensor(coef[:, q, :], csum, gates[:, q, 0:16], ALU.mult).then_inc(V.sem, V.up())

            @block.tensor
            def _(pe):
                pe.wait_ge(V.sem, V.n)
                for g in range(4):
                    last = TE.transpose(ps[6][:, g * P:(g + 1) * P], act_s[:, q, g * P:(g + 1) * P], ident)
                last.then_inc(T.sem, T.up())

            @block.scalar
            def _(act):
                act.wait_ge(T.sem, T.n)
                act.wait_ge(used, blocks["pe"])
                E.activation(tmp[:, q, :], ps[6][:, :], ACT.Copy).then_inc(A.sem, A.up())

            @block.tensor
            def _(pe):
                pe.wait_ge(A.sem, A.n)
                for g in range(4):
                    last = TE.matmul(ps[2 * q + g // 2][:, (g % 2) * L:(g % 2 + 1) * L], tmp[:, q, g * P:(g + 1) * P],
                                     vcmp[:, g, :], start=True, stop=True)
                last.then_inc(T.sem, T.up())

            @block.vector
            def _(dve):
                dve.wait_ge(T.sem, T.n)
                dve.wait_ge(used, blocks["pe"])
                for f in range(2):
                    VE.tensor_tensor(om2[:, q, f * 512:(f + 1) * 512].rearrange("p (h d) -> p h d", d=64),
                                       ps[2 * q + f][:, :].rearrange("p (h d) -> p h d", d=64),
                                       coef[:, q, 8 * f:8 * f + 8].unsqueeze(2).to_broadcast([P, 8, 64]), ALU.mult).then_inc(V.sem, V.up())

        def nsa_scores(n, q, kts):
            h = n % HEADS
            b = 64 * (h % 2)
            return [(qT[b:b + 64, h // 2, q * P:(q + 1) * P], kd[n // HEADS][b:b + 64, h // 4, 0:P * len(kts)])]

        def nsa_out(dve, n, acc, sums, rinv):
            h, which = n % HEADS, n // HEADS
            VE.reciprocal(rinv, sums).then_inc(V.sem, V.up())
            dve.wait_ge(V.sem, V.n)
            c = (1 + which) * 16 + h
            VE.tensor_tensor(rinv, rinv, gates[:, :, c:c + 1].rearrange("p q a -> p (q a)"), ALU.mult).then_inc(V.sem, V.up())
            dve.wait_ge(V.sem, V.n)
            for q in range(QT):
                o = om2[:, q, h * 64:(h + 1) * 64]
                VE.scalar_tensor_tensor(out=o, in0=acc[:, q * 64:(q + 1) * 64], scalar=rinv[:, q:q + 1], in1=o,
                                          op0=ALU.mult, op1=ALU.add).then_inc(V.sem, V.up())

        @block.vector
        def _(dve):
            dve.wait_ge(biasld.sem, biasld.n)

        attention(2 * HEADS, [[0], [0, 1]], 64, nsa_scores,
                  lambda n, kt: vd[n // HEADS][:, kt, ((n % HEADS) // 4) * 64:((n % HEADS) // 4 + 1) * 64], 64, nsa_out,
                  scale64, lambda n: [(0, P, bias_t[:, n % HEADS, P:2 * P]), (P, 3 * P, bias_t[:, n % HEADS, :])])

        @block.vector
        def _(dve):
            dve.wait_ge(V.sem, V.n)
            for q in range(QT):
                VE.tensor_tensor(om2[:, q, :], om2[:, q, :], gattn[:, q, :], ALU.mult).then_inc(V.sem, V.up())
            dve.wait_ge(V.sem, V.n)
            for q in range(QT):
                VE.tensor_tensor(ymix[:, q, :], ymix[:, q, :], om2[:, q, :], ALU.add).then_inc(V.sem, V.up())
        turn(lambda q: ymix[:, q, :], KT)
        rows_product(KT, D)
        add_residual(None)
        memt = ar(0, QT, D)
        kx, vx, qx, ox = ar(2048, KT, L), ar(4096, QT, D), ar(6144, KT, L), ar(8192, QT, D)

        @block.gpsimd
        def _(pool):
            pool.wait_ge(V.sem, V.n)
            pool.wait_ge(T.sem, T.n)
            pool.wait_ge(used, blocks["pe"])
            pool.wait_ge(A.sem, A.n)
            pool.dma_start(memt, a["mem"].rearrange("(q p) d -> p q d", p=P)).then_inc(later.sem, later.up(16))

        @block.tensor
        def _(pe):
            pe.wait_ge(later.sem, later.n)
        turn(lambda q: memt[:, q, :], KT)
        columns_product(8, evac_q(kx))
        rows_product(KT, D)
        evac_rows(vx, ACT.Copy)
        norm_x(lambda k, n: col("nx", k, n))
        columns_product(8, evac_q(qx))

        def cross_out(dve, h, acc, sums, rinv):
            VE.reciprocal(rinv, sums).then_inc(V.sem, V.up())
            dve.wait_ge(V.sem, V.n)
            for q in range(QT):
                VE.tensor_scalar(ox[:, q, h * L:(h + 1) * L], acc[:, q * L:(q + 1) * L], rinv[:, q:q + 1], None,
                                   ALU.mult).then_inc(V.sem, V.up())
        attention(4, [[0, 1], [0, 1]], 256,
                  lambda h, q, kts: [(qx[:, 2 * h + j, q * P:(q + 1) * P], kx[:, 2 * h + j, :]) for j in range(2)],
                  lambda h, kt: vx[:, kt, h * L:(h + 1) * L], 256, cross_out, 1.0 / 16.0, None)
        turn(lambda q: ox[:, q, :], KT)
        rows_product(KT, D)
        add_residual(None)
        norm_x(lambda k, n: col("nffn", k, n))
        ffn(4, 0, 0, None)
        norm_rows("g_last")

        @block.sync
        def _(sp):
            sp.wait_ge(V.sem, V.n)
            sp.dma_start(a["out"].rearrange("(q p) d -> p q d", p=P), x[:, :, :]).then_inc(stored.sem, stored.up(16))
            sp.wait_ge(stored.sem, stored.n)


_NAMES = ("x c positions mod_w mod_b norm_g ffn_w13 ffn_w2 ab_w_in pool_w pool_scale ssd_conv_w ssd_conv_b "
          "ssd_dt_bias ssd_a_log ssd_d ssd_norm_g ab_w_out mla_w_in mla_q_norm_g mla_w_uq mla_kv_norm_g mla_w_ukv "
          "mla_w_o final_norm_g mem_2 norm_mix_g_2 w_in_2 conv_dw_w_2 conv_dw_b_2 conv_ln_g_2 conv_ln_b_2 "
          "conv_pw_w_2 cmp_pos_2 cmp_w1_2 cmp_w2_2 w_out_2 norm_x_g_2 xq_w_2 xkv_w_2 xo_w_2 norm_ffn_g_2 "
          "ffn_in_w_2 ffn_out_w_2 rel_bias_2 final_norm_g_2").split()


def by_columns(w):
    n = w.shape[1] // P
    return w.reshape(KT, P, n, P).transpose(2, 1, 0, 3).reshape(n, P, BLK)


def by_rows(w):
    k, n = w.shape
    per = BLK // n
    v = w.reshape(k // P, P, n)
    return v.reshape(k // P // per, per, P, n).transpose(0, 2, 1, 3).reshape(-1, P, BLK)


def ffn_blocks(w13, w2):
    a_, b_ = by_columns(w13[:, :FF]), by_columns(w13[:, FF:])
    r = w2.reshape(FT, P, D)
    six = [a_[0::2], b_[0::2], a_[1::2], b_[1::2], r[0::2], r[1::2]]
    return np.stack(six, axis=1).reshape(-1, P, BLK)


def pack_stream(i):
    ab, mi, w = i["ab_w_in"][0], i["mla_w_in"][0], i["w_in_2"][0]
    uq, ukv, xkv = i["mla_w_uq"][0], i["mla_w_ukv"][0], i["xkv_w_2"][0]
    parts = [
        ffn_blocks(i["ffn_w13"][0, 0], i["ffn_w2"][0, 0]),
        by_columns(ab[:, 1536:3072]), by_columns(ab[:, 0:512]), by_rows(ab[:, 512:1536]), by_rows(np.roll(i["ab_w_out"][0], -512, axis=0)),
        ffn_blocks(i["ffn_w13"][0, 1], i["ffn_w2"][0, 1]),
        ffn_blocks(i["ffn_w13"][1, 0], i["ffn_w2"][1, 0]),
        by_rows(mi[:, 0:1024]), by_rows(uq[:, 0:1024]), by_rows(uq[:, 1024:1536]),
        by_rows(ukv[:, 0:1024]), by_rows(ukv[:, 1024:2048]), by_rows(i["mla_w_o"][0]),
        ffn_blocks(i["ffn_w13"][1, 1], i["ffn_w2"][1, 1]),
        by_columns(np.concatenate([w[:, :2048].reshape(D, 2, KT, P)[:, 0], w[:, :2048].reshape(D, 2, KT, P)[:, 1]],
                                  axis=2).reshape(D, 2048)),
        by_columns(w[:, 3072:3584]), by_columns(w[:, 3584:3840]), by_columns(w[:, 4096:4352]),
        by_columns(w[:, 2048:3072]),
        by_rows(w[:, 3840:4096]), by_rows(w[:, 4352:4608]), by_rows(w[:, 4656:5680]), by_rows(w[:, 5680:6704]),
        by_rows(i["conv_pw_w_2"][0]), by_rows(i["w_out_2"][0]),
        by_columns(xkv[:, 0:1024]), by_rows(xkv[:, 1024:2048]), by_columns(i["xq_w_2"][0]), by_rows(i["xo_w_2"][0]),
        ffn_blocks(i["ffn_in_w_2"][0], i["ffn_out_w_2"][0]),
    ]
    out = np.concatenate(parts, axis=0)
    assert out.shape[0] == N_BLOCKS, (out.shape, N_BLOCKS)
    return out


def pack_cols(i):
    c = {
        "c": i["c"].reshape(8, P), "mod_b": i["mod_b"].reshape(144, P), "norm_g": i["norm_g"].reshape(48, P),
        "pool_scale": i["pool_scale"].reshape(4, P), "conv_w": i["ssd_conv_w"].reshape(48, P),
        "conv_b": i["ssd_conv_b"].reshape(12, P), "q_norm": i["mla_q_norm_g"].reshape(6, P),
        "kv_norm": i["mla_kv_norm_g"].reshape(2, P), "ssd_norm": i["ssd_norm_g"].reshape(8, P),
        "mix": i["norm_mix_g_2"].reshape(8, P), "dw_w": i["conv_dw_w_2"].reshape(248, P),
        "dw_b": i["conv_dw_b_2"].reshape(8, P), "ln_g": i["conv_ln_g_2"].reshape(8, P),
        "ln_b": i["conv_ln_b_2"].reshape(8, P), "nx": i["norm_x_g_2"].reshape(8, P),
        "nffn": i["norm_ffn_g_2"].reshape(8, P),
    }
    return np.ascontiguousarray(np.concatenate([c[n] for n, _ in COLS], axis=0).T)


def tiles_on_partitions(w):
    return w.reshape(-1, P, w.shape[1]).transpose(1, 0, 2).reshape(P, -1)


def pack_small(i):
    f = np.float32
    w1 = i["cmp_w1_2"][0].reshape(2, 16, 2, 64, 64).transpose(2, 3, 0, 1, 4).reshape(P, 2048)
    w2 = np.concatenate([i["cmp_w2_2"][0].transpose(1, 0, 2).reshape(64, 128), np.zeros((64, 128), f)], axis=0)
    pos = i["cmp_pos_2"][0].reshape(2, 16, 2, 64).transpose(2, 3, 0, 1).reshape(P, 32)
    relb = np.concatenate([i["rel_bias_2"], np.zeros((96, 16), f)], axis=0)
    ab, mi, w = i["ab_w_in"][0], i["mla_w_in"][0], i["w_in_2"][0]
    return np.ascontiguousarray(np.concatenate([
        tiles_on_partitions(ab[:, 3072:3088]), tiles_on_partitions(mi[:, 1024:1056]),
        tiles_on_partitions(w[:, 4608:4656]), i["pool_w"][0].transpose(1, 0, 2).reshape(P, 512), w1, w2, pos, relb],
        axis=1))


def constants():
    f = np.float32
    p, j = np.arange(P)[:, None], np.arange(P)[None, :]
    j2 = np.arange(256)[None, :]
    q = np.arange(L).reshape(QT, P).T[:, :, None]
    seen = np.zeros((P, QT, 16), bool)
    seen[:, :, :N_CMP] = q >= 16 * np.arange(N_CMP)[None, None, :] + 31
    sel = (np.arange(P) % 32 == 0)[:, None]
    invf = np.float32(10000.0) ** (-np.arange(0, 32, 2, dtype=f) / f(32))
    recip = np.stack([f(1) / np.minimum(np.arange(16, dtype=f) + 1, f(win)) for win in (2, 4, 8, 16)])
    c = {
        "ident": p == j, "upper": p <= j, "ssd_mask": np.where(p <= j, 0, NEG),
        "causal": np.where(j2 - P <= p, 0, NEG), "ones": np.ones((P, P)), "sel": sel,
        "invf": np.broadcast_to(invf, (P, 16)), "recip": np.broadcast_to(recip.reshape(1, 64), (P, 64)),
        "cmp01": seen.reshape(P, 32), "cmpneg": np.where(seen, 0, NEG).reshape(P, 32),
    }
    return np.ascontiguousarray(np.concatenate([np.asarray(c[n], f) for n, _ in CONST], axis=1))


def onehots():
    n = np.arange(-256, 256)
    nn = np.maximum(n, 1).astype(np.float32)
    large = 16 + (np.log(nn / np.float32(16)) / np.float32(math.log(8)) * np.float32(16)).astype(np.int32)
    bucket = np.where(n < 16, np.maximum(n, 0), np.minimum(large, 31))
    by_distance = (np.arange(33)[:, None] == bucket[None, :]).astype(np.float32)
    back = 255 - np.arange(512)
    out = np.zeros((33, 1024), np.float32)
    out[:, 0:512] = np.where(back[None, :] >= 0, by_distance[:, np.clip(back + 256, 0, 511)], 0)
    out[32, 0:512] = back < 0
    out[:, 512:1024] = by_distance
    return out


def kernel(**inputs):
    import concourse.bacc as _bacc
    from concourse.bass_utils import run_bass_kernel_spmd as _run

    i = {n: np.asarray(inputs[n]) for n in _NAMES}
    mod = i["mod_w"].reshape(2, 2, 4, P, 18, MODC).transpose(0, 4, 1, 3, 2, 5).reshape(N_MOD, 2, P, 4 * MODC)
    arrays = {
        "stream": pack_stream(i), "mod_w": np.ascontiguousarray(mod), "cols": pack_cols(i), "small": pack_small(i),
        "const": constants(), "onehot": onehots(), "x": i["x"].reshape(L, D), "mem": i["mem_2"].reshape(L, D),
        "rows": np.concatenate([i["ssd_dt_bias"][0], i["ssd_a_log"][0], i["ssd_d"][0]]).reshape(1, 48),
        "positions": np.ascontiguousarray(i["positions"].reshape(QT, P).T),
        "g_first": i["final_norm_g"].reshape(1, D), "g_last": i["final_norm_g_2"].reshape(1, D),
    }
    arrays = {f"in_{n}": v for n, v in arrays.items()}
    nc = _bacc.Bacc("TRN2", target_bir_lowering=False, num_devices=1)
    aps = {n[3:]: nc.dram_tensor(n, v.shape, mybir.dt.from_np(v.dtype), kind="ExternalInput").ap()
           for n, v in arrays.items()}
    aps["out"] = nc.dram_tensor("out_0", (L, D), F32, kind="ExternalOutput").ap()
    build(nc, aps)
    r = _run(nc, [arrays], core_ids=[0])
    return np.asarray(r.results[0]["out_0"]).reshape(1, L, D)
```

```python
from contextlib import ExitStack
import math

import numpy as np

import concourse.bass as bass
from concourse import mybir

F32 = mybir.dt.float32
F32R = mybir.dt.float32r
I32 = mybir.dt.int32
ALU = mybir.AluOpType
ACT = mybir.ActivationFunctionType
AX = mybir.AxisListType.X

P = 128
D = 1024
L = 256
QT = L // P
KT = D // P
FF = 2816
FT = FF // P
FG = FT // 2
EPS = 1e-6
NEG = -1e30
BLK = 1024
RING = 6
MODC = 512
N_MOD = 2 * 9 * D // MODC
HEADS = 16
N_CMP = (L - 32) // 16 + 1


COLS = [("c", 8), ("mod_b", 144), ("norm_g", 48), ("pool_scale", 4), ("conv_w", 48), ("conv_b", 12),
        ("q_norm", 6), ("kv_norm", 2), ("ssd_norm", 8), ("mix", 8), ("dw_w", 248), ("dw_b", 8),
        ("ln_g", 8), ("ln_b", 8), ("nx", 8), ("nffn", 8)]
SMALL = [("pool_w", 512), ("w1", 2048), ("w2", 128),
         ("pos", 32), ("relb", 16)]
CONST = [("ident", 128), ("upper", 128), ("ssd_mask", 128), ("causal", 256), ("ones", 128), ("sel", 1),
         ("invf", 16), ("recip", 64), ("cmp01", 32), ("cmpneg", 32)]


def offsets(table):
    at, out = 0, {}
    for name, width in table:
        out[name] = (at, at + width)
        at += width
    return out, at


COL, NCOL = offsets(COLS)
SML, NSML = offsets(SMALL)
CST, NCST = offsets(CONST)


N_BLOCKS = 5 * FG * 6 + (1 + 16 + 8) + 12 + (1 + 8 + 6 + 3 + 4 + 8) + (1 + 16 + 8 + 2 + 2 + 2 + 2 + 2 + 2 + 8 + 8 + 8 + 8) \
    + (8 + 8 + 8 + 8)


def build(nc, a):
    n_stream = N_BLOCKS
    ctx = ExitStack()
    with ctx:
        def sb(name, shape, dt=F32):
            return ctx.enter_context(nc.sbuf_tensor(name, shape, dt))

        def sem(name):
            return ctx.enter_context(nc.semaphore(name))

        class Count:

            def __init__(self, name):
                self.sem, self.n = sem(name), 0

            def up(self, by=1):
                self.n += by
                return by

        raw = sb("raw", [P, RING, BLK])
        w_hi = sb("w_hi", [P, RING, BLK], F32R)
        w_lo = sb("w_lo", [P, RING, BLK], F32R)
        x = sb("resid", [P, QT, D])
        t_hi = sb("t_hi", [P, 12, L], F32R)
        t_lo = sb("t_lo", [P, 12, L], F32R)
        tmp = sb("tmp", [P, 2, 512])
        act_s = sb("act_s", [P, 2, 512])
        g_hi = sb("g_hi", [P, 2, L], F32R)
        g_lo = sb("g_lo", [P, 2, L], F32R)
        cols = sb("cols", [P, NCOL])
        small = sb("small", [P, NSML])
        cst = sb("cst", [P, NCST])
        modc = sb("modc", [P, 144])
        sg = sb("sg", [P, 8])
        grow = sb("grow", [P, D])
        cb = sb("cb", [P, KT, 32])
        biasc = sb("biasc", [P, QT, 16, HEADS])
        st = sb("st", [P, 64])
        rowv = sb("rowv", [P, 48])
        posi = sb("posi", [P, QT], I32)
        AW = 16448
        arena = sb("arena", [P, AW])
        ps = [ctx.enter_context(nc.psum_tensor(f"ps{i}", [P, 512], F32)) for i in range(8)]
        u_dram = nc.dram_tensor("u_scratch", [HEADS, P, 384], F32, kind="Internal").ap()

        def col(name, i=0, n=1):
            return cols[:, COL[name][0] + i:COL[name][0] + i + n]

        def cs(name, lo=0, hi=None, rows=P):
            s, e = CST[name]
            return cst[0:rows, s + lo:(e if hi is None else s + hi)]

        def sm(name, lo=0, hi=None, rows=slice(0, P)):
            s, e = SML[name]
            return small[rows, s + lo:(e if hi is None else s + hi)]

        def ar(at, *shape, parts=slice(0, P)):
            n = int(np.prod(shape))
            assert at + n <= AW, (at, shape)
            v = arena[parts, at:at + n]
            if len(shape) == 2:
                return v.rearrange("p (a b) -> p a b", b=shape[1])
            if len(shape) == 3:
                return v.rearrange("p (a b c) -> p a b c", b=shape[1], c=shape[2])
            return v

        ident = cs("ident")

        V, A, T, G = Count("vector_steps"), Count("scalar_steps"), Count("tensor_steps"), Count("pool_steps")
        landed = [sem(f"block_landed{i}") for i in range(RING)]
        hi_done, lo_done, used = sem("block_hi_done"), sem("block_lo_done"), sem("block_used")
        mod_landed = [sem("mod_landed0"), sem("mod_landed1")]
        mod_used = sem("mod_half_used")
        gated, gate_hi, gate_lo = sem("hidden_gated"), sem("hidden_hi_done"), sem("hidden_lo_done")
        silu_done = sem("silu_done")
        diag_made, row_summed, row_kept = sem("gate_diagonal_made"), sem("gate_row_summed"), sem("gate_row_kept")
        mod_kept, mod_cols, mod_added = sem("mod_kept"), sem("mod_columns"), sem("mod_added")
        inputs, later, scratch, stored = Count("inputs_landed"), Count("rows_landed"), Count("scratch_stored"), Count("output_stored")
        biasld, first_in = Count("bias_landed"), Count("columns_and_constants_landed")

        block = ctx.enter_context(nc.Block())
        E, VE, TE, GE = nc.scalar, nc.vector, nc.tensor, nc.gpsimd

        blocks = {"pe": 0, "hi": 0, "lo": 0}

        def split_hi(act, h):
            s = h % RING
            act.wait_ge(landed[s], 16 * (h // RING + 1))
            if h >= RING:
                act.wait_ge(used, h - (RING - 1))
            E.activation(w_hi[:, s, :], raw[:, s, :], ACT.Copy).then_inc(hi_done, 1)

        def split_lo(dve, h):
            s = h % RING
            dve.wait_ge(hi_done, h + 1)
            VE.tensor_tensor(w_lo[:, s, :], raw[:, s, :], w_hi[:, s, :].bitcast(F32),
                             ALU.subtract).then_inc(lo_done, 1)

        meanwhile = []

        def next_split():
            h = blocks["hi"]
            if h >= n_stream:
                return
            blocks["hi"] += 1

            @block.scalar
            def _(act):
                split_hi(act, h)

            @block.vector
            def _(dve):
                split_lo(dve, h)
            for work in meanwhile:
                work()

        owed = [0]

        def pay_splits():
            while owed[0]:
                owed[0] -= 1
                next_split()

        @block.sync
        def _(sp):
            for s in range(RING):
                sp.dma_start(raw[:, s, :], a["stream"][s, :, :]).then_inc(landed[s], 16)
            with sp.Fori(1, n_stream // RING) as i:
                for s in range(RING):
                    sp.wait_ge(lo_done, i * RING + (s - RING + 1))
                    sp.dma_start(raw[:, s, :], a["stream"][bass.ds(i * RING + s, 1), :, :]
                                 .rearrange("a p n -> p (a n)")).then_inc(landed[s], 16)
            for h in range(n_stream // RING * RING, n_stream):
                sp.wait_ge(lo_done, h - RING + 1)
                sp.dma_start(raw[:, h % RING, :], a["stream"][h, :, :]).then_inc(landed[h % RING], 16)

        oh = ar(0, 512, parts=slice(0, 33))
        ohd = ar(512, 512, parts=slice(0, 32))
        relx = ar(1024, 16, parts=slice(0, 33))

        @block.gpsimd
        def _(pool):
            for dst, src in ((cols[:, :], a["cols"]), (cst[:, :], a["const"])):
                pool.dma_start(dst, src).then_inc(first_in.sem, first_in.up(16))
            for dst, src in ((x[:, :, :], a["x"].rearrange("(q p) d -> p q d", p=P)),
                             (small[:, :], a["small"]), (rowv[:, :], a["rows"][0:1, :].to_broadcast([P, 48])),
                             (posi[:, :], a["positions"]), (oh, a["onehot"][:, 0:512]), (ohd, a["onehot"][0:32, 512:1024]),
                             (relx[0:32, :], a["small"][0:32, SML["relb"][0]:SML["relb"][1]])):
                pool.dma_start(dst, src).then_inc(inputs.sem, inputs.up(16))
            GE.memset(relx[32:33, :], NEG).then_inc(G.sem, G.up())
            pool.wait_ge(G.sem, G.n)
            GE.memset(st[:, 60:62], -0.5).then_inc(G.sem, G.up())

        mraw = ar(2048, 2, 4, MODC)
        modp = ar(6144, MODC)

        def mod_load(act, half, c, first=False):
            if not first:
                act.wait_ge(mod_used, c * 2 + (half - 1))
            act.dma_start(mraw[:, half, :, :], (a["mod_w"][c, half, :, :] if isinstance(c, int) else
                          a["mod_w"][bass.ds(c, 1), half, :, :].rearrange("a p n -> p (a n)"))
                          .rearrange("p (t n) -> p t n", t=4)).then_inc(mod_landed[half], 16)

        def mod_products(pe, c, first=False):
            for half in range(2):
                pe.wait_ge(mod_landed[half], c * 16 + 16)
                if half == 0 and not first:
                    pe.wait_ge(mod_kept, c)
                for t in range(4):
                    last = TE.matmul(ps[6][32 * t:32 * t + 32, :], cb[:, half * 4 + t, :], mraw[:, half, t, :],
                                     start=(half == 0), stop=(half == 1), tile_position=(0, 32 * t))
                last.then_inc(mod_used, 1)

        def mod_keep(dve, c, first=False):
            dve.wait_ge(mod_used, c * 2 + 2)
            if not first:
                dve.wait_ge(mod_cols, c)
            VE.tensor_copy(modp, ps[6][:, :]).then_inc(mod_kept, 1)

        def mod_turn(pe, c, first=False):
            pe.wait_ge(mod_kept, c + 1)
            if not first:
                pe.wait_ge(mod_added, c)
            for j in range(4):
                last = TE.matmul(ps[7][:, j:j + 1], modp[:, j * P:(j + 1) * P], cs("sel"), start=True, stop=True)
            last.then_inc(mod_cols, 1)

        def mod_add(dve, c):
            dve.wait_ge(mod_cols, c + 1)
            sl = slice(c * 4, c * 4 + 4) if isinstance(c, int) else bass.ds(c * 4, 4)
            bl = slice(COL["mod_b"][0] + c * 4, COL["mod_b"][0] + c * 4 + 4) if isinstance(c, int) \
                else bass.ds(c * 4 + COL["mod_b"][0], 4)
            VE.tensor_tensor(modc[:, sl], ps[7][:, 0:4], cols[:, bl], ALU.add).then_inc(mod_added, 1)

        @block.scalar
        def _(act):
            for half in range(2):
                mod_load(act, half, 0, first=True)
            act.wait_ge(first_in.sem, first_in.n)
            E.activation(st[:, 0:8], col("c", 0, 8), ACT.Silu).then_inc(A.sem, A.up())

        @block.vector
        def _(dve):
            dve.wait_ge(A.sem, A.n)
            VE.tensor_copy(cb[:, :, :], st[:, 0:8].unsqueeze(2).to_broadcast([P, KT, 32])).then_inc(V.sem, V.up())

        def bias_tables():
            @block.tensor
            def _(pe):
                pe.wait_ge(V.sem, V.n)
                pe.wait_ge(G.sem, G.n)
                pe.wait_ge(inputs.sem, inputs.n)
                TE.matmul(ps[0][0:16, :], relx, oh, start=True, stop=True).then_inc(T.sem, T.up())
                for q in range(QT):
                    for n in range(N_CMP):
                        d0 = 256 + q * P - (16 * n + 31)
                        last = TE.matmul(ps[1][:, (q * 16 + n) * 16:(q * 16 + n + 1) * 16], ohd[:, d0:d0 + P],
                                         sm("relb", rows=slice(0, 32)), start=True, stop=True)
                last.then_inc(T.sem, T.up())

            @block.vector
            def _(dve):
                dve.wait_ge(T.sem, T.n)
                dve.wait_ge(used, blocks["pe"])
                VE.tensor_copy(ar(1100, 512, parts=slice(0, 16)), ps[0][0:16, :]).then_inc(V.sem, V.up())
                for q in range(QT):
                    VE.tensor_copy(biasc[:, q, 0:N_CMP, :],
                                     ps[1][:, q * 256:q * 256 + N_CMP * 16].rearrange("p (n h) -> p n h", h=16)).then_inc(V.sem, V.up())

            @block.scalar
            def _(act):
                act.wait_ge(V.sem, V.n)
                act.dma_start(u_dram, ar(1100, 384, parts=slice(0, 16)).unsqueeze(1)
                                      .to_broadcast([HEADS, P, 384])).then_inc(scratch.sem, scratch.up(16))

        PRE = 5
        for c in range(PRE):
            if c == 2:
                for _i in range(RING):
                    next_split()
                bias_tables()

            @block.tensor
            def _(pe):
                if c == 0:
                    pe.wait_ge(V.sem, V.n)
                    pe.wait_ge(first_in.sem, first_in.n)
                mod_products(pe, c, first=c == 0)

            @block.scalar
            def _(act):
                for half in range(2):
                    mod_load(act, half, c + 1)

            @block.vector
            def _(dve):
                if c == 0:
                    dve.wait_ge(first_in.sem, first_in.n)
                mod_keep(dve, c, first=c == 0)

            @block.tensor
            def _(pe):
                mod_turn(pe, c, first=c == 0)

            @block.vector
            def _(dve):
                mod_add(dve, c)

        x_ready = {}
        kt_ready = {}
        turned = {"at": (0, 0)}

        def turn(src, n_kt, segs=None, scale=None, shift=None, kt0=0, dst=None, ready=None):
            halves = (slice(0, 512), slice(512, 1024))
            src_ready = ready or {(q, f): V.n for q in range(QT) for f in range(2)}
            pooled = {}
            if segs and segs[0] == (0, D):
                for q in range(QT):
                    @block.scalar
                    def _(act):
                        act.wait_ge(A.sem, A.n)
                        act.wait_ge(T.sem, T.n)
                        act.wait_ge(used, blocks["pe"])
                        for f, fs in enumerate(halves):
                            act.wait_ge(V.sem, src_ready[q, f])
                            E.activation(dst(q)[:, fs], src(q)[:, fs], ACT.Square, scale=1.0 / 32,
                                           accum_out=st[:, 2 * q + f:2 * q + f + 1]).then_inc(A.sem, A.up())

                    @block.gpsimd
                    def _(pool):
                        pool.wait_ge(A.sem, A.n)
                        GE.tensor_scalar(st[:, 8 + q:9 + q], st[:, 2 * q:2 * q + 1], st[:, 2 * q + 1:2 * q + 2], EPS,
                                           ALU.add, ALU.add).then_inc(G.sem, G.up())
                        pool.wait_ge(G.sem, G.n)
                        GE.tensor_tensor(st[:, 16 + q:17 + q], st[:, 8 + q:9 + q], st[:, 60:61], ALU.pow).then_inc(G.sem, G.up())
                    pooled[q] = G.n

                @block.vector
                def _(dve):
                    for q in range(QT):
                        dve.wait_ge(G.sem, pooled[q])
                        for f, fs in enumerate(halves):
                            VE.tensor_scalar(dst(q)[:, fs], src(q)[:, fs], st[:, 16 + q:17 + q], None, ALU.mult).then_inc(V.sem, V.up())
                            src_ready[q, f] = V.n
                src = dst
            elif segs:
                n = len(segs)

                @block.scalar
                def _(act):
                    act.wait_ge(V.sem, V.n)
                    act.wait_ge(A.sem, A.n)
                    for q in range(QT):
                        for s, (b, e) in enumerate(segs):
                            E.activation(dst(q)[:, b:e], src(q)[:, b:e], ACT.Square,
                                           accum_out=st[:, q * n + s:q * n + s + 1]).then_inc(A.sem, A.up())

                @block.vector
                def _(dve):
                    dve.wait_ge(A.sem, A.n)
                    for q in range(QT):
                        for s, (b, e) in enumerate(segs):
                            i = q * n + s
                            VE.tensor_scalar(st[:, 8 + i:9 + i], st[:, i:i + 1], 1.0 / (e - b), EPS,
                                               ALU.mult, ALU.add).then_inc(V.sem, V.up())

                @block.gpsimd
                def _(pool):
                    pool.wait_ge(V.sem, V.n)
                    GE.tensor_tensor(st[:, 16:16 + 2 * n], st[:, 8:8 + 2 * n],
                                       st[:, 60:61].to_broadcast([P, 2 * n]), ALU.pow).then_inc(G.sem, G.up())

                @block.vector
                def _(dve):
                    dve.wait_ge(G.sem, G.n)
                    for q in range(QT):
                        for s, (b, e) in enumerate(segs):
                            i = q * n + s
                            VE.tensor_scalar(dst(q)[:, b:e], src(q)[:, b:e], st[:, 16 + i:17 + i], None, ALU.mult).then_inc(V.sem, V.up())
                        for f in range(2):
                            src_ready[q, f] = V.n
                src = dst

            def pair_slot(kt):
                return (tmp if kt < 4 else act_s)[:, (kt // 2) % 2, :]
            entry = (V.n, A.n)
            emptied = {}
            hi_step, turned_at = {}, {}

            def bank_of(kt):
                return ps[4 + kt] if kt < 4 else ps[6 + kt % 2]

            def transpose_tile(kt):
                @block.tensor
                def _(pe):
                    if kt == 0:
                        pe.wait_ge(A.sem, entry[1])
                    prior = kt - 2
                    if kt >= 4 and prior % 2 == 0:
                        pe.wait_ge(V.sem, emptied[prior])
                    if kt >= 4 and prior % 2 == 1:
                        pe.wait_ge(A.sem, emptied[prior])
                    for q in range(QT):
                        pe.wait_ge(V.sem, src_ready[q, kt // 4])
                        last = TE.transpose(bank_of(kt)[:, q * P:(q + 1) * P], src(q)[:, kt * P:(kt + 1) * P], ident)
                    last.then_inc(T.sem, T.up())
                turned_at[kt] = T.n

            def empty_tile(kt):
                bank, slot = bank_of(kt)[:, 0:L], pair_slot(kt)[:, (kt % 2) * L:(kt % 2 + 1) * L]
                if kt % 2 == 0:
                    @block.vector
                    def _(dve):
                        dve.wait_ge(T.sem, turned_at[kt])
                        dve.wait_ge(A.sem, entry[1])
                        if scale is None:
                            VE.tensor_copy(slot, bank).then_inc(V.sem, V.up())
                        elif shift is None:
                            VE.tensor_scalar(slot, bank, scale(kt), None, ALU.mult).then_inc(V.sem, V.up())
                        else:
                            VE.tensor_scalar(slot, bank, scale(kt), shift(kt), ALU.mult, ALU.add).then_inc(V.sem, V.up())
                    emptied[kt] = V.n
                else:
                    @block.scalar
                    def _(act):
                        act.wait_ge(T.sem, turned_at[kt])
                        act.wait_ge(V.sem, entry[0])
                        if scale is None:
                            E.activation(slot, bank, ACT.Copy).then_inc(A.sem, A.up())
                        elif shift is None:
                            E.activation(slot, bank, ACT.Copy, scale=scale(kt)).then_inc(A.sem, A.up())
                        else:
                            E.activation(slot, bank, ACT.Identity, scale=scale(kt), bias=shift(kt)).then_inc(A.sem, A.up())
                    emptied[kt] = A.n

            def split_pair(kt):
                src2 = pair_slot(kt)
                hi2 = t_hi[:, kt0 + kt:kt0 + kt + 2, :].rearrange("p a b -> p (a b)")

                @block.scalar
                def _(act):
                    act.wait_ge(V.sem, emptied[kt])
                    act.wait_ge(A.sem, emptied[kt + 1])
                    E.activation(hi2, src2, ACT.Copy).then_inc(A.sem, A.up())
                hi_step[kt] = hi_step[kt + 1] = A.n

            def split_rest(kt):
                src2 = pair_slot(kt)
                hi2 = t_hi[:, kt0 + kt:kt0 + kt + 2, :].rearrange("p a b -> p (a b)")
                lo2 = t_lo[:, kt0 + kt:kt0 + kt + 2, :].rearrange("p a b -> p (a b)")

                @block.vector
                def _(dve):
                    dve.wait_ge(A.sem, hi_step[kt])
                    VE.tensor_tensor(lo2, src2, hi2.bitcast(F32), ALU.subtract).then_inc(V.sem, V.up())
                kt_ready[kt0 + kt] = kt_ready[kt0 + kt + 1] = (V.n, hi_step[kt])

            for kt in range(0, n_kt, 2):
                transpose_tile(kt)
                transpose_tile(kt + 1)
                empty_tile(kt)
                empty_tile(kt + 1)
                split_pair(kt)
                if kt:
                    split_rest(kt - 2)
            split_rest(n_kt - 2)
            turned["at"] = (V.n, A.n)
            pay_splits()

        def split_T(src, kt, n):
            @block.scalar
            def _(act):
                act.wait_ge(V.sem, V.n)
                act.wait_ge(T.sem, T.n)
                act.wait_ge(used, blocks["pe"])
                E.activation(t_hi[:, kt:kt + n, :].rearrange("p a b -> p (a b)"), src, ACT.Copy).then_inc(A.sem, A.up())

            @block.vector
            def _(dve):
                dve.wait_ge(A.sem, A.n)
                VE.tensor_tensor(t_lo[:, kt:kt + n, :].rearrange("p a b -> p (a b)"), src,
                                   t_hi[:, kt:kt + n, :].rearrange("p a b -> p (a b)").bitcast(F32), ALU.subtract).then_inc(V.sem, V.up())
            for k in range(kt, kt + n):
                kt_ready[k] = (V.n, A.n)

        rows_made = [0]
        gate_diag = ar(AW - 1024, KT, P)

        def gate_start(kind):
            rows_made[0] += 1

            @block.vector
            def _(dve):
                dve.wait_ge(A.sem, A.n)
                dve.wait_ge(T.sem, T.n)
                dve.wait_ge(used, blocks["pe"])
                dve.wait_ge(mod_added, min(N_MOD, kind[0] // 4 + 2))
                if rows_made[0] > 1:
                    dve.wait_ge(row_kept, rows_made[0] - 1)
                VE.tensor_tensor(gate_diag, ident.unsqueeze(1).to_broadcast([P, KT, P]),
                                 modc[:, kind[0]:kind[0] + 8].unsqueeze(2).to_broadcast([P, KT, P]),
                                 ALU.mult).then_inc(diag_made, 1)

        def gate_products(pe):
            pe.wait_ge(diag_made, rows_made[0])
            for k in range(2):
                last = TE.matmul(ps[6 + k][:, :], cs("ones"),
                                 gate_diag[:, 4 * k:4 * k + 4, :].rearrange("p a b -> p (a b)"), start=True, stop=True)
            last.then_inc(row_summed, 1)

        def gate_keep(act, kind):
            act.wait_ge(row_summed, rows_made[0])
            E.activation(grow[:, 0:512], ps[6][:, :], ACT.Copy, scale=float(kind[1]))
            E.activation(grow[:, 512:1024], ps[7][:, :], ACT.Copy, scale=float(kind[1])).then_inc(row_kept, 1)

        def triple(out, xh, xl, wh, wl, w_first, start, stop):
            for i, (xx, ww) in enumerate(((xh, wh), (xl, wh), (xh, wl))):
                lhs, rhs = (ww, xx) if w_first else (xx, ww)
                last = TE.matmul(out, lhs, rhs, start=start and i == 0, stop=stop and i == 2)
            return last

        def rows_product(n_kt, width, kt0=0, kind=None, put_off=False, chained=False):
            per = BLK // width
            hv = (width + 511) // 512
            wd = min(width, 512)
            n_blk = -(-n_kt // per)
            fresh = turned["at"] == (V.n, A.n)
            tail = min(2, n_blk)
            groups = [[i] for i in range(n_blk - tail)] + [list(range(n_blk - tail, n_blk))]
            h0 = blocks["pe"]
            for group in groups:
                blocks["pe"] += len(group)

                @block.tensor
                def _(pe):
                    if group[0] == 0 and not fresh and not chained:
                        pe.wait_ge(V.sem, V.n)
                        pe.wait_ge(A.sem, A.n)
                    for q in range(QT):
                        qs = slice(q * P, (q + 1) * P)
                        if group[0] == 0 and chained:
                            pe.wait_ge(V.sem, acc_free[q][0])
                            pe.wait_ge(A.sem, acc_free[q][1])
                        for i in group:
                            s = (h0 + i) % RING
                            if q == 0:
                                pe.wait_ge(lo_done, h0 + i + 1)
                            for j in range(min(per, n_kt - i * per)):
                                k = i * per + j
                                if q == 0 and (fresh or chained):
                                    pe.wait_ge(V.sem, kt_ready[kt0 + k][0])
                                    pe.wait_ge(A.sem, kt_ready[kt0 + k][1])
                                for f in range(hv):
                                    ws = slice(j * width + f * 512, j * width + f * 512 + wd)
                                    last = triple(ps[q * 2 + f][:, 0:wd], t_hi[:, kt0 + k, qs], t_lo[:, kt0 + k, qs],
                                                  w_hi[:, s, ws], w_lo[:, s, ws], False, k == 0, k == n_kt - 1)
                            if q == QT - 1:
                                last.then_inc(used, 1)
                        if q == 0 and group[-1] == n_blk - 1:
                            last.then_inc(T.sem, T.up())
                            acc_step[0] = T.n
                if put_off and len(group) > 1:
                    owed[0] = len(group)
                else:
                    for _ in group:
                        next_split()
                if kind is not None and group[0] == 1:
                    gate_start(kind)
                if kind is not None and group[0] == 3:
                    @block.tensor
                    def _(pe):
                        gate_products(pe)

                    @block.scalar
                    def _(act):
                        gate_keep(act, kind)

        acc_free = {}
        bank_free = {}

        def narrow_product(n, bank):
            h = blocks["pe"]
            blocks["pe"] += 1
            s = h % RING
            fresh = turned["at"] == (V.n, A.n)
            turned["at"] = (V.n, A.n + 1) if fresh else (0, 0)

            @block.tensor
            def _(pe):
                if not fresh:
                    pe.wait_ge(V.sem, V.n)
                    pe.wait_ge(A.sem, A.n)
                pe.wait_ge(lo_done, h + 1)
                for k in range(KT):
                    if fresh:
                        pe.wait_ge(V.sem, kt_ready[k][0])
                        pe.wait_ge(A.sem, kt_ready[k][1])
                    ws = slice(k * n, (k + 1) * n)
                    last = triple(bank[0:n, 0:L], t_hi[:, k, :], t_lo[:, k, :], w_hi[:, s, ws], w_lo[:, s, ws], True,
                                  k == 0, k == KT - 1)
                last.then_inc(used, 1)
            next_split()

            @block.scalar
            def _(act):
                act.wait_ge(T.sem, T.n)
                act.wait_ge(used, blocks["pe"])
                act.wait_ge(V.sem, V.n)
                E.activation(tmp[0:n, 0, 0:L], bank[0:n, 0:L], ACT.Copy).then_inc(A.sem, A.up())
            acc_free[0] = acc_free[1] = (V.n, A.n)

        def keep_rows(keep):
            for q in range(QT):
                @block.scalar
                def _(act):
                    if q == 0:
                        act.wait_ge(T.sem, acc_step[0])
                    else:
                        act.wait_ge(T.sem, T.n)
                        act.wait_ge(used, blocks["pe"])
                    keep(q)
                acc_free[q] = (acc_free[q][0], A.n)
            pay_splits()

        def narrow_turn(n, bank):
            @block.tensor
            def _(pe):
                pe.wait_ge(A.sem, A.n)
                for q in range(QT):
                    last = TE.transpose(bank[:, q * n:(q + 1) * n], tmp[0:n, 0, q * P:(q + 1) * P], ident[0:n, 0:n])
                last.then_inc(T.sem, T.up())

        def columns_product(n_tiles, evac, chained=False):
            fresh = turned["at"] == (V.n, A.n)
            for pair in range(n_tiles // 2):
                bank = ps[4 + pair % 2]
                for half in range(2):
                    h = blocks["pe"]
                    blocks["pe"] += 1
                    s = h % RING

                    @block.tensor
                    def _(pe):
                        if half == 0:
                            if pair >= 2 or chained:
                                pe.wait_ge(V.sem, bank_free[pair % 2][0])
                                pe.wait_ge(A.sem, bank_free[pair % 2][1])
                            elif not fresh:
                                pe.wait_ge(V.sem, V.n)
                                pe.wait_ge(A.sem, A.n)
                        pe.wait_ge(lo_done, h + 1)
                        wv_hi = w_hi[:, s, :].rearrange("p (k c) -> p k c", c=P)
                        wv_lo = w_lo[:, s, :].rearrange("p (k c) -> p k c", c=P)
                        for k in range(KT):
                            if pair == 0 and half == 0 and fresh:
                                pe.wait_ge(V.sem, kt_ready[k][0])
                                pe.wait_ge(A.sem, kt_ready[k][1])
                            last = triple(bank[:, half * L:(half + 1) * L], t_hi[:, k, :], t_lo[:, k, :],
                                          wv_hi[:, k, :], wv_lo[:, k, :], True, k == 0, k == KT - 1)
                        last.then_inc(used, 1)
                    if half == 0:
                        next_split()
                evac(pair, bank)
                bank_free[pair % 2] = (V.n, A.n)
                next_split()

        def mod_first(c):
            @block.scalar
            def _(act):
                act.wait_ge(V.sem, V.n)
                act.wait_ge(T.sem, T.n)
                act.wait_ge(used, blocks["pe"])
                for half in range(2):
                    mod_load(act, half, c)

        def ffn(call, n_mod, mod0, residual):
            h0 = blocks["pe"]
            assert blocks["hi"] == h0 + RING

            hb = 2 * FG * call
            A0, V0 = A.n, V.n
            fresh = turned["at"] == (V.n, A.n)

            def slot(j):
                return (h0 + j) % RING

            def pe_body(pe, i, first, last_body, mod):
                for t in range(2):
                    for which in range(2):
                        j = 2 * t + which
                        pe.wait_ge(lo_done, h0 + j + 1 + RING * i)
                        if which == 0 and not (first and call == 0):
                            pe.wait_ge(gated, hb + 2 * i + (t - 1))
                        wh = w_hi[:, slot(j), :].rearrange("p (k c) -> p k c", c=P)
                        wl = w_lo[:, slot(j), :].rearrange("p (k c) -> p k c", c=P)
                        for k in range(KT):
                            if first and j == 0 and fresh:
                                pe.wait_ge(V.sem, kt_ready[k][0])
                                pe.wait_ge(A.sem, kt_ready[k][1])
                            last = triple(ps[4 + t][:, which * L:(which + 1) * L], t_hi[:, k, :], t_lo[:, k, :],
                                          wh[:, k, :], wl[:, k, :], True, k == 0, k == KT - 1)
                        last.then_inc(used, 1)
                        if last_body and t == 0 and which == 0 and residual is not None:
                            gate_products(pe)
                    if t == 0 and mod is not None:
                        if last_body and residual is not None:
                            pe.wait_ge(row_kept, rows_made[0])
                        mod_products(pe, mod)
                if last_body:
                    for q in range(QT):
                        qs = slice(q * P, (q + 1) * P)
                        for t in range(2):
                            j = 4 + t
                            if q == 0:
                                pe.wait_ge(lo_done, h0 + j + 1 + RING * i)
                                pe.wait_ge(gate_lo, hb + t + 1 + 2 * i)
                            for f in range(2):
                                fs = slice(f * 512, (f + 1) * 512)
                                last = triple(ps[2 * q + f][:, :], g_hi[:, t, qs], g_lo[:, t, qs],
                                              w_hi[:, slot(j), fs], w_lo[:, slot(j), fs], False, False, t == 1)
                            if q == 1:
                                last.then_inc(used, 1)
                        if q == 0:
                            last.then_inc(T.sem, T.up())
                            acc_step[0] = T.n
                            if mod is not None:
                                mod_turn(pe, mod)
                    return
                for t in range(2):
                    j = 4 + t
                    pe.wait_ge(lo_done, h0 + j + 1 + RING * i)
                    pe.wait_ge(gate_lo, hb + t + 1 + 2 * i)
                    for q in range(QT):
                        qs = slice(q * P, (q + 1) * P)
                        for f in range(2):
                            fs = slice(f * 512, (f + 1) * 512)
                            last = triple(ps[2 * q + f][:, :], g_hi[:, t, qs], g_lo[:, t, qs],
                                          w_hi[:, slot(j), fs], w_lo[:, slot(j), fs], False,
                                          first and t == 0, last_body and t == 1)
                    last.then_inc(used, 1)
                    if t == 0 and mod is not None:
                        mod_turn(pe, mod)

            def hi_next(act, i, j, static):
                h = h0 + j + RING
                if static:
                    if h + RING * i >= n_stream:
                        return
                    split_hi(act, h + RING * i)
                    return
                s = slot(j)
                act.wait_ge(landed[s], 16 * (h // RING + 1) + 16 * i)
                act.wait_ge(used, h - (RING - 1) + RING * i)
                E.activation(w_hi[:, s, :], raw[:, s, :], ACT.Copy).then_inc(hi_done, 1)

            def lo_next(dve, i, j, static):
                h = h0 + j + RING
                if static:
                    if h + RING * i >= n_stream:
                        return
                    split_lo(dve, h + RING * i)
                    return
                s = slot(j)
                dve.wait_ge(hi_done, h + 1 + RING * i)
                VE.tensor_tensor(w_lo[:, s, :], raw[:, s, :], w_hi[:, s, :].bitcast(F32),
                                 ALU.subtract).then_inc(lo_done, 1)

            def act_body(act, i, static, mod, more):
                for t in range(2):
                    hi_next(act, i, 2 * t, static)
                    if t == 0 and static and i == FG - 1 and residual is not None:
                        gate_keep(act, residual)
                    act.wait_ge(used, h0 + 2 * t + 2 + RING * i)
                    E.activation(act_s[:, t, 0:L], ps[4 + t][:, 0:L], ACT.Silu).then_inc(silu_done, 1)
                    act.wait_ge(gated, hb + t + 1 + 2 * i)
                    E.activation(g_hi[:, t, :], act_s[:, t, L:2 * L], ACT.Copy).then_inc(gate_hi, 1)
                    hi_next(act, i, 2 * t + 1, static)
                    if t == 0 and mod is not None and more:
                        for half in range(2):
                            mod_load(act, half, mod + 1)
                if not (static and i == FG - 1):
                    hi_next(act, i, 4, static)
                    hi_next(act, i, 5, static)

            def dve_body(dve, i, static, mod):
                for t in range(2):
                    lo_next(dve, i, 2 * t, static)
                    dve.wait_ge(silu_done, hb + t + 1 + 2 * i)
                    VE.tensor_tensor(act_s[:, t, L:2 * L], ps[4 + t][:, L:2 * L], act_s[:, t, 0:L],
                                     ALU.mult).then_inc(gated, 1)
                    dve.wait_ge(gate_hi, hb + t + 1 + 2 * i)
                    VE.tensor_tensor(g_lo[:, t, :], act_s[:, t, L:2 * L], g_hi[:, t, :].bitcast(F32),
                                     ALU.subtract).then_inc(gate_lo, 1)
                    lo_next(dve, i, 2 * t + 1, static)
                    if t == 0 and mod is not None:
                        mod_keep(dve, mod)
                late = static and i == FG - 1
                if not late:
                    lo_next(dve, i, 4, static)
                if mod is not None:
                    mod_add(dve, mod)
                if not late:
                    lo_next(dve, i, 5, static)

            def emit(lo, hi, mod_of):
                loop = hi - lo > 1

                @block.tensor
                def _(pe):
                    if lo == 0 and not fresh:
                        pe.wait_ge(V.sem, V0)
                        pe.wait_ge(A.sem, A0)
                    if loop:
                        with pe.Fori(lo, hi) as i:
                            pe_body(pe, i, False, False, mod_of(i))
                    else:
                        pe_body(pe, lo, lo == 0, lo == FG - 1, mod_of(lo))

                @block.scalar
                def _(act):
                    if loop:
                        with act.Fori(lo, hi) as i:
                            act_body(act, i, False, mod_of(i), True)
                    else:
                        m = mod_of(lo)
                        act_body(act, lo, True, m, m is not None and lo + 1 < n_mod)

                @block.vector
                def _(dve):
                    if loop:
                        with dve.Fori(lo, hi) as i:
                            dve_body(dve, i, False, mod_of(i))
                    else:
                        dve_body(dve, lo, True, mod_of(lo))

            def with_mod(i):
                return i + mod0

            def no_mod(i):
                return None
            if n_mod:
                blocks["hi"] = h0 + RING
                emit(0, 1, with_mod)
                if n_mod == FG:
                    emit(1, FG - 1, with_mod)
                    if residual is not None:
                        gate_start(residual)
                    emit(FG - 1, FG, with_mod)
                else:
                    emit(1, n_mod - 1, with_mod)
                    emit(n_mod - 1, n_mod, with_mod)
                    for i in range(n_mod, FG):
                        if i == FG - 1 and residual is not None:
                            gate_start(residual)
                        emit(i, i + 1, no_mod)
            else:
                emit(0, 1, no_mod)
                emit(1, FG - 1, no_mod)
                if residual is not None:
                    gate_start(residual)
                emit(FG - 1, FG, no_mod)
            blocks["pe"] = h0 + FG * RING
            blocks["hi"] = min(n_stream, h0 + FG * RING + RING - 2)
            owed[0] = 2

            add_residual(residual)

        acc_step = {}

        def add_residual(kind):
            for q in range(QT):
                @block.vector
                def _(dve):
                    if q == 0:
                        dve.wait_ge(T.sem, acc_step[0])
                        dve.wait_ge(A.sem, A.n)
                    else:
                        dve.wait_ge(T.sem, T.n)
                        dve.wait_ge(used, blocks["pe"])
                    product = (tmp if q == 0 else act_s)
                    if kind is not None:
                        dve.wait_ge(row_kept, rows_made[0])
                        for f in range(2):
                            VE.tensor_tensor(product[:, f, :], ps[2 * q + f][:, :], grow[:, f * 512:(f + 1) * 512],
                                               ALU.mult).then_inc(V.sem, V.up())
                    for f in range(2):
                        fs = slice(f * 512, (f + 1) * 512)
                        if kind is not None:
                            dve.wait_ge(V.sem, V.n - 1)
                            VE.tensor_tensor(x[:, q, fs], x[:, q, fs], product[:, f, :], ALU.add).then_inc(V.sem, V.up())
                        else:
                            VE.tensor_tensor(x[:, q, fs], x[:, q, fs], ps[2 * q + f][:, :], ALU.add).then_inc(V.sem, V.up())
                        x_ready[q, f] = V.n

        XN = AW - 2048

        def norm_x(gain, mods=None):
            if mods is not None:
                sh, sc = mods

                @block.vector
                def _(dve):
                    dve.wait_ge(T.sem, T.n)
                    dve.wait_ge(used, blocks["pe"])
                    dve.wait_ge(A.sem, A.n)
                    dve.wait_ge(mod_added, (max(sh, sc) + 8) // 4)
                    VE.scalar_tensor_tensor(out=sg[:, :], in0=modc[:, sc:sc + 8], scalar=1.0, in1=gain(0, 8),
                                              op0=ALU.add, op1=ALU.mult).then_inc(V.sem, V.up())
                turn(lambda q: x[:, q, :], KT, [(0, D)], lambda k: sg[:, k:k + 1], lambda k: modc[:, sh + k:sh + k + 1],
                     dst=lambda q: ar(XN, QT, D)[:, q, :], ready=dict(x_ready) or None)
            else:
                turn(lambda q: x[:, q, :], KT, [(0, D)], lambda k: gain(k, 1), None,
                     dst=lambda q: ar(XN, QT, D)[:, q, :], ready=dict(x_ready) or None)

        def mod_at(layer, which):
            return layer * 72 + which * 8

        norm_x(lambda k, n: col("norm_g", k, n), (mod_at(0, 0), mod_at(0, 1)))
        ffn(0, FG, PRE, (mod_at(0, 2), 0.5))

        norm_x(lambda k, n: col("norm_g", 8 + k, n), (mod_at(0, 3), mod_at(0, 4)))
        xb = ar(0, 12, 259)
        xc = ar(3108, 12, L)
        up = ar(6180, 4, 272)
        zt = ar(7268, QT, D)
        xdt, xde = ar(0, QT, D), ar(2048, D)
        xs = ar(9316, QT, D)
        ys = ar(11364, QT, D)
        btok = ar(13412, 2, P)
        s0 = 13668
        dtr, dtm, dte, dtu, dtv, adt, acs, eacs = (ar(s0 + 32 * k, QT, 16) for k in range(8))
        flat = {id(v): ar(s0 + 32 * k, 32) for k, v in enumerate((dtr, dtm, dte, dtu, dtv, adt, acs, eacs))}
        alog, dend = ar(s0 + 256, 16), ar(s0 + 272, 16)
        decay = ar(13960, 2, 512)
        state = ar(14984, D)

        narrow_product(16, ps[0])

        @block.gpsimd
        def _(pool):
            pool.wait_ge(T.sem, T.n)
            pool.wait_ge(used, blocks["pe"])
            GE.memset(xb[:, :, 0:3], 0.0).then_inc(G.sem, G.up())
            GE.memset(up[:, :, 0:16], 0.0).then_inc(G.sem, G.up())

        def step_sizes():
            narrow_turn(16, ps[7])

            @block.vector
            def _(dve):
                dve.wait_ge(T.sem, T.n)
                dve.wait_ge(used, blocks["pe"])
                for q in range(QT):
                    VE.tensor_tensor(dtr[:, q, :], ps[7][:, q * 16:(q + 1) * 16], rowv[:, 0:16], ALU.add).then_inc(V.sem, V.up())
                dve.wait_ge(V.sem, V.n)
                VE.tensor_scalar(dtu, dtr, -1.0, None, ALU.mult).then_inc(V.sem, V.up())
                VE.tensor_scalar(dtm, dtr, 0.0, None, ALU.max).then_inc(V.sem, V.up())
                dve.wait_ge(V.sem, V.n)
                VE.tensor_tensor(dtu, dtu, dtr, ALU.min).then_inc(V.sem, V.up())

            @block.scalar
            def _(act):
                act.wait_ge(V.sem, V.n)
                E.activation(dte, dtu, ACT.Exp).then_inc(A.sem, A.up())
                E.activation(alog, rowv[:, 16:32], ACT.Exp).then_inc(A.sem, A.up())

            @block.vector
            def _(dve):
                dve.wait_ge(A.sem, A.n)
                VE.tensor_scalar(dtu, dte, 1.0, None, ALU.add).then_inc(V.sem, V.up())

            @block.scalar
            def _(act):
                act.wait_ge(V.sem, V.n)
                E.activation(dtv, dtu, ACT.Ln).then_inc(A.sem, A.up())

            @block.vector
            def _(dve):
                dve.wait_ge(A.sem, A.n)
                VE.tensor_tensor(dtm, dtm, dtv, ALU.add).then_inc(V.sem, V.up())
                VE.tensor_scalar(adt, dtu, -1.0, None, ALU.add).then_inc(V.sem, V.up())
                dve.wait_ge(V.sem, V.n)
                VE.tensor_tensor(dte, dte, adt, ALU.subtract).then_inc(V.sem, V.up())
                VE.reciprocal(dtu, dtu).then_inc(V.sem, V.up())
                dve.wait_ge(V.sem, V.n)
                VE.tensor_tensor(dte, dte, dtu, ALU.mult).then_inc(V.sem, V.up())
                dve.wait_ge(V.sem, V.n)
                VE.tensor_tensor(dtr, dtm, dte, ALU.add).then_inc(V.sem, V.up())
                VE.tensor_scalar(alog, alog, -1.0, None, ALU.mult).then_inc(V.sem, V.up())
                dve.wait_ge(V.sem, V.n)
                VE.tensor_tensor(adt, dtr, alog.unsqueeze(1).to_broadcast([P, QT, 16]), ALU.mult).then_inc(V.sem, V.up())

        def evac_xbc(pair, bank):
            dst = xb[:, 2 * pair:2 * pair + 2, 3:259] if pair < 6 else up[:, 2 * pair - 12:2 * pair - 10, 16:272]

            @block.scalar
            def _(act):
                act.wait_ge(T.sem, T.n)
                act.wait_ge(used, blocks["pe"])
                act.wait_ge(V.sem, V.n)
                E.activation(dst, bank[:, :].rearrange("p (a b) -> p a b", b=L), ACT.Copy).then_inc(A.sem, A.up())
            if pair >= 6:
                return

            @block.vector
            def _(dve):
                dve.wait_ge(A.sem, A.n)
                dve.wait_ge(G.sem, G.n)
                for k in range(4):
                    for tl in (2 * pair, 2 * pair + 1):
                        if k == 0:
                            VE.tensor_scalar(xc[:, tl, :], xb[:, tl, 0:L], col("conv_w", tl), col("conv_b", tl),
                                               ALU.mult, ALU.add).then_inc(V.sem, V.up())
                        else:
                            VE.scalar_tensor_tensor(out=xc[:, tl, :], in0=xb[:, tl, k:k + L],
                                                      scalar=col("conv_w", 12 * k + tl), in1=xc[:, tl, :],
                                                      op0=ALU.mult, op1=ALU.add).then_inc(V.sem, V.up())
                    if k < 3:
                        dve.wait_ge(V.sem, V.n)

            @block.scalar
            def _(act):
                act.wait_ge(V.sem, V.n)
                E.activation(xc[:, 2 * pair:2 * pair + 2, :], xc[:, 2 * pair:2 * pair + 2, :], ACT.Silu).then_inc(A.sem, A.up())
            if pair == 0:
                step_sizes()

        columns_product(16, evac_xbc)

        windows = (2, 4, 8, 16)
        win_buf = [[ar(11364 + (2 * g + k) * 272, 272) for k in range(2)] for g in range(4)]
        win_at = [0]

        WIN_LAST = (1, 0, 1, 0)

        def window_step():
            step = win_at[0]
            win_at[0] += 1

            @block.vector
            def _(dve):
                if step == 0:
                    dve.wait_ge(A.sem, A.n)
                    dve.wait_ge(G.sem, G.n)
                if step < 7:
                    dve.wait_ge(V.sem, V.n)
                for g, win in enumerate(windows):
                    w_ = 2 ** step
                    out = win_buf[g][WIN_LAST[g]]
                    total = win_buf[g][1 - WIN_LAST[g]]
                    if step < 4 and w_ < win:
                        cur = up[:, g, :] if step == 0 else win_buf[g][1 - step % 2]
                        VE.tensor_tensor(win_buf[g][step % 2][:, 2 * w_:272], cur[:, 2 * w_:272],
                                           cur[:, w_:272 - w_], ALU.add).then_inc(V.sem, V.up())
                    elif step == 4:
                        VE.tensor_scalar(out[:, 16:272], total[:, 16:272], 1.0 / win, None, ALU.mult).then_inc(V.sem, V.up())
                    elif step == 5:
                        VE.tensor_tensor(out[:, 16:32], total[:, 16:32], cs("recip", 16 * g, 16 * g + 16), ALU.mult).then_inc(V.sem, V.up())
                    elif step == 6:
                        VE.tensor_tensor(out[:, 16:272], out[:, 16:272], up[:, g, 16:272], ALU.subtract).then_inc(V.sem, V.up())
        meanwhile.append(window_step)
        rows_product(KT, D, chained=True, put_off=True)
        meanwhile.clear()
        while win_at[0] < 7:
            window_step()

        def keep_z(q):
            for f in range(2):
                E.activation(zt[:, q, f * 512:(f + 1) * 512], ps[2 * q + f][:, :], ACT.Silu).then_inc(A.sem, A.up())
        keep_rows(keep_z)

        @block.tensor
        def _(pe):
            pe.wait_ge(V.sem, V.n)
            for c in range(QT):
                TE.matmul(ps[7][:, c * 16:(c + 1) * 16], cs("upper"), adt[:, c, :], start=True, stop=True)
            TE.matmul(ps[7][:, 32:48], cs("ones"), adt[:, 0, :], start=True, stop=True).then_inc(T.sem, T.up())
            for g in range(4):
                TE.matmul(ps[4 + g // 2][:, (g % 2) * L:(g % 2 + 1) * L], sm("pool_w", g * P, (g + 1) * P),
                            win_buf[g][WIN_LAST[g]][:, 16:272], start=True, stop=True).then_inc(T.sem, T.up())
        pooled_at = T.n

        @block.vector
        def _(dve):
            dve.wait_ge(T.sem, pooled_at - 4)
            VE.tensor_copy(acs, ps[7][:, 0:32].rearrange("p (q h) -> p q h", h=16)).then_inc(V.sem, V.up())
            dve.wait_ge(V.sem, V.n)
            VE.tensor_tensor(dend, ps[7][:, 32:48], acs[:, 0, :], ALU.subtract).then_inc(V.sem, V.up())
            dve.wait_ge(T.sem, T.n)
            dve.wait_ge(used, blocks["pe"])
            for g in range(4):
                VE.tensor_scalar(tmp[:, g // 2, (g % 2) * L:(g % 2 + 1) * L],
                                   ps[4 + g // 2][:, (g % 2) * L:(g % 2 + 1) * L], col("pool_scale", g), None, ALU.mult).then_inc(V.sem, V.up())

        xs_at, xs_turned = {}, {}
        for n in range(5):
            bank = ps[(6, 7, 4, 5, 6)[n]]
            q, t0 = (n // 2, 4 * (n % 2)) if n < 4 else (0, 8)
            tiles = 4 if n < 4 else 2

            @block.tensor
            def _(pe):
                if n == 0:
                    pe.wait_ge(A.sem, A.n)
                    pe.wait_ge(V.sem, V.n)
                if n == 4:
                    pe.wait_ge(V.sem, xs_at[0])
                for k in range(tiles):
                    last = TE.transpose(bank[:, k * P:(k + 1) * P], xc[:, t0 + k, q * P:(q + 1) * P], ident)
                last.then_inc(T.sem, T.up())
            if n == 0:
                for pair in range(2):
                    split_T(tmp[:, pair, :], 8 + 2 * pair, 2)

                @block.scalar
                def _(act):
                    act.wait_ge(V.sem, V.n)
                    E.activation(dend, dend, ACT.Exp).then_inc(A.sem, A.up())
                    E.activation(eacs, acs, ACT.Exp).then_inc(A.sem, A.up())
            if n % 2 == 0 and n < 4:
                @block.vector
                def _(dve):
                    dve.wait_ge(T.sem, T.n)
                    dve.wait_ge(used, blocks["pe"])
                    VE.tensor_copy(xs[:, q, t0 * P:(t0 + 4) * P], bank[:, :]).then_inc(V.sem, V.up())
                xs_at[n] = V.n
            else:
                @block.scalar
                def _(act):
                    act.wait_ge(T.sem, T.n)
                    act.wait_ge(used, blocks["pe"])
                    if n < 4:
                        E.activation(xs[:, q, t0 * P:(t0 + 4) * P], bank[:, :], ACT.Copy).then_inc(A.sem, A.up())
                    else:
                        E.activation(btok[:, :, :].rearrange("p a b -> p (a b)"), bank[:, 0:2 * P], ACT.Copy).then_inc(A.sem, A.up())

        @block.vector
        def _(dve):
            dve.wait_ge(A.sem, A.n)
            dve.wait_ge(V.sem, V.n)
            for q in range(QT):
                VE.tensor_tensor(xdt[:, q, :].rearrange("p (h d) -> p h d", d=64),
                                   xs[:, q, :].rearrange("p (h d) -> p h d", d=64),
                                   dtr[:, q, :].unsqueeze(2).to_broadcast([P, 16, 64]), ALU.mult).then_inc(V.sem, V.up())
            dve.wait_ge(V.sem, V.n - 1)
            VE.tensor_tensor(xde.rearrange("p (h d) -> p h d", d=64), xdt[:, 0, :].rearrange("p (h d) -> p h d", d=64),
                               dend.unsqueeze(2).to_broadcast([P, 16, 64]), ALU.mult).then_inc(V.sem, V.up())

        @block.tensor
        def _(pe):
            pe.wait_ge(A.sem, A.n)
            for c in range(QT):
                for g in range(2):
                    last = TE.matmul(ps[6][:, (2 * c + g) * P:(2 * c + g + 1) * P], xc[:, 8 + g, c * P:(c + 1) * P],
                                     xc[:, 10 + g, c * P:(c + 1) * P], start=True, stop=True)
            pe.wait_ge(V.sem, V.n)
            for g in range(2):
                last = TE.matmul(ps[4 + g][:, :], btok[:, g, :], xde[:, g * 512:(g + 1) * 512], start=True, stop=True)
            last.then_inc(T.sem, T.up())
        cbt = tmp[:, 0, :]

        @block.vector
        def _(dve):
            dve.wait_ge(T.sem, T.n)
            dve.wait_ge(used, blocks["pe"])
            dve.wait_ge(A.sem, A.n)
            VE.tensor_copy(cbt, ps[6][:, :]).then_inc(V.sem, V.up())
            for g in range(2):
                VE.tensor_copy(state[:, g * 512:(g + 1) * 512], ps[4 + g][:, :]).then_inc(V.sem, V.up())
        state_at = V.n

        sums_at, less_at, exp_at, decay_at, y_at, gone_at = {}, {}, {}, {}, {}, {}

        def sums_on_all_rows(n):
            @block.tensor
            def _(pe):
                pe.wait_ge(V.sem, less_at.get(n - 2, state_at))
                for h in range(4):
                    last = TE.matmul(ps[6 + n % 2][:, h * P:(h + 1) * P],
                                     adt[:, n // 4, 4 * (n % 4) + h:4 * (n % 4) + h + 1].to_broadcast([P, P]),
                                     cs("upper"), start=True, stop=True)
                last.then_inc(T.sem, T.up())
            sums_at[n] = T.n

            @block.vector
            def _(dve):
                dve.wait_ge(T.sem, sums_at[n])
                for h in range(4):
                    head = 4 * (n % 4) + h
                    VE.scalar_tensor_tensor(out=decay[:, n % 2, h * P:(h + 1) * P],
                                              in0=ps[6 + n % 2][:, h * P:(h + 1) * P],
                                              scalar=acs[:, n // 4, head:head + 1], in1=cs("ssd_mask"),
                                              op0=ALU.subtract, op1=ALU.add).then_inc(V.sem, V.up())
            less_at[n] = V.n

            @block.scalar
            def _(act):
                act.wait_ge(V.sem, less_at[n])
                E.activation(decay[:, n % 2, :], decay[:, n % 2, :], ACT.Exp).then_inc(A.sem, A.up())
            exp_at[n] = A.n

        def heads(v):
            return v.rearrange("p (h d) -> p h d", d=64)
        for n in range(-1, 8):
            c, quad = n // 4, n % 4
            g = quad // 2
            if n + 1 < 8:
                sums_on_all_rows(n + 1)
            if n < 0:
                @block.tensor
                def _(pe):
                    for g_ in range(2):
                        last = TE.matmul(ps[4 + g_][:, :], xc[:, 10 + g_, P:2 * P], state[:, g_ * 512:(g_ + 1) * 512],
                                         start=True, stop=True)
                    last.then_inc(T.sem, T.up())
                continue

            @block.vector
            def _(dve):
                dve.wait_ge(A.sem, exp_at[n])
                VE.tensor_tensor(decay[:, n % 2, :].rearrange("p (h s) -> p h s", s=P),
                                   decay[:, n % 2, :].rearrange("p (h s) -> p h s", s=P),
                                   cbt[:, (2 * c + g) * P:(2 * c + g + 1) * P].unsqueeze(1).to_broadcast([P, 4, P]),
                                   ALU.mult).then_inc(V.sem, V.up())
            decay_at[n] = V.n

            @block.tensor
            def _(pe):
                pe.wait_ge(V.sem, decay_at[n])
                for h in range(4):
                    hh = 4 * quad + h
                    last = TE.matmul(ps[2 * c + g][:, (hh % 8) * 64:(hh % 8 + 1) * 64],
                                     decay[:, n % 2, h * P:(h + 1) * P], xdt[:, c, hh * 64:(hh + 1) * 64],
                                     start=True, stop=True)
                last.then_inc(T.sem, T.up())
            y_at[n] = T.n

            @block.vector
            def _(dve):
                gs = slice((n % 2) * 512, (n % 2 + 1) * 512)
                if n < 4:
                    VE.tensor_tensor(heads(ys[:, n // 2, gs]), heads(xs[:, n // 2, gs]),
                                       rowv[:, 32 + 8 * (n % 2):40 + 8 * (n % 2)].unsqueeze(2).to_broadcast([P, 8, 64]),
                                       ALU.mult).then_inc(V.sem, V.up())
                    gone_at[n] = V.n
                if n in (2, 3):
                    dve.wait_ge(T.sem, y_at[0])
                    VE.tensor_tensor(heads(act_s[:, n % 2, :]), heads(ps[4 + n % 2][:, :]),
                                       eacs[:, 1, 8 * (n % 2):8 * (n % 2) + 8].unsqueeze(2).to_broadcast([P, 8, 64]),
                                       ALU.mult).then_inc(V.sem, V.up())
                    gone_at[n + 2] = V.n
                if n in (4, 5):
                    dve.wait_ge(V.sem, gone_at[n])
                    VE.tensor_tensor(ys[:, 1, gs], ys[:, 1, gs], act_s[:, n % 2, :], ALU.add).then_inc(V.sem, V.up())
                    dve.wait_ge(T.sem, y_at[3])
                    VE.tensor_tensor(ys[:, 0, gs], ys[:, 0, gs], ps[n % 2][:, :], ALU.add).then_inc(V.sem, V.up())
                    gone_at[n + 2] = V.n
                if n in (6, 7):
                    dve.wait_ge(V.sem, gone_at[n])
                    VE.tensor_tensor(ys[:, 0, gs], ys[:, 0, gs], zt[:, 0, gs], ALU.mult).then_inc(V.sem, V.up())

        @block.vector
        def _(dve):
            dve.wait_ge(V.sem, V.n)
            for g in range(2):
                dve.wait_ge(T.sem, y_at[5 + 2 * g])
                VE.tensor_tensor(ys[:, 1, g * 512:(g + 1) * 512], ys[:, 1, g * 512:(g + 1) * 512], ps[2 + g][:, :],
                                   ALU.add).then_inc(V.sem, V.up())
            for g in range(2):
                dve.wait_ge(V.sem, V.n - 1)
                VE.tensor_tensor(ys[:, 1, g * 512:(g + 1) * 512], ys[:, 1, g * 512:(g + 1) * 512],
                                   zt[:, 1, g * 512:(g + 1) * 512], ALU.mult).then_inc(V.sem, V.up())
        turn(lambda q: ys[:, q, :], KT, [(0, 512), (512, 1024)], lambda k: col("ssd_norm", k), None,
             dst=lambda q: xs[:, q, :])
        rows_product(12, D, kind=(mod_at(0, 5), 1.0), put_off=True)
        add_residual((mod_at(0, 5), 1.0))

        mod_first(PRE + FG)
        norm_x(lambda k, n: col("norm_g", 16 + k, n), (mod_at(0, 6), mod_at(0, 7)))
        ffn(1, FG, PRE + FG, (mod_at(0, 8), 0.5))
        mod_first(PRE + 2 * FG)
        norm_x(lambda k, n: col("norm_g", 24 + k, n), (mod_at(1, 0), mod_at(1, 1)))
        ffn(2, N_MOD - PRE - 2 * FG, PRE + 2 * FG, (mod_at(1, 2), 0.5))
        def attention(n, spans, dk, scores, values, dv, out, scale, bias, prepare=None, v0=0):
            at = [0]
            for kts in spans:
                at.append(at[-1] + P * len(kts))
            width = at[-1]
            prep_done, prep_free, exp_done, sc_free, pt_done, pt_evac, out_done = {}, {}, {}, {}, {}, {}, {}
            s_used, pv_done = {}, {}
            start = (V.n, A.n)
            for step in range(n + 3):
                h = step
                if prepare is not None and h < n:
                    prepare(h, prep_done, prep_free, start)
                h = step - 1
                if 0 <= h < n:
                    bank = ps[2 + h % 2]
                    sl = act_s[:, h % 2, 0:width]
                    nm, sums = st[:, 20 + 4 * (h % 2):22 + 4 * (h % 2)], st[:, 32 + 2 * (h % 4):34 + 2 * (h % 4)]

                    @block.tensor
                    def _(pe):
                        pe.wait_ge(V.sem, sc_free.get(h - 2, start[0]))
                        pe.wait_ge(A.sem, prep_done.get(h, start[1]))
                        for q, kts in enumerate(spans):
                            steps = scores(h, q, kts)
                            for i, (lhs, rhs) in enumerate(steps):
                                last = TE.matmul(bank[:, at[q]:at[q + 1]], lhs, rhs, start=i == 0,
                                                 stop=i == len(steps) - 1)
                        last.then_inc(T.sem, T.up())
                        prep_free[h] = T.n

                    @block.vector
                    def _(dve):
                        dve.wait_ge(T.sem, prep_free[h])
                        if bias is None:
                            VE.tensor_scalar(sl, bank[:, 0:width], scale, None, ALU.mult).then_inc(V.sem, V.up())
                            sc_free[h] = V.n
                        else:
                            for lo, hi, b in bias(h):
                                VE.scalar_tensor_tensor(out=sl[:, lo:hi], in0=bank[:, lo:hi],
                                                                       scalar=scale, in1=b, op0=ALU.mult,
                                                                       op1=ALU.add).then_inc(V.sem, V.up())
                                sc_free[h] = V.n
                        dve.wait_ge(V.sem, V.n)
                        for q in range(QT):
                            VE.tensor_reduce(nm[:, q:q + 1], sl[:, at[q]:at[q + 1]], AX, ALU.max, negate=True).then_inc(V.sem, V.up())

                    @block.scalar
                    def _(act):
                        act.wait_ge(V.sem, V.n)
                        for q in range(QT):
                            E.activation(sl[:, at[q]:at[q + 1]], sl[:, at[q]:at[q + 1]], ACT.Exp,
                                                         bias=nm[:, q:q + 1], accum_out=sums[:, q:q + 1]).then_inc(A.sem, A.up())
                            exp_done[h] = A.n
                h = step - 2
                if 0 <= h < n:
                    sl = act_s[:, h % 2, 0:width]
                    pbank = ps[4 + h % 2]

                    @block.tensor
                    def _(pe):
                        pe.wait_ge(A.sem, exp_done[h])
                        pe.wait_ge(A.sem, pt_evac.get(h - 2, 0))
                        for k in range(width // P):
                            last = TE.transpose(pbank[:, k * P:(k + 1) * P], sl[:, k * P:(k + 1) * P], ident)
                        last.then_inc(T.sem, T.up())
                        s_used[h] = T.n

                    @block.scalar
                    def _(act):
                        act.wait_ge(T.sem, s_used[h])
                        E.activation(tmp[:, h % 2, 0:width], pbank[:, 0:width], ACT.Copy).then_inc(A.sem, A.up())
                        pt_evac[h] = A.n
                h = step - 3
                if 0 <= h < n:
                    obank = ps[6 + h % 2]
                    sums, rinv = st[:, 32 + 2 * (h % 4):34 + 2 * (h % 4)], st[:, 40 + 2 * (h % 4):42 + 2 * (h % 4)]

                    @block.tensor
                    def _(pe):
                        pe.wait_ge(A.sem, pt_evac[h])
                        pe.wait_ge(V.sem, out_done.get(h - 2, start[0]))
                        for q, kts in enumerate(spans):
                            for i, kt in enumerate(kts):
                                c = at[q] + i * P
                                last = TE.matmul(obank[:, q * dv:(q + 1) * dv], tmp[:, h % 2, c:c + P], values(h, kt),
                                                 start=i == 0, stop=i == len(kts) - 1)
                        last.then_inc(T.sem, T.up())
                        pv_done[h] = T.n

                    @block.vector
                    def _(dve):
                        dve.wait_ge(T.sem, pv_done[h])
                        dve.wait_ge(A.sem, exp_done[h])
                        out(dve, h, obank, sums, rinv)
                        out_done[h] = V.n

        norm_x(lambda k, n: col("norm_g", 32 + k, n), (mod_at(1, 3), mod_at(1, 4)))
        qa = ar(0, QT, D)
        qm = ar(2048, QT, 1536)
        kf = ar(5120, QT, 1536)
        vm = ar(8192, QT, D)
        om = ar(10240, QT, D)
        qk = ar(12288, 2, 512)
        kr = ar(13312, QT, 32)
        cosr, sinr = ar(13376, QT, 16), ar(13408, QT, 16)
        ang, rnd = ar(13440, QT, 16), ar(13472, QT, 16)
        posf = ar(13504, QT)
        rt = [ar(13520 + 256 * k, 256) for k in range(4)]

        narrow_product(32, ps[4])

        @block.vector
        def _(dve):
            dve.wait_ge(T.sem, T.n)
            dve.wait_ge(used, blocks["pe"])
            dve.wait_ge(A.sem, A.n)
            TWO_PI = 2 * math.pi
            parts, rest = [], TWO_PI
            for bits in (6, 9, 22):
                c = float(np.float32(math.floor(rest * 2 ** bits) / 2 ** bits)) if bits < 22 else float(np.float32(rest))
                parts.append(c)
                rest -= c
            big = 1.5 * 2.0 ** 23
            edge = 3.1415925
            VE.tensor_copy(posf, posi[:, :]).then_inc(V.sem, V.up())
            dve.wait_ge(V.sem, V.n)
            for q in range(QT):
                VE.tensor_scalar(ang[:, q, :], cs("invf"), posf[:, q:q + 1], None, ALU.mult).then_inc(V.sem, V.up())
            dve.wait_ge(V.sem, V.n)
            VE.tensor_scalar(rnd, ang, 1.0 / TWO_PI, big, ALU.mult, ALU.add).then_inc(V.sem, V.up())
            dve.wait_ge(V.sem, V.n)
            VE.tensor_scalar(rnd, rnd, -big, None, ALU.add).then_inc(V.sem, V.up())
            for c in parts:
                dve.wait_ge(V.sem, V.n)
                VE.scalar_tensor_tensor(out=ang, in0=rnd, scalar=-c, in1=ang, op0=ALU.mult, op1=ALU.add).then_inc(V.sem, V.up())
            dve.wait_ge(V.sem, V.n)
            VE.tensor_scalar(rnd, ang, math.pi / 2, -TWO_PI, ALU.is_gt, ALU.mult).then_inc(V.sem, V.up())
            dve.wait_ge(V.sem, V.n)
            VE.scalar_tensor_tensor(out=rnd, in0=ang, scalar=math.pi / 2, in1=rnd, op0=ALU.add, op1=ALU.add).then_inc(V.sem, V.up())
            dve.wait_ge(V.sem, V.n)
            for v in (ang, rnd):
                VE.tensor_scalar(v, v, edge, -edge, ALU.min, ALU.max).then_inc(V.sem, V.up())

        @block.scalar
        def _(act):
            act.wait_ge(V.sem, V.n)
            E.activation(sinr, ang, ACT.Sin).then_inc(A.sem, A.up())
            E.activation(cosr, rnd, ACT.Sin).then_inc(A.sem, A.up())

        def rope(dve, dst, src, q, heads, out1, out2):
            def wide(v):
                return v[:, q, :].unsqueeze(1).to_broadcast([P, heads, 16])
            t = [r[:, 0:heads * 16].rearrange("p (h d) -> p h d", d=16) for r in rt]
            x1, x2 = src[:, :, 0:16], src[:, :, 16:32]
            VE.tensor_tensor(t[0], x1, wide(cosr), ALU.mult).then_inc(V.sem, V.up())
            VE.tensor_tensor(t[1], x2, wide(sinr), ALU.mult).then_inc(V.sem, V.up())
            VE.tensor_tensor(t[2], x2, wide(cosr), ALU.mult).then_inc(V.sem, V.up())
            VE.tensor_tensor(t[3], x1, wide(sinr), ALU.mult).then_inc(V.sem, V.up())
            dve.wait_ge(V.sem, V.n)
            VE.tensor_tensor(out1, t[0], t[1], ALU.subtract).then_inc(V.sem, V.up())
            VE.tensor_tensor(out2, t[2], t[3], ALU.add).then_inc(V.sem, V.up())
            dve.wait_ge(V.sem, V.n)

        rows_product(KT, D, put_off=True)

        def keep_qa(q):
            for f in range(2):
                E.activation(qa[:, q, f * 512:(f + 1) * 512], ps[2 * q + f][:, :], ACT.Copy).then_inc(A.sem, A.up())
        keep_rows(keep_qa)

        narrow_turn(32, ps[7])

        @block.vector
        def _(dve):
            dve.wait_ge(T.sem, T.n)
            dve.wait_ge(used, blocks["pe"])
            dve.wait_ge(A.sem, A.n)
            for q in range(QT):
                VE.tensor_copy(kr[:, q, :], ps[7][:, q * 32:(q + 1) * 32]).then_inc(V.sem, V.up())
            dve.wait_ge(V.sem, V.n)
            for q in range(QT):
                k3 = kf[:, q, :].rearrange("p (h d) -> p h d", d=96)
                s3 = kr[:, q, :].rearrange("p (h d) -> p h d", d=32)
                rope(dve, None, s3, q, 1, kr[:, q, 0:16].unsqueeze(1), kr[:, q, 16:32].unsqueeze(1))
                VE.tensor_copy(k3[:, :, 64:96], kr[:, q, :].unsqueeze(1).to_broadcast([P, HEADS, 32])).then_inc(V.sem, V.up())

        turn(lambda q: qa[:, q, :], KT, [(0, 768), (768, 1024)],
             lambda k: col("q_norm", k) if k < 6 else col("kv_norm", k - 6), None, dst=lambda q: ar(XN - 512, QT, D)[:, q, :])
        rows_product(6, D, put_off=True)

        def keep_qm(q):
            for f in range(2):
                E.activation(qm[:, q, f * 512:(f + 1) * 512], ps[2 * q + f][:, :], ACT.Copy).then_inc(A.sem, A.up())
        keep_rows(keep_qm)
        rows_product(6, 512, chained=True, put_off=True)

        def keep_qm_rest(q):
            E.activation(qm[:, q, 1024:1536], ps[2 * q][:, :], ACT.Copy).then_inc(A.sem, A.up())
        keep_rows(keep_qm_rest)

        @block.vector
        def _(dve):
            dve.wait_ge(A.sem, A.n)
            for q in range(QT):
                q3 = qm[:, q, :].rearrange("p (h d) -> p h d", d=96)
                rope(dve, None, q3[:, :, 64:96], q, HEADS, q3[:, :, 64:80], q3[:, :, 80:96])
        for part in range(2):
            rows_product(2, D, kt0=6, chained=True, put_off=True)

            def keep_kv(q):
                for f in range(2):
                    src = ps[2 * q + f][:, :].rearrange("p (h d) -> p h d", d=P)
                    h0 = 8 * part + 4 * f
                    k3 = kf[:, q, :].rearrange("p (h d) -> p h d", d=96)
                    v3 = vm[:, q, :].rearrange("p (h d) -> p h d", d=64)
                    E.activation(k3[:, h0:h0 + 4, 0:64], src[:, :, 0:64], ACT.Copy).then_inc(A.sem, A.up())
                    E.activation(v3[:, h0:h0 + 4, :], src[:, :, 64:128], ACT.Copy).then_inc(A.sem, A.up())
            keep_rows(keep_kv)

        def mla_prepare(h, done, free, start):
            bank = ps[h % 2]

            @block.tensor
            def _(pe):
                pe.wait_ge(V.sem, start[0])
                pe.wait_ge(A.sem, done.get(h - 2, start[1]))
                for i, src in enumerate((qm, kf)):
                    for q in range(QT):
                        last = TE.transpose(bank[0:96, (2 * i + q) * P:(2 * i + q + 1) * P],
                                            src[:, q, h * 96:(h + 1) * 96], ident)
                last.then_inc(T.sem, T.up())

            @block.scalar
            def _(act):
                act.wait_ge(T.sem, T.n)
                act.wait_ge(used, blocks["pe"])
                act.wait_ge(T.sem, free.get(h - 2, 0))
                E.activation(qk[0:96, h % 2, :], bank[0:96, :], ACT.Copy).then_inc(A.sem, A.up())
                done[h] = A.n

        def mla_out(dve, h, acc, sums, rinv):
            VE.reciprocal(rinv, sums).then_inc(V.sem, V.up())
            dve.wait_ge(V.sem, V.n)
            for q in range(QT):
                VE.tensor_scalar(om[:, q, h * 64:(h + 1) * 64], acc[:, q * 64:(q + 1) * 64], rinv[:, q:q + 1], None,
                                   ALU.mult).then_inc(V.sem, V.up())
        causal = cs("causal")
        attention(HEADS, [[0], [0, 1]], 96,
                  lambda h, q, kts: [(qk[0:96, h % 2, q * P:(q + 1) * P], qk[0:96, h % 2, 2 * P:2 * P + P * len(kts)])],
                  lambda h, kt: vm[:, kt, h * 64:(h + 1) * 64], 64, mla_out, 1.0 / math.sqrt(96.0),
                  lambda h: [(0, P, causal[:, P:2 * P]), (P, 3 * P, causal)], mla_prepare)
        turn(lambda q: om[:, q, :], KT)
        rows_product(KT, D, kind=(mod_at(1, 5), 1.0), put_off=True)
        add_residual((mod_at(1, 5), 1.0))
        norm_x(lambda k, n: col("norm_g", 40 + k, n), (mod_at(1, 6), mod_at(1, 7)))
        ffn(3, 0, 0, (mod_at(1, 8), 0.5))
        def norm_rows(gain):
            @block.gpsimd
            def _(pool):
                pool.wait_ge(V.sem, V.n)
                pool.dma_start(grow[:, :], a[gain][0:1, :].to_broadcast([P, D])).then_inc(later.sem, later.up(16))

            for q in range(QT):
                @block.scalar
                def _(act):
                    act.wait_ge(A.sem, A.n)
                    act.wait_ge(T.sem, T.n)
                    act.wait_ge(used, blocks["pe"])
                    for f in range(2):
                        fs = slice(f * 512, (f + 1) * 512)
                        act.wait_ge(V.sem, x_ready[q, f])
                        E.activation(ar(XN, QT, D)[:, q, fs], x[:, q, fs], ACT.Square, scale=1.0 / 32,
                                       accum_out=st[:, 2 * q + f:2 * q + f + 1]).then_inc(A.sem, A.up())

                @block.gpsimd
                def _(pool):
                    pool.wait_ge(A.sem, A.n)
                    GE.tensor_scalar(st[:, 8 + q:9 + q], st[:, 2 * q:2 * q + 1], st[:, 2 * q + 1:2 * q + 2], EPS,
                                       ALU.add, ALU.add).then_inc(G.sem, G.up())
                    pool.wait_ge(G.sem, G.n)
                    GE.tensor_tensor(st[:, 16 + q:17 + q], st[:, 8 + q:9 + q], st[:, 60:61], ALU.pow).then_inc(G.sem, G.up())

                @block.vector
                def _(dve):
                    dve.wait_ge(G.sem, G.n)
                    dve.wait_ge(later.sem, later.n)
                    for f in range(2):
                        fs = slice(f * 512, (f + 1) * 512)
                        VE.scalar_tensor_tensor(out=x[:, q, fs], in0=x[:, q, fs], scalar=st[:, 16 + q:17 + q],
                                                  in1=grow[:, fs], op0=ALU.mult, op1=ALU.mult).then_inc(V.sem, V.up())
                        x_ready[q, f] = V.n
        norm_rows("g_first")
        norm_x(lambda k, n: col("mix", k, n))
        qT = ar(0, KT, L)
        kd = [ar(2048, 4, L), ar(3072, 4, L)]
        vd = [ar(4096, QT, L), ar(4608, QT, L)]
        gattn = ar(5120, QT, D)
        cin = ar(7168, KT, 286)
        cv = ar(9456, KT, L)
        gconv = ar(11504, QT, D)
        cmp_in = [ar(13552, 4, L), ar(14576, 4, L)]
        gates = ar(15600, QT, 48)
        kcmp = ar(15700, 64)
        zc = ar(15764, 64)
        coef = ar(15828, QT, 16)
        cm, csum = ar(15860, QT, 16), ar(15892, QT, 16)
        ymix, om2 = gconv, ar(13552, QT, D)
        bias_t = ar(7168, HEADS, L)
        vcmp = grow[:, :].rearrange("p (g n) -> p g n", g=4)

        narrow_product(48, ps[0])

        @block.gpsimd
        def _(pool):
            pool.wait_ge(T.sem, T.n)
            pool.wait_ge(used, blocks["pe"])
            pool.wait_ge(V.sem, V.n)
            GE.memset(cin[:, :, 0:30], 0.0).then_inc(G.sem, G.up())
            GE.memset(grow[:, :], 0.0).then_inc(G.sem, G.up())

        cin_step = {}
        cin_at = V.n
        pending = [(pair, lo, min(31, lo + 3)) for pair in range(KT // 2) for lo in range(0, 31, 3)]

        def next_taps():
            if pending and 2 * pending[0][0] + 1 in cin_step:
                taps(*pending.pop(0))
        meanwhile.append(next_taps)

        def evac_conv(pair, bank):
            s = act_s[:, pair % 2, 0:L]

            @block.scalar
            def _(act):
                act.wait_ge(T.sem, T.n)
                act.wait_ge(used, blocks["pe"])
                act.wait_ge(V.sem, cin_step.get(pair - 2, cin_at))
                E.activation(s, bank[:, L:2 * L], ACT.Sigmoid).then_inc(A.sem, A.up())

            @block.vector
            def _(dve):
                dve.wait_ge(A.sem, A.n)
                VE.tensor_tensor(cin[:, pair, 30:286], bank[:, 0:L], s, ALU.mult).then_inc(V.sem, V.up())
            cin_step[pair] = V.n
            if pair == 0:
                narrow_turn(48, ps[7])

                @block.scalar
                def _(act):
                    act.wait_ge(T.sem, T.n)
                    act.wait_ge(used, blocks["pe"])
                    E.activation(gates[:, :, :].rearrange("p a b -> p (a b)"), ps[7][:, 0:96], ACT.Sigmoid).then_inc(A.sem, A.up())

        tap_step = {}

        def taps(pair, lo, hi):
            @block.vector
            def _(dve):
                dve.wait_ge(G.sem, G.n)
                for k in range(lo, hi):
                    for tile in (2 * pair, 2 * pair + 1):
                        if k == 0:
                            dve.wait_ge(V.sem, cin_step[tile])
                            VE.tensor_scalar(cv[:, tile, :], cin[:, tile, 0:L], col("dw_w", tile), col("dw_b", tile),
                                               ALU.mult, ALU.add).then_inc(V.sem, V.up())
                        else:
                            dve.wait_ge(V.sem, tap_step[tile])
                            VE.scalar_tensor_tensor(out=cv[:, tile, :], in0=cin[:, tile, k:k + L],
                                                      scalar=col("dw_w", 8 * k + tile), in1=cv[:, tile, :],
                                                      op0=ALU.mult, op1=ALU.add).then_inc(V.sem, V.up())
                        tap_step[tile] = V.n

        columns_product(16, evac_conv)

        @block.gpsimd
        def _(pool):
            pool.wait_ge(V.sem, V.n)
            pool.wait_ge(A.sem, A.n)
            GE.memset(act_s[:, :, :], 0.0).then_inc(G.sem, G.up())

        def evac_cmp_in(pair, bank):
            b3 = bank[:, :].rearrange("p (a b) -> p a b", b=L)
            dst = cmp_in[pair]

            @block.scalar
            def _(act):
                act.wait_ge(T.sem, T.n)
                act.wait_ge(used, blocks["pe"])
                for half in range(2):
                    src = b3[64 * half:64 * half + 64]
                    E.activation(dst[0:64, half:4:2, :], src, ACT.Copy).then_inc(A.sem, A.up())
                    E.activation(dst[64:128, half:4:2, 0:L - 1], src[:, :, 1:L], ACT.Copy).then_inc(A.sem, A.up())

        def evac_keys(which):
            def evac(pair, bank):
                b3 = bank[:, :].rearrange("p (a b) -> p a b", b=L)

                @block.scalar
                def _(act):
                    act.wait_ge(T.sem, T.n)
                    act.wait_ge(used, blocks["pe"])
                    for half in range(2):
                        for to in range(2):
                            E.activation(kd[which][64 * to:64 * to + 64, half:4:2, :],
                                           b3[64 * half:64 * half + 64], ACT.Copy).then_inc(A.sem, A.up())
            return evac

        def evac_q(dst):
            def evac(pair, bank):
                @block.scalar
                def _(act):
                    act.wait_ge(T.sem, T.n)
                    act.wait_ge(used, blocks["pe"])
                    E.activation(dst[:, 2 * pair:2 * pair + 2, :].rearrange("p a b -> p (a b)"), bank[:, :],
                                   ACT.Copy).then_inc(A.sem, A.up())
            return evac
        columns_product(4, evac_cmp_in, chained=True)
        columns_product(2, evac_keys(0), chained=True)
        columns_product(2, evac_keys(1), chained=True)
        columns_product(8, evac_q(qT), chained=True)
        for kind in range(2):
            src = cmp_in[kind]

            @block.tensor
            def _(pe):
                pe.wait_ge(A.sem, A.n)
                for lp in range(16):
                    w = sm("w1", (kind * 16 + lp) * 64, (kind * 16 + lp + 1) * 64)
                    TE.matmul(ps[6][0:64, 0:60], w, src[:, :, 2 * lp:2 * lp + 16 * (N_CMP - 1) + 1:16],
                              start=lp == 0, stop=lp == 15)
                for lp in range(16):
                    w = sm("w1", (kind * 16 + lp) * 64, (kind * 16 + lp + 1) * 64)
                    last = TE.matmul(ps[7][0:64, 0:1], w, sm("pos", kind * 16 + lp, kind * 16 + lp + 1),
                                     start=lp == 0, stop=lp == 15)
                last.then_inc(T.sem, T.up())

            @block.scalar
            def _(act):
                act.wait_ge(T.sem, T.n)
                act.wait_ge(used, blocks["pe"])
                act.wait_ge(A.sem, A.n)
                E.activation(zc[0:64, 60:61], ps[7][0:64, 0:1], ACT.Copy).then_inc(A.sem, A.up())
                act.wait_ge(A.sem, A.n)
                E.activation(zc[0:64, 0:60], ps[6][0:64, 0:60], ACT.Silu, bias=zc[0:64, 60:61]).then_inc(A.sem, A.up())

            @block.tensor
            def _(pe):
                pe.wait_ge(A.sem, A.n)
                w = sm("w2", kind * 64, kind * 64 + 64, rows=slice(0, 64))
                if kind == 0:
                    TE.matmul(ps[7][0:64, 0:60], w, zc[0:64, 0:60], start=True, stop=True).then_inc(T.sem, T.up())
                else:
                    for g in range(4):
                        last = TE.matmul(ps[7][0:N_CMP, g * 64:(g + 1) * 64], zc[0:64, g * N_CMP:(g + 1) * N_CMP], w,
                                         start=True, stop=True)
                    last.then_inc(T.sem, T.up())

            @block.scalar
            def _(act):
                act.wait_ge(T.sem, T.n)
                act.wait_ge(used, blocks["pe"])
                act.wait_ge(G.sem, G.n)
                if kind == 0:
                    for to in range(2):
                        E.activation(kcmp[64 * to:64 * to + 64, 0:60], ps[7][0:64, 0:60], ACT.Copy).then_inc(A.sem, A.up())
                else:
                    for r in range(4):
                        E.activation(vcmp[32 * r:32 * r + N_CMP, :, r * 64:(r + 1) * 64],
                                       ps[7][0:N_CMP, 0:256].rearrange("p (g d) -> p g d", d=64), ACT.Copy).then_inc(A.sem, A.up())
            for _i in range(3):
                next_taps()
        for which in range(2):
            rows_product(KT, L, chained=True, put_off=True)

            def keep_v(q):
                E.activation(vd[which][:, q, :], ps[2 * q][:, 0:L], ACT.Copy).then_inc(A.sem, A.up())
            keep_rows(keep_v)

        @block.tensor
        def _(pe):
            pe.wait_ge(A.sem, A.n)
            for q in range(QT):
                for h in range(HEADS):
                    b = 64 * (h % 2)
                    c = q * 256 + (h // 2) * 32
                    last = TE.matmul(ps[4 + h % 2][:, c:c + N_CMP], qT[b:b + 64, h // 2, q * P:(q + 1) * P],
                                     kcmp[b:b + 64, (h // 4) * N_CMP:(h // 4 + 1) * N_CMP], start=True, stop=True)
            last.then_inc(T.sem, T.up())
        scores_at = T.n
        for _i in range(5):
            next_taps()

        def evac_rows(dst, func):
            def keep(q):
                for f in range(2):
                    E.activation(dst[:, q, f * 512:(f + 1) * 512], ps[2 * q + f][:, :], func).then_inc(A.sem, A.up())
            keep_rows(keep)
        rows_product(KT, D, chained=True, put_off=True)
        evac_rows(gconv, ACT.Sigmoid)

        meanwhile.clear()
        while pending:
            next_taps()

        def channel_sums(src, bank):
            @block.tensor
            def _(pe):
                pe.wait_ge(V.sem, V.n)
                pe.wait_ge(A.sem, A.n)
                for k in range(KT):
                    last = TE.matmul(bank[:, 0:L], cs("ones"), src[:, k, :], start=k == 0, stop=k == KT - 1)
                last.then_inc(T.sem, T.up())
        square = cin[:, :, 0:L]
        mean, rstd = tmp[:, 0, 0:L], tmp[:, 0, L:2 * L]
        channel_sums(cv, ps[6])

        @block.vector
        def _(dve):
            dve.wait_ge(T.sem, T.n)
            dve.wait_ge(used, blocks["pe"])
            dve.wait_ge(A.sem, A.n)
            VE.tensor_scalar(mean, ps[6][:, 0:L], 1.0 / D, None, ALU.mult).then_inc(V.sem, V.up())
            dve.wait_ge(V.sem, V.n)
            VE.tensor_tensor(cv, cv, mean.unsqueeze(1).to_broadcast([P, KT, L]), ALU.subtract).then_inc(V.sem, V.up())

        @block.scalar
        def _(act):
            act.wait_ge(V.sem, V.n)
            E.activation(square, cv, ACT.Square).then_inc(A.sem, A.up())

        scale64 = 1.0 / math.sqrt(64.0)
        pt = act_s[:, :, :].rearrange("p q (h n) -> p q h n", n=32)
        pn = pt[:, :, :, 0:N_CMP]
        by_head = [P, QT, HEADS, N_CMP]

        def over_heads(v):
            return v.rearrange("p (q n) -> p q n", n=16)[:, :, 0:N_CMP].unsqueeze(2).to_broadcast(by_head)

        def over_keys(v):
            return v.unsqueeze(3).to_broadcast(by_head)

        @block.vector
        def _(dve):
            dve.wait_ge(G.sem, G.n)
            dve.wait_ge(T.sem, scores_at)
            for q in range(QT):
                for odd in range(2):
                    VE.scalar_tensor_tensor(
                        out=pn[:, q, odd:HEADS:2, :],
                        in0=ps[4 + odd][:, q * 256:(q + 1) * 256].rearrange("p (h n) -> p h n", n=32)[:, :, 0:N_CMP],
                        scalar=scale64, in1=biasc[:, q, 0:N_CMP, odd:HEADS:2].rearrange("p n h -> p h n"),
                        op0=ALU.mult, op1=ALU.add).then_inc(V.sem, V.up())
            dve.wait_ge(V.sem, V.n)
            VE.tensor_tensor(pn, pn, over_heads(cs("cmpneg")), ALU.add).then_inc(V.sem, V.up())
            dve.wait_ge(V.sem, V.n)
            VE.tensor_reduce(cm, pn, AX, ALU.max).then_inc(V.sem, V.up())
            dve.wait_ge(V.sem, V.n)
            VE.tensor_tensor(pn, pn, over_keys(cm), ALU.subtract).then_inc(V.sem, V.up())

        @block.scalar
        def _(act):
            act.wait_ge(V.sem, V.n)
            E.activation(pn, pn, ACT.Exp).then_inc(A.sem, A.up())

        @block.vector
        def _(dve):
            dve.wait_ge(A.sem, A.n)
            VE.tensor_tensor(pn, pn, over_heads(cs("cmp01")), ALU.mult).then_inc(V.sem, V.up())
            dve.wait_ge(V.sem, V.n)
            VE.tensor_reduce(csum, pn, AX, ALU.add).then_inc(V.sem, V.up())
            dve.wait_ge(V.sem, V.n)
            VE.tensor_scalar(csum, csum, 1e-30, None, ALU.max).then_inc(V.sem, V.up())
            dve.wait_ge(V.sem, V.n)
            VE.reciprocal(csum, csum).then_inc(V.sem, V.up())
            dve.wait_ge(V.sem, V.n)
            VE.tensor_tensor(coef, csum, gates[:, :, 0:16], ALU.mult).then_inc(V.sem, V.up())
        probs_at = V.n

        def deviation():
            channel_sums(square, ps[7])

            @block.vector
            def _(dve):
                dve.wait_ge(T.sem, T.n)
                dve.wait_ge(used, blocks["pe"])
                VE.tensor_scalar(rstd, ps[7][:, 0:L], 1.0 / D, EPS, ALU.mult, ALU.add).then_inc(V.sem, V.up())

            @block.scalar
            def _(act):
                act.wait_ge(V.sem, V.n)
                E.activation(rstd, rstd, ACT.Sqrt).then_inc(A.sem, A.up())

            @block.vector
            def _(dve):
                dve.wait_ge(A.sem, A.n)
                VE.reciprocal(rstd, rstd).then_inc(V.sem, V.up())
                dve.wait_ge(V.sem, V.n)
                VE.tensor_tensor(cv, cv, rstd.unsqueeze(1).to_broadcast([P, KT, L]), ALU.mult).then_inc(V.sem, V.up())

            @block.scalar
            def _(act):
                act.wait_ge(V.sem, V.n)
                for k in range(KT):
                    E.activation(cv[:, k, :], cv[:, k, :], ACT.Silu, scale=col("ln_g", k), bias=col("ln_b", k)).then_inc(A.sem, A.up())

        def compressed_values(q):
            @block.tensor
            def _(pe):
                pe.wait_ge(V.sem, probs_at)
                pe.wait_ge(A.sem, A.n)
                for g in range(4):
                    last = TE.transpose(ps[6][:, g * P:(g + 1) * P], act_s[:, q, g * P:(g + 1) * P], ident)
                last.then_inc(T.sem, T.up())

            @block.scalar
            def _(act):
                act.wait_ge(T.sem, T.n)
                act.wait_ge(used, blocks["pe"])
                act.wait_ge(V.sem, V.n)
                E.activation(tmp[:, 1, :], ps[6][:, :], ACT.Copy).then_inc(A.sem, A.up())

            @block.tensor
            def _(pe):
                pe.wait_ge(A.sem, A.n)
                for g in range(4):
                    last = TE.matmul(ps[4 + g // 2][:, (g % 2) * L:(g % 2 + 1) * L], tmp[:, 1, g * P:(g + 1) * P],
                                     vcmp[:, g, :], start=True, stop=True)
                last.then_inc(T.sem, T.up())

            @block.vector
            def _(dve):
                dve.wait_ge(T.sem, T.n)
                dve.wait_ge(used, blocks["pe"])
                for f in range(2):
                    VE.tensor_tensor(om2[:, q, f * 512:(f + 1) * 512].rearrange("p (h d) -> p h d", d=64),
                                       ps[4 + f][:, :].rearrange("p (h d) -> p h d", d=64),
                                       coef[:, q, 8 * f:8 * f + 8].unsqueeze(2).to_broadcast([P, 8, 64]), ALU.mult).then_inc(V.sem, V.up())
        blocks_taken = [0]

        def between_blocks():
            blocks_taken[0] += 1
            if blocks_taken[0] == 3:
                deviation()
            if blocks_taken[0] in (5, 6):
                compressed_values(blocks_taken[0] - 5)
        meanwhile.append(between_blocks)
        rows_product(KT, D, chained=True)
        meanwhile.clear()
        evac_rows(gattn, ACT.Sigmoid)
        for k in range(0, KT, 2):
            split_T(cv[:, k:k + 2, :].rearrange("p a b -> p (a b)"), k, 2)
        turned["at"] = (V.n, A.n)

        @block.gpsimd
        def _(pool):
            pool.wait_ge(V.sem, V.n)
            pool.wait_ge(A.sem, A.n)
            pool.wait_ge(T.sem, T.n)
            pool.wait_ge(used, blocks["pe"])
            pool.wait_ge(scratch.sem, scratch.n)
            skew = bass.AP(tensor=u_dram.tensor, offset=P - 1, ap=[[383, P], [P * 384, HEADS], [1, L]])
            pool.dma_start(bias_t, skew).then_inc(biasld.sem, biasld.up(16))
        rows_product(KT, D)

        @block.vector
        def _(dve):
            dve.wait_ge(T.sem, T.n)
            dve.wait_ge(used, blocks["pe"])
            dve.wait_ge(A.sem, A.n)
            for q in range(QT):
                for f in range(2):
                    fs = slice(f * 512, (f + 1) * 512)
                    VE.tensor_tensor(ymix[:, q, fs], ps[2 * q + f][:, :], gconv[:, q, fs], ALU.mult).then_inc(V.sem, V.up())

        def nsa_scores(n, q, kts):
            h = n % HEADS
            b = 64 * (h % 2)
            return [(qT[b:b + 64, h // 2, q * P:(q + 1) * P], kd[n // HEADS][b:b + 64, h // 4, 0:P * len(kts)])]

        def nsa_out(dve, n, acc, sums, rinv):
            h, which = n % HEADS, n // HEADS
            VE.reciprocal(rinv, sums).then_inc(V.sem, V.up())
            dve.wait_ge(V.sem, V.n)
            c = (1 + which) * 16 + h
            VE.tensor_tensor(rinv, rinv, gates[:, :, c:c + 1].rearrange("p q a -> p (q a)"), ALU.mult).then_inc(V.sem, V.up())
            dve.wait_ge(V.sem, V.n)
            for q in range(QT):
                o = om2[:, q, h * 64:(h + 1) * 64]
                VE.scalar_tensor_tensor(out=o, in0=acc[:, q * 64:(q + 1) * 64], scalar=rinv[:, q:q + 1], in1=o,
                                          op0=ALU.mult, op1=ALU.add).then_inc(V.sem, V.up())

        @block.vector
        def _(dve):
            dve.wait_ge(biasld.sem, biasld.n)

        attention(2 * HEADS, [[0], [0, 1]], 64, nsa_scores,
                  lambda n, kt: vd[n // HEADS][:, kt, ((n % HEADS) // 4) * 64:((n % HEADS) // 4 + 1) * 64], 64, nsa_out,
                  scale64, lambda n: [(0, P, bias_t[:, n % HEADS, P:2 * P]), (P, 3 * P, bias_t[:, n % HEADS, :])])

        @block.vector
        def _(dve):
            dve.wait_ge(V.sem, V.n)
            for q in range(QT):
                VE.tensor_tensor(om2[:, q, :], om2[:, q, :], gattn[:, q, :], ALU.mult).then_inc(V.sem, V.up())
            dve.wait_ge(V.sem, V.n)
            for q in range(QT):
                VE.tensor_tensor(ymix[:, q, :], ymix[:, q, :], om2[:, q, :], ALU.add).then_inc(V.sem, V.up())
        memt = ar(0, QT, D)

        @block.gpsimd
        def _(pool):
            pool.wait_ge(V.sem, V.n)
            pool.wait_ge(T.sem, T.n)
            pool.wait_ge(used, blocks["pe"])
            pool.wait_ge(A.sem, A.n)
            pool.dma_start(memt, a["mem"].rearrange("(q p) d -> p q d", p=P)).then_inc(later.sem, later.up(16))

        turn(lambda q: ymix[:, q, :], KT)
        rows_product(KT, D, put_off=True)
        kx, vx, qx, ox = ar(2048, KT, L), ar(4096, QT, D), ar(6144, KT, L), ar(8192, QT, D)

        @block.tensor
        def _(pe):
            pe.wait_ge(later.sem, later.n)
        turn(lambda q: memt[:, q, :], KT)
        add_residual(None)
        turned["at"] = (V.n, A.n)
        columns_product(8, evac_q(kx))
        rows_product(KT, D, put_off=True)
        evac_rows(vx, ACT.Copy)
        norm_x(lambda k, n: col("nx", k, n))
        columns_product(8, evac_q(qx))

        def cross_out(dve, h, acc, sums, rinv):
            VE.reciprocal(rinv, sums).then_inc(V.sem, V.up())
            dve.wait_ge(V.sem, V.n)
            for q in range(QT):
                VE.tensor_scalar(ox[:, q, h * L:(h + 1) * L], acc[:, q * L:(q + 1) * L], rinv[:, q:q + 1], None,
                                   ALU.mult).then_inc(V.sem, V.up())
        attention(4, [[0, 1], [0, 1]], 256,
                  lambda h, q, kts: [(qx[:, 2 * h + j, q * P:(q + 1) * P], kx[:, 2 * h + j, :]) for j in range(2)],
                  lambda h, kt: vx[:, kt, h * L:(h + 1) * L], 256, cross_out, 1.0 / 16.0, None)
        turn(lambda q: ox[:, q, :], KT)
        rows_product(KT, D, put_off=True)
        add_residual(None)
        norm_x(lambda k, n: col("nffn", k, n))
        ffn(4, 0, 0, None)
        norm_rows("g_last")

        @block.sync
        def _(sp):
            sp.wait_ge(V.sem, V.n)
            sp.dma_start(a["out"].rearrange("(q p) d -> p q d", p=P), x[:, :, :]).then_inc(stored.sem, stored.up(16))
            sp.wait_ge(stored.sem, stored.n)


_NAMES = ("x c positions mod_w mod_b norm_g ffn_w13 ffn_w2 ab_w_in pool_w pool_scale ssd_conv_w ssd_conv_b "
          "ssd_dt_bias ssd_a_log ssd_d ssd_norm_g ab_w_out mla_w_in mla_q_norm_g mla_w_uq mla_kv_norm_g mla_w_ukv "
          "mla_w_o final_norm_g mem_2 norm_mix_g_2 w_in_2 conv_dw_w_2 conv_dw_b_2 conv_ln_g_2 conv_ln_b_2 "
          "conv_pw_w_2 cmp_pos_2 cmp_w1_2 cmp_w2_2 w_out_2 norm_x_g_2 xq_w_2 xkv_w_2 xo_w_2 norm_ffn_g_2 "
          "ffn_in_w_2 ffn_out_w_2 rel_bias_2 final_norm_g_2").split()


def by_columns(w):
    n = w.shape[1] // P
    return w.reshape(KT, P, n, P).transpose(2, 1, 0, 3).reshape(n, P, BLK)


def by_rows(w):
    k, n = w.shape
    per = BLK // n
    v = w.reshape(k // P, P, n)
    return v.reshape(k // P // per, per, P, n).transpose(0, 2, 1, 3).reshape(-1, P, BLK)


def in_one_block(w):
    return np.concatenate([tiles_on_partitions(w), np.zeros((P, BLK - KT * w.shape[1]), w.dtype)], axis=1)[None]


def ffn_blocks(w13, w2):
    a_, b_ = by_columns(w13[:, :FF]), by_columns(w13[:, FF:])
    r = w2.reshape(FT, P, D)
    six = [a_[0::2], b_[0::2], a_[1::2], b_[1::2], r[0::2], r[1::2]]
    return np.stack(six, axis=1).reshape(-1, P, BLK)


def pack_stream(i):
    ab, mi, w = i["ab_w_in"][0], i["mla_w_in"][0], i["w_in_2"][0]
    uq, ukv, xkv = i["mla_w_uq"][0], i["mla_w_ukv"][0], i["xkv_w_2"][0]
    parts = [
        ffn_blocks(i["ffn_w13"][0, 0], i["ffn_w2"][0, 0]),
        in_one_block(ab[:, 3072:3088]), by_columns(ab[:, 1536:3072]), by_columns(ab[:, 0:512]), by_rows(ab[:, 512:1536]), by_rows(np.roll(i["ab_w_out"][0], -512, axis=0)),
        ffn_blocks(i["ffn_w13"][0, 1], i["ffn_w2"][0, 1]),
        ffn_blocks(i["ffn_w13"][1, 0], i["ffn_w2"][1, 0]),
        in_one_block(mi[:, 1024:1056]), by_rows(mi[:, 0:1024]), by_rows(uq[:, 0:1024]), by_rows(uq[:, 1024:1536]),
        by_rows(ukv[:, 0:1024]), by_rows(ukv[:, 1024:2048]), by_rows(i["mla_w_o"][0]),
        ffn_blocks(i["ffn_w13"][1, 1], i["ffn_w2"][1, 1]),
        in_one_block(w[:, 4608:4656]),
        by_columns(np.concatenate([w[:, :2048].reshape(D, 2, KT, P)[:, 0], w[:, :2048].reshape(D, 2, KT, P)[:, 1]],
                                  axis=2).reshape(D, 2048)),
        by_columns(w[:, 3072:3584]), by_columns(w[:, 3584:3840]), by_columns(w[:, 4096:4352]),
        by_columns(w[:, 2048:3072]),
        by_rows(w[:, 3840:4096]), by_rows(w[:, 4352:4608]), by_rows(w[:, 4656:5680]), by_rows(w[:, 5680:6704]),
        by_rows(i["conv_pw_w_2"][0]), by_rows(i["w_out_2"][0]),
        by_columns(xkv[:, 0:1024]), by_rows(xkv[:, 1024:2048]), by_columns(i["xq_w_2"][0]), by_rows(i["xo_w_2"][0]),
        ffn_blocks(i["ffn_in_w_2"][0], i["ffn_out_w_2"][0]),
    ]
    out = np.concatenate(parts, axis=0)
    assert out.shape[0] == N_BLOCKS, (out.shape, N_BLOCKS)
    return out


def pack_cols(i):
    c = {
        "c": i["c"].reshape(8, P), "mod_b": i["mod_b"].reshape(144, P), "norm_g": i["norm_g"].reshape(48, P),
        "pool_scale": i["pool_scale"].reshape(4, P), "conv_w": i["ssd_conv_w"].reshape(48, P),
        "conv_b": i["ssd_conv_b"].reshape(12, P), "q_norm": i["mla_q_norm_g"].reshape(6, P),
        "kv_norm": i["mla_kv_norm_g"].reshape(2, P), "ssd_norm": i["ssd_norm_g"].reshape(8, P),
        "mix": i["norm_mix_g_2"].reshape(8, P), "dw_w": i["conv_dw_w_2"].reshape(248, P),
        "dw_b": i["conv_dw_b_2"].reshape(8, P), "ln_g": i["conv_ln_g_2"].reshape(8, P),
        "ln_b": i["conv_ln_b_2"].reshape(8, P), "nx": i["norm_x_g_2"].reshape(8, P),
        "nffn": i["norm_ffn_g_2"].reshape(8, P),
    }
    return np.ascontiguousarray(np.concatenate([c[n] for n, _ in COLS], axis=0).T)


def tiles_on_partitions(w):
    return w.reshape(-1, P, w.shape[1]).transpose(1, 0, 2).reshape(P, -1)


def pack_small(i):
    f = np.float32
    w1 = i["cmp_w1_2"][0].reshape(2, 16, 2, 64, 64).transpose(2, 3, 0, 1, 4).reshape(P, 2048)
    w2 = np.concatenate([i["cmp_w2_2"][0].transpose(1, 0, 2).reshape(64, 128), np.zeros((64, 128), f)], axis=0)
    pos = i["cmp_pos_2"][0].reshape(2, 16, 2, 64).transpose(2, 3, 0, 1).reshape(P, 32)
    relb = np.concatenate([i["rel_bias_2"], np.zeros((96, 16), f)], axis=0)
    return np.ascontiguousarray(np.concatenate([
        i["pool_w"][0].transpose(1, 0, 2).reshape(P, 512), w1, w2, pos, relb],
        axis=1))


def constants():
    f = np.float32
    p, j = np.arange(P)[:, None], np.arange(P)[None, :]
    j2 = np.arange(256)[None, :]
    q = np.arange(L).reshape(QT, P).T[:, :, None]
    seen = np.zeros((P, QT, 16), bool)
    seen[:, :, :N_CMP] = q >= 16 * np.arange(N_CMP)[None, None, :] + 31
    sel = (np.arange(P) % 32 == 0)[:, None]
    invf = np.float32(10000.0) ** (-np.arange(0, 32, 2, dtype=f) / f(32))
    recip = np.stack([f(1) / np.minimum(np.arange(16, dtype=f) + 1, f(win)) for win in (2, 4, 8, 16)])
    c = {
        "ident": p == j, "upper": p <= j, "ssd_mask": np.where(p <= j, 0, NEG),
        "causal": np.where(j2 - P <= p, 0, NEG), "ones": np.ones((P, P)), "sel": sel,
        "invf": np.broadcast_to(invf, (P, 16)), "recip": np.broadcast_to(recip.reshape(1, 64), (P, 64)),
        "cmp01": seen.reshape(P, 32), "cmpneg": np.where(seen, 0, NEG).reshape(P, 32),
    }
    return np.ascontiguousarray(np.concatenate([np.asarray(c[n], f) for n, _ in CONST], axis=1))


def onehots():
    n = np.arange(-256, 256)
    nn = np.maximum(n, 1).astype(np.float32)
    large = 16 + (np.log(nn / np.float32(16)) / np.float32(math.log(8)) * np.float32(16)).astype(np.int32)
    bucket = np.where(n < 16, np.maximum(n, 0), np.minimum(large, 31))
    by_distance = (np.arange(33)[:, None] == bucket[None, :]).astype(np.float32)
    back = 255 - np.arange(512)
    out = np.zeros((33, 1024), np.float32)
    out[:, 0:512] = np.where(back[None, :] >= 0, by_distance[:, np.clip(back + 256, 0, 511)], 0)
    out[32, 0:512] = back < 0
    out[:, 512:1024] = by_distance
    return out


def kernel(**inputs):
    import concourse.bacc as _bacc
    from concourse.bass_utils import run_bass_kernel_spmd as _run

    i = {n: np.asarray(inputs[n]) for n in _NAMES}
    mod = i["mod_w"].reshape(2, 2, 4, P, 18, MODC).transpose(0, 4, 1, 3, 2, 5).reshape(N_MOD, 2, P, 4 * MODC)
    arrays = {
        "stream": pack_stream(i), "mod_w": np.ascontiguousarray(mod), "cols": pack_cols(i), "small": pack_small(i),
        "const": constants(), "onehot": onehots(), "x": i["x"].reshape(L, D), "mem": i["mem_2"].reshape(L, D),
        "rows": np.concatenate([i["ssd_dt_bias"][0], i["ssd_a_log"][0], i["ssd_d"][0]]).reshape(1, 48),
        "positions": np.ascontiguousarray(i["positions"].reshape(QT, P).T),
        "g_first": i["final_norm_g"].reshape(1, D), "g_last": i["final_norm_g_2"].reshape(1, D),
    }
    arrays = {f"in_{n}": v for n, v in arrays.items()}
    nc = _bacc.Bacc("TRN2", target_bir_lowering=False, num_devices=1)
    aps = {n[3:]: nc.dram_tensor(n, v.shape, mybir.dt.from_np(v.dtype), kind="ExternalInput").ap()
           for n, v in arrays.items()}
    aps["out"] = nc.dram_tensor("out_0", (L, D), F32, kind="ExternalOutput").ap()
    build(nc, aps)
    r = _run(nc, [arrays], core_ids=[0])
    return np.asarray(r.results[0]["out_0"]).reshape(1, L, D)
```
